# Optimizing a Trainium2 kernel written in Bass

```python
import math
import jax, jax.numpy as jnp
from jax import lax
import numpy as np

D_MODEL = 1024
BATCH = 1
SEQ = 256
DEPTH = 1
DEC_BATCH = 8
DEC_SEQ = 8
PAST_LEN = 2048
PAGE_SIZE = 128

PLE_DIM = 256
M_HEADS = 4
D_MLSTM = D_MODEL
M_HEAD_DIM = D_MLSTM // M_HEADS
M_CONV_W = 4
MLSTM_CHUNK = 64
D_SCONV = D_MODEL
S_CONV_W = 3
N_GROUPS = 4
EXPERTS_PER_GROUP = 8
N_EXPERTS = N_GROUPS * EXPERTS_PER_GROUP
TOP_K_IN_GROUP = 2
D_EXPERT = D_MODEL // 4
RMS_EPS = 1e-6
D_IN = 3 * D_MLSTM + 2 * M_HEADS + 3 * D_SCONV + 2 * D_MODEL

kernel_name = 'hybrid_mlstm_shortconv_hmoe_step'

def rms_norm(x, g):
    xf = x.astype(jnp.float32)
    xf = xf * lax.rsqrt(jnp.mean(xf * xf, axis=-1, keepdims=True) + RMS_EPS)
    return (xf * g.astype(jnp.float32)).astype(x.dtype)

def causal_depthwise_conv(x, buf, w):
    t = x.shape[1]
    xp = jnp.concatenate([buf.astype(x.dtype), x], axis=1)
    y = sum(xp[:, j:j + t] * w[j] for j in range(w.shape[0]))
    return y, xp[:, t:]

def mlstm_chunkwise(q, k, v, log_i, log_f, c0, n0, m0):
    b, t, h, dh = q.shape
    L = math.gcd(t, MLSTM_CHUNK)
    nc = t // L

    def blocks(a):
        a = a.reshape((b, nc, L, h) + a.shape[3:])
        return jnp.moveaxis(jnp.moveaxis(a, 1, 0), 2, 3)

    causal = jnp.tril(jnp.ones((L, L), dtype=bool))

    def step(carry, inp):
        c, n, m = carry
        qc, kc, vc, lic, lfc = inp
        bcum = jnp.cumsum(lfc, axis=-1)
        d = jnp.where(causal, bcum[..., :, None] - bcum[..., None, :] + lic[..., None, :], -jnp.inf)
        inter = m[..., None] + bcum
        m_t = jnp.maximum(inter, jnp.max(d, axis=-1))
        w_inter = jnp.exp(inter - m_t)
        s = jnp.exp(d - m_t[..., None]) * jnp.einsum('bhtd,bhsd->bhts', qc, kc)
        num = w_inter[..., None] * jnp.einsum('bhtd,bhde->bhte', qc, c) + jnp.einsum('bhts,bhse->bhte', s, vc)
        den = w_inter * jnp.einsum('bhtd,bhd->bht', qc, n) + jnp.sum(s, axis=-1)
        out = num / jnp.maximum(jnp.abs(den), jnp.exp(-m_t))[..., None]
        b_last = bcum[..., -1]
        lw = b_last[..., None] - bcum + lic
        m_new = jnp.maximum(m + b_last, jnp.max(lw, axis=-1))
        decay = jnp.exp(m + b_last - m_new)
        wk = jnp.exp(lw - m_new[..., None])[..., None] * kc
        c_new = decay[..., None, None] * c + jnp.einsum('bhsd,bhse->bhde', wk, vc)
        n_new = decay[..., None] * n + jnp.sum(wk, axis=2)
        return (c_new, n_new, m_new), out

    xs = (blocks(q), blocks(k), blocks(v), blocks(log_i), blocks(log_f))
    (c1, n1, m1), hs = lax.scan(step, (c0, n0, m0), xs)
    hs = jnp.moveaxis(jnp.moveaxis(hs, 3, 2), 0, 1).reshape(b, t, h, dh)
    return hs, c1, n1, m1

def hierarchical_moe(h, w_rg, b_rg, w_re, b_re, w_gate, w_up, w_down):
    shp = h.shape
    hf = h.reshape(-1, shp[-1])
    g_logits = (hf @ w_rg + b_rg).astype(jnp.float32)
    g_sel = jnp.argmax(g_logits, axis=-1)
    p_grp = jnp.take_along_axis(jax.nn.softmax(g_logits, axis=-1), g_sel[:, None], axis=-1)
    e_logits = (hf @ w_re + b_re).astype(jnp.float32).reshape(-1, N_GROUPS, EXPERTS_PER_GROUP)
    e_in = jnp.take_along_axis(e_logits, g_sel[:, None, None], axis=1)[:, 0]
    top_v, top_i = lax.top_k(e_in, TOP_K_IN_GROUP)
    top_w = jax.nn.softmax(top_v, axis=-1) * p_grp
    expert_id = g_sel[:, None] * EXPERTS_PER_GROUP + top_i
    combine = jnp.sum(jax.nn.one_hot(expert_id, N_EXPERTS, dtype=jnp.float32) * top_w[..., None], axis=1).astype(h.dtype)
    out = jnp.zeros_like(hf)
    for e in range(N_EXPERTS):
        he = jax.nn.silu(hf @ w_gate[e]) * (hf @ w_up[e])
        out = out + combine[:, e:e + 1] * (he @ w_down[e])
    return out.reshape(shp)

def hybrid_layer(x, p, mconv_buf, sconv_buf, c0, n0, m0,
                 g_mix, w_in, w_mconv, w_q, w_k, b_i, b_f, g_head, w_a, w_sconv, w_sout, w_o,
                 g_ffn, w_rg, b_rg, w_re, b_re, w_gate, w_up, w_down, g_ple, w_ple_gate, w_ple_proj):
    bsz, t, _ = x.shape
    f32 = jnp.float32
    h = rms_norm(x, g_mix)
    sizes = (D_MLSTM, D_MLSTM, D_MLSTM, M_HEADS, M_HEADS, D_SCONV, D_SCONV, D_SCONV, D_MODEL, D_MODEL)
    points = [int(s) for s in np.cumsum(sizes)[:-1]]
    xm, v, o_pre, i_pre, f_pre, s_b, s_c, s_x, gate_a, gate_b = jnp.split(h @ w_in, points, axis=-1)
    xq, mconv_new = causal_depthwise_conv(xm, mconv_buf, w_mconv)
    xq = jax.nn.silu(xq).reshape(bsz, t, M_HEADS, M_HEAD_DIM)
    q = jnp.einsum('bthd,hde->bthe', xq, w_q).astype(f32) * (M_HEAD_DIM ** -0.5)
    k = jnp.einsum('bthd,hde->bthe', xq, w_k).astype(f32)
    vh = v.reshape(bsz, t, M_HEADS, M_HEAD_DIM).astype(f32)
    log_i = (i_pre + b_i).astype(f32)
    log_f = jax.nn.log_sigmoid((f_pre + b_f).astype(f32))
    hm, c1, n1, m1 = mlstm_chunkwise(q, k, vh, log_i, log_f, c0.astype(f32), n0.astype(f32), m0.astype(f32))
    hm = hm * lax.rsqrt(jnp.mean(hm * hm, axis=-1, keepdims=True) + RMS_EPS) * g_head.astype(f32)
    y_a = (jax.nn.sigmoid(o_pre) * hm.reshape(bsz, t, D_MLSTM).astype(x.dtype)) @ w_a
    u, sconv_new = causal_depthwise_conv(s_c * s_x, sconv_buf, w_sconv)
    y_b = (s_b * u) @ w_sout
    merged = jax.nn.sigmoid(gate_a) * y_a + jax.nn.sigmoid(gate_b) * y_b
    x = x + merged @ w_o
    x = x + hierarchical_moe(rms_norm(x, g_ffn), w_rg, b_rg, w_re, b_re, w_gate, w_up, w_down)
    x = x + jax.nn.sigmoid(rms_norm(x, g_ple) @ w_ple_gate) * (p.astype(x.dtype) @ w_ple_proj)
    return x, c1, n1, m1, mconv_new, sconv_new

def setup_inputs(seed: int = 0) -> dict:
    key = jax.random.key(seed)
    ks = iter(jax.random.split(key, 48))
    f32 = jnp.float32
    L = DEPTH

    def nrm(shape, scale):
        return jax.random.normal(next(ks), shape, f32) * scale

    def gain(shape):
        return 1.0 + nrm(shape, 0.05)

    return {
        'x_prompt': nrm((BATCH, SEQ, D_MODEL), 1.0),
        'x_sample': nrm((DEC_BATCH, DEC_SEQ, D_MODEL), 1.0),
        'p_prompt': nrm((DEPTH, BATCH, SEQ, PLE_DIM), 1.0),
        'p_sample': nrm((DEPTH, DEC_BATCH, DEC_SEQ, PLE_DIM), 1.0),
        'state_mlstm_C': nrm((DEPTH, DEC_BATCH, M_HEADS, M_HEAD_DIM, M_HEAD_DIM), M_HEAD_DIM ** -0.5),
        'state_mlstm_n': nrm((DEPTH, DEC_BATCH, M_HEADS, M_HEAD_DIM), 1.0),
        'state_mlstm_m': nrm((DEPTH, DEC_BATCH, M_HEADS), 1.0),
        'state_mlstm_conv': nrm((DEPTH, DEC_BATCH, M_CONV_W - 1, D_MLSTM), 1.0),
        'state_sconv': nrm((DEPTH, DEC_BATCH, S_CONV_W - 1, D_SCONV), 1.0),
        'g_mix': gain((L, D_MODEL)),
        'w_in': nrm((L, D_MODEL, D_IN), D_MODEL ** -0.5),
        'w_mconv': nrm((L, M_CONV_W, D_MLSTM), M_CONV_W ** -0.5),
        'w_q': nrm((L, M_HEADS, M_HEAD_DIM, M_HEAD_DIM), M_HEAD_DIM ** -0.5),
        'w_k': nrm((L, M_HEADS, M_HEAD_DIM, M_HEAD_DIM), M_HEAD_DIM ** -0.5),
        'b_i': nrm((L, M_HEADS), 0.1),
        'b_f': jnp.linspace(3.0, 6.0, M_HEADS, dtype=f32)[None, :] + nrm((L, M_HEADS), 0.1),
        'g_head': gain((L, M_HEADS, M_HEAD_DIM)),
        'w_a': nrm((L, D_MLSTM, D_MODEL), D_MLSTM ** -0.5),
        'w_sconv': nrm((L, S_CONV_W, D_SCONV), S_CONV_W ** -0.5),
        'w_sout': nrm((L, D_SCONV, D_MODEL), D_SCONV ** -0.5),
        'w_o': nrm((L, D_MODEL, D_MODEL), D_MODEL ** -0.5),
        'g_ffn': gain((L, D_MODEL)),
        'w_rg': nrm((L, D_MODEL, N_GROUPS), D_MODEL ** -0.5),
        'b_rg': nrm((L, N_GROUPS), 0.01),
        'w_re': nrm((L, D_MODEL, N_EXPERTS), D_MODEL ** -0.5),
        'b_re': nrm((L, N_EXPERTS), 0.01),
        'w_gate': nrm((L, N_EXPERTS, D_MODEL, D_EXPERT), D_MODEL ** -0.5),
        'w_up': nrm((L, N_EXPERTS, D_MODEL, D_EXPERT), D_MODEL ** -0.5),
        'w_down': nrm((L, N_EXPERTS, D_EXPERT, D_MODEL), D_EXPERT ** -0.5),
        'g_ple': gain((L, D_MODEL)),
        'w_ple_gate': nrm((L, D_MODEL, D_MODEL), D_MODEL ** -0.5),
        'w_ple_proj': nrm((L, PLE_DIM, D_MODEL), PLE_DIM ** -0.5),
        'g_final': gain((D_MODEL,)),
    }

def reference(x_prompt, x_sample, p_prompt, p_sample, state_mlstm_C, state_mlstm_n, state_mlstm_m,
              state_mlstm_conv, state_sconv, g_mix, w_in, w_mconv, w_q, w_k, b_i, b_f, g_head, w_a,
              w_sconv, w_sout, w_o, g_ffn, w_rg, b_rg, w_re, b_re, w_gate, w_up, w_down,
              g_ple, w_ple_gate, w_ple_proj, g_final):
    f32 = jnp.float32
    bp = x_prompt.shape[0]
    yp, ys = x_prompt, x_sample
    new_p, new_s = [], []
    for i in range(DEPTH):
        lw = [a[i] for a in (g_mix, w_in, w_mconv, w_q, w_k, b_i, b_f, g_head, w_a, w_sconv, w_sout, w_o,
                             g_ffn, w_rg, b_rg, w_re, b_re, w_gate, w_up, w_down, g_ple, w_ple_gate, w_ple_proj)]
        yp, *st_p = hybrid_layer(
            yp, p_prompt[i],
            jnp.zeros((bp, M_CONV_W - 1, D_MLSTM), yp.dtype),
            jnp.zeros((bp, S_CONV_W - 1, D_SCONV), yp.dtype),
            jnp.zeros((bp, M_HEADS, M_HEAD_DIM, M_HEAD_DIM), f32),
            jnp.zeros((bp, M_HEADS, M_HEAD_DIM), f32),
            jnp.zeros((bp, M_HEADS), f32),
            *lw)
        ys, *st_s = hybrid_layer(
            ys, p_sample[i], state_mlstm_conv[i], state_sconv[i],
            state_mlstm_C[i], state_mlstm_n[i], state_mlstm_m[i], *lw)
        new_p.append(st_p)
        new_s.append(st_s)

    def stack(sts, j):
        return jnp.stack([s[j] for s in sts])

    y_prompt = rms_norm(yp, g_final)
    y_sample = rms_norm(ys, g_final)
    return (y_prompt, y_sample,
            stack(new_p, 0), stack(new_p, 1), stack(new_p, 2), stack(new_p, 3), stack(new_p, 4),
            stack(new_s, 0), stack(new_s, 1), stack(new_s, 2), stack(new_s, 3), stack(new_s, 4))


_drawn_inputs = setup_inputs


def setup_inputs(seed=0):
    import zlib

    import numpy as np

    out = dict(_drawn_inputs(seed))
    spreads = {}
    factors = {'b_rg': 8.0, 'b_re': 3.587, 'g_ple': 7.284}
    for name, (base, spread) in spreads.items():
        noise = np.random.default_rng([zlib.crc32(name.encode()), seed]).standard_normal(out[name].shape)
        drawn = base * np.exp(spread * noise) if base else spread * noise
        out[name] = __import__('jax').numpy.asarray(drawn.astype(out[name].dtype))
    for name, factor in factors.items():
        out[name] = (out[name] * factor).astype(out[name].dtype)
    return out
```

```python
from contextlib import ExitStack

import numpy as np
import concourse.bass as bass
from concourse import mybir

F32 = mybir.dt.float32
I32 = mybir.dt.int32
ALU = mybir.AluOpType
ACT = mybir.ActivationFunctionType
AX = mybir.AxisListType

P = 128
D = 1024
KD = D // P
TP, NB, TS = 256, 8, 8
NS = NB * TS
T = TP + NS
TILES = [(0, 128), (128, 128), (256, 64)]
H, DH = 4, 256
E, G, EG = 32, 4, 8
FE = 256
PLE = 256
EPS = 1e-6
NEG = -1e30
CAP = 64
PAIRS = 2 * T
SLOTS = PAIRS + CAP
ST = PAIRS // P
JX = T // CAP - 1
MAXB = 9
RING = 3
FIRST = RING + E % RING
WR = 2
ACC = 3
XM, VV, OO, IF, SB, SC, SX, GA, GB = 0, 1024, 2048, 3072, 3080, 4104, 5128, 6152, 7176
R_MIX, R_HEAD, R_FFN, R_PLE, R_FIN, R_MCW, R_SCW, R_MCH, R_SCH, R_ALL = 0, 1, 2, 3, 4, 5, 9, 12, 36, 52
PX, SXX = TP + 3, TS + 3
PU, SU = TP + 2, TS + 2
XE, UE = PX + NB * SXX, PU + NB * SU


def slot(e):
    return e % RING


def hybrid_step(nc, I, O):
    with ExitStack() as ctx:
        plan = {}
        base = [nc.sbuf_base + (-nc.sbuf_base) % 64]

        def at(name, shape, offset, dt=F32):
            plan[name] = (offset, offset + 4 * int(np.prod(shape[1:])))
            return nc.alloc_sbuf_tensor_at(name, shape, dt, offset=offset)

        def new(name, shape, dt=F32):
            t = at(name, shape, base[0], dt)
            base[0] = plan[name][1] + (-plan[name][1]) % 64
            return t

        def sem(name):
            return ctx.enter_context(nc.semaphore(name))

        ident = new("ident", [P, P])
        ones = new("ones", [P, P])
        cols = new("cols", [P, KD, R_ALL])
        eps = new("eps", [P, 1])
        xT = new("xT", [P, KD, T])
        hT = new("hT", [P, KD, 3 * P])
        pT = new("pT", [P, 2, T])
        root = new("root", [P, T])
        rstd = new("rstd", [P, T])
        wring = new("wring", [P, WR, KD, 512])
        wr36 = new("wr36", [P, KD, G + E])
        wif = new("wif", [P, KD, 2 * H])
        brow = new("brow", [1, G + E])
        phase = base[0]

        vn = new("vn", [P, 3, D])
        kn = new("kn", [P, 2, 3, DH])
        qT = new("qT", [P, 2, 2, T])
        kT = new("kT", [P, 2, 2, T])
        s1 = new("s1", [P, KD, T])
        xme = new("xme", [P, KD, XE])
        cxe = at("cxe", [P, KD, UE], plan["xme"][0])
        cv_all = new("cv", [P, KD, XE])
        u_all = at("uT", [P, KD, UE], plan["cv"][0])
        cv, uT = cv_all[:, :, 0:XE - 3], u_all[:, :, 0:UE - 2]
        xq = new("xq", [P, KD, T])
        s4 = new("s4", [P, KD, T])
        cbuf = new("cbuf", [P, NB, 2, DH])
        oT = at("oT", [P, KD, T], plan["cbuf"][0])
        xnat = at("xnat", [P, 3, D], plan["cbuf"][0])
        sqx = at("sqx", [P, KD, T], plan["s1"][0])
        rowsn = at("rowsn", [R_ALL, D], plan["s4"][0])
        pnat = at("pnat", [P, 3, PLE], plan["s4"][0] + 4096)
        nnat = at("nnat", [NB * H, DH], plan["s4"][0] + 8192)
        wqk = new("wqk", [P, 2, 2, DH])
        rows = new("rows", [H, 8, T])
        m0r = new("m0r", [H, NB])
        mo = new("mo", [H, NB + 1])
        bif = new("bif", [H, 2])
        selh = new("selh", [H, H, P])
        mask = new("mask", [P, 448])
        expo = new("expo", [P, 448])
        pt = new("pt", [P, 448])
        awT = new("awT", [P, 2, 3, H])
        oneb = new("oneb", [NS, NB])
        wsel = new("wsel", [NS, H, NB])
        wint = new("wint", [P, NS])
        qw = new("qw", [P, 2, NS])
        qn = new("qn", [P, 2, NS])
        wkm = new("wkm", [NS, NB, DH])
        wkp = new("wkp", [P, 2, DH])
        cpn = new("cpn", [P, 2, DH])
        nT = new("nT", [P, 2, NB * H])
        nnT = new("nnT", [P, 2, NB * H + H])
        den = new("den", [P, T])
        ssT = new("ssT", [P, H, T])
        tailc = new("tailc", [P, KD, 27])
        tailu = new("tailu", [P, KD, 18])
        hsq = at("hsq", [P, 2, T], plan["expo"][0])
        mixer_end = base[0]
        assert mixer_end <= nc.sbuf_usable_end, mixer_end
        tailn = at("tailn", [27, D], plan["s4"][0])
        tails = at("tails", [18, D], plan["cbuf"][0] + 4 * KD * T)
        nno = at("nno", [NB * H + H, DH], plan["wkm"][0])

        base[0] = phase
        eg = [None] * RING
        eu = [None] * RING
        ed = [None] * RING
        for s in range(RING):
            eg[s] = new(f"eg{s}", [P, KD, FE])
            eu[s] = new(f"eu{s}", [P, KD, FE])
            ed[s] = new(f"ed{s}", [P, 2, D])
        xs = new("xs", [P, KD, SLOTS])
        ys = new("ys", [P, KD, SLOTS])
        hn = at("hn", [P, 3, D], plan["ys"][0])
        ynat = at("ynat", [P, ST, D], plan["eg0"][0])
        x4n = at("x4n", [P, 3, D], plan["xs"][0])
        sqm = at("sqm", [P, KD, T], plan["xs"][0])
        gsel = new("gsel", [P, 3, PAIRS])
        base[0] += 512
        wcT = new("wcT", [P, ST, T])
        ppr = at("ppr", [P, KD, T], plan["ys"][0])
        wpp = at("wpp", [P, 2, D], plan["gsel"][0])
        sg = new("sg", [P, RING, 2, CAP])
        eh = new("eh", [P, RING, 2, CAP])
        lg = new("lg", [P, 3, G + E])
        r4 = new("r4", [P, 3, 4, G])
        r8 = new("r8", [P, 3, 8, EG])
        r1 = new("r1", [P, 3, 12])
        pick = new("pick", [P, 2, 3, E])
        m32 = new("m32", [P, 3, E])
        pos = new("pos", [P, 3, E])
        tri = new("tri", [P, P])
        io4 = new("io4", [P, G])
        io8 = new("io8", [P, EG])
        valid = new("valid", [P, 3])
        cnt = new("cnt", [P, 3, E])
        blk = new("blk", [1, 4, JX, E])
        ioe = new("ioe", [1, JX, E])
        ioj = new("ioj", [1, JX, E])
        wl = new("wl", [1, 2 * MAXB + 1])
        offi = new("offi", [1, E], I32)
        wli = new("wli", [1, 2 * MAXB + 1], I32)
        ys_tmp = at("ys_tmp", [P, 3, PAIRS], plan["ys"][0] + 12288)
        ios = at("ios", [P, PAIRS], plan["wcT"][0])
        assert base[0] <= nc.sbuf_usable_end, base[0]

        bank = [ctx.enter_context(nc.psum_tensor(f"bank{i}", [P, 512], F32)) for i in range(8)]
        b_enm, b_s, b_bc, b_num = bank[3], bank[4], bank[5], (bank[6], bank[7])

        fills = [("x", k) for k in range(KD)] + [("rows",), ("nn",), ("pn", 0), ("pn", 1), ("ss", 0)]
        who = {("rows",): "dve", ("nn",): "dve"}

        def section(name, by, n=KD):
            for m in range(n):
                fills.append((name, m))
                who[(name, m)] = by

        section("xm", "act")
        section("if", "dve", 2)
        section("v", "act", 6)
        section("aw", "dve", 1)

        def qk_fills(h):
            fills.extend([("qk", h, n) for n in range(4)] + [("kn", h, n) for n in range(3)])

        def state_fills(h):
            for f in [("C", h, b) for b in range(NB)] + [("Cp", h), ("n", h)]:
                fills.append(f)
                who[f] = "act" if f[0] == "Cp" else "dve"

        MID = [("sc", "act"), ("sx", "dve"), ("sb", "dve"), ("gb", "act")]
        qk_fills(0)
        section("to", "act", 2)
        qk_fills(1)
        for h in range(H):
            section(*MID[h])
            state_fills(h)
            if h + 2 < H:
                qk_fills(h + 2)
        section("tn", "act", 1)
        section("tu", "act", 2)
        section("o", "act")
        section("sout", "dve")
        section("ga", "act")
        section("a", "dve")
        section("wo", "dve")
        fills.append(("ss", 1))
        section("lg", "dve", 1)
        section("hn", "act", 6)
        section("rank", "dve", 1)
        section("xs", "act", 2 * KD)
        section("wc", "act", ST)
        section("yn", "act", 2 * ST)
        section("mo", "dve")
        section("pp", "act")
        fills.append(("ss", 2))
        section("pg", "act")
        fills.append(("ss", 3))
        section("yo", "act", 6)
        index = {f: n for n, f in enumerate(fills)}
        emptied = {}
        done = {"act": 0, "dve": 0}
        for f in fills:
            w = who.setdefault(f, "act")
            done[w] += 1
            emptied[f] = (w, done[w])

        acc_full = sem("acc_full")
        acc_empty = {"act": sem("acc_empty_act"), "dve": sem("acc_empty_dve")}

        def acc(f):
            return bank[index[f] % ACC]

        def refill(pe, f):
            if index[f] >= ACC:
                w, n = emptied[fills[index[f] - ACC]]
                pe.wait_ge(acc_empty[w], n)

        def moved(eng, f):
            w, n = emptied[f]
            eng.wait_ge(acc_empty[w], n)

        def filled(eng, f):
            eng.wait_ge(acc_full, index[f] + 1)

        order = ["xm", "v", "sc", "sx", "sb", "gb", "o", "sout", "ga", "a", "wo", "pg"]
        w_in = I["w_in"][0]
        source = {"xm": w_in[:, XM:XM + D], "v": w_in[:, VV:VV + D], "o": w_in[:, OO:OO + D],
                  "sb": w_in[:, SB:SB + D], "sc": w_in[:, SC:SC + D], "sx": w_in[:, SX:SX + D],
                  "ga": w_in[:, GA:GA + D], "gb": w_in[:, GB:GB + D], "a": I["w_a"][0],
                  "sout": I["w_sout"][0], "wo": I["w_o"][0], "pg": I["w_ple_gate"][0]}
        halves = [(s, j) for s in order for j in range(2)]
        w_landed = [sem(f"w_landed{i}") for i in range(WR)]

        def weights(eng, s, j):
            n = halves.index((s, j))
            eng.wait_ge(w_landed[n % WR], 16 * (n // WR + 1))
            return wring[:, n % WR]

        in_x = sem("in_x"); in_rows = sem("in_rows"); in_small = sem("in_small"); in_m0 = sem("in_m0")
        consts = sem("consts"); pool_step = sem("pool_step"); dve_step = sem("dve_step"); act_step = sem("act_step")
        x_ready = sem("x_ready"); cols_ready = sem("cols_ready"); sq_ready = sem("sq_ready")
        root_ready = sem("root_ready"); h_ready = sem("h_ready")
        xm_ready = sem("xm_ready"); conv_done = sem("conv_done"); sig_ready = sem("sig_ready"); xq_ready = sem("xq_ready")
        gate_step = sem("gate_step"); gate_act = sem("gate_act"); rows_ready = sem("rows_ready"); aw_ready = sem("aw_ready")
        wqk_landed = sem("wqk_landed"); wqk_used = sem("wqk_used"); qk_ready = sem("qk_ready")
        scores_full = sem("scores_full"); args_ready = sem("args_ready"); exps_ready = sem("exps_ready")
        probs_ready = sem("probs_ready"); c_landed = sem("c_landed"); c_updated = sem("c_updated"); c_stored = sem("c_stored")
        pv_full = sem("pv_full"); enm_used = sem("enm_used"); hm_ready = sem("hm_ready"); hsq_ready = sem("hsq_ready")
        ss_full = sem("ss_full"); ss_taken = sem("ss_taken"); wk_ready = sem("wk_ready"); states_full = sem("states_full")
        cp_ready = sem("cp_ready"); cp_stored = sem("cp_stored"); n_ready = sem("n_ready"); tails_ready = sem("tails_ready")
        rows_out = sem("rows_out"); stored = sem("stored"); u_ready = sem("u_ready"); su_ready = sem("su_ready")
        o_ready = sem("o_ready"); ga_ready = sem("ga_ready"); ya_ready = sem("ya_ready"); merged = sem("merged")
        hroot = sem("hroot"); x2_ready = sem("x2_ready"); m_ready = sem("m_ready"); gb_ready = sem("gb_ready")
        lg_ready = sem("lg_ready"); rt_exp = sem("rt_exp"); rt_arg = sem("rt_arg"); m32_ready = sem("m32_ready")
        gsel_ready = sem("gsel_ready"); gw_ready = sem("gw_ready"); hn_ready = sem("hn_ready"); xs_ready = sem("xs_ready")
        offs_ready = sem("offs_ready"); wc_ready = sem("wc_ready")
        e_landed = [sem(f"e_landed{s}") for s in range(RING)]
        gu_full = sem("gu_full"); esig_ready = sem("esig_ready"); eh_ready = sem("eh_ready")
        y_full = sem("y_full"); ys_ready = sem("ys_ready"); est = sem("est")
        xb_landed = sem("xb_landed"); xb_gu = sem("xb_gu"); xb_sig = sem("xb_sig"); xb_h = sem("xb_h"); xb_st = sem("xb_st")
        xb_y = sem("xb_y"); xb_done = sem("xb_done")
        late_full = sem("late_full"); late_act = sem("late_act"); late_dve = sem("late_dve"); wpp_landed = sem("wpp_landed")
        consts2 = sem("consts2"); out_stored = sem("out_stored"); experts_done = sem("experts_done"); mo_ready = sem("mo_ready")

        hist_ready = sem("hist_ready"); tailn_stored = sem("tailn_stored"); x4_ready = sem("x4_ready")
        cbuf_rows = cbuf[:, :, :, :].rearrange("p b d e -> p b (d e)")
        cv_sample = lambda k: cv_all[:, k, PX:PX + NB * SXX].rearrange("p (b j) -> p b j", b=NB)[:, :, 0:TS]
        uT_sample = lambda k: u_all[:, k, PU:PU + NB * SU]

        def step(eng, signal, count):
            def go(ins):
                count[0] += 1
                ins.then_inc(signal, 1)
                eng.wait_ge(signal, count[0])
            return go

        ctx.enter_context(nc.allow_non_contiguous_dma(reason="gate biases and m: 4 to 32 elements"))
        block = ctx.enter_context(nc.Block())

        @block.sync
        def _(sp):
            for i, (t0, n) in enumerate(TILES):
                src = I["x_prompt"][0, t0:t0 + n] if i < 2 else I["x_sample"].rearrange("b t d -> (b t) d")
                sp.dma_start(xnat[0:n, i, :], src).then_inc(in_x, 16)
            one = lambda a: a.rearrange("(a d) -> a d", a=1)
            for r, src in ((R_MIX, I["g_mix"]), (R_HEAD, I["g_head"].rearrange("a h d -> a (h d)")), (R_FFN, I["g_ffn"]),
                           (R_PLE, I["g_ple"]), (R_FIN, one(I["g_final"])), (R_MCW, I["w_mconv"][0]), (R_SCW, I["w_sconv"][0]),
                           (R_MCH, I["state_mlstm_conv"][0].rearrange("b j d -> (b j) d")),
                           (R_SCH, I["state_sconv"][0].rearrange("b j d -> (b j) d"))):
                sp.dma_start(rowsn[r:r + src.shape[0], :], src).then_inc(in_rows, 16)
            for i, (t0, n) in enumerate(TILES):
                src = I["p_prompt"][0, 0, t0:t0 + n] if i < 2 else I["p_sample"][0].rearrange("b t d -> (b t) d")
                sp.dma_start(pnat[0:n, i, :], src).then_inc(in_rows, 16)
            sp.dma_start(nnat[:, :], I["state_mlstm_n"][0].rearrange("b h d -> (b h) d")).then_inc(in_rows, 16)

            def half(n):
                s, j = halves[n]
                if n >= WR:
                    before, i = halves[n - WR]
                    sp.wait_ge(acc_full, index[(before, 3 * i + 2 if before == "v" else 4 * i + 3)] + 1)
                sp.dma_start(wring[:, n % WR], source[s][:, 512 * j:512 * j + 512].rearrange("(k p) c -> p k c", p=P))\
                    .then_inc(w_landed[n % WR], 16)

            half(0)
            half(1)
            sp.dma_start(wif[:, :, :], w_in[:, IF:IF + 2 * H].rearrange("(k p) c -> p k c", p=P)).then_inc(in_small, 16)
            sp.dma_start(bif[:, 0:1], I["b_i"].rearrange("a h -> h a")).then_inc(in_small, 16)
            sp.dma_start(bif[:, 1:2], I["b_f"].rearrange("a h -> h a")).then_inc(in_small, 16)
            sp.dma_start(m0r[:, :], I["state_mlstm_m"][0].rearrange("b h -> h b")).then_inc(in_small, 16)
            sp.dma_start(brow[:, 0:G], I["b_rg"]).then_inc(in_small, 16)
            sp.dma_start(brow[:, G:G + E], I["b_re"]).then_inc(in_small, 16)
            sp.dma_start(wr36[:, :, 0:G], I["w_rg"][0].rearrange("(k p) c -> p k c", p=P)).then_inc(in_small, 16)
            sp.dma_start(wr36[:, :, G:G + E], I["w_re"][0].rearrange("(k p) c -> p k c", p=P)).then_inc(in_small, 16)
            for n in range(WR, 2 * order.index("pg")):
                half(n)
            w_g, w_u, w_d = I["w_gate"][0], I["w_up"][0], I["w_down"][0]

            def expert(e, s, signal):
                dyn = not isinstance(e, int)
                pick_ = lambda w: (w[bass.ds(e, 1)] if dyn else w[e:e + 1])
                sp.dma_start(eg[s][:, :, :], pick_(w_g).rearrange("a (k p) c -> p (a k) c", p=P)).then_inc(signal, 16)
                sp.dma_start(eu[s][:, :, :], pick_(w_u).rearrange("a (k p) c -> p (a k) c", p=P)).then_inc(signal, 16)
                sp.dma_start(ed[s][:, :, :], pick_(w_d).rearrange("a (k p) c -> p (a k) c", p=P)).then_inc(signal, 16)

            moved(sp, ("wo", KD - 1))
            sp.wait_ge(stored, 16 * 6)
            sp.wait_ge(tailn_stored, 32)
            sp.wait_ge(c_stored, 16 * H)
            sp.wait_ge(cp_stored, 16 * H)
            for e in range(RING):
                expert(e, slot(e), e_landed[slot(e)])
            with sp.Fori(0, (E - FIRST) // RING) as i:
                for j in range(RING):
                    sp.wait_ge(y_full, 3 * i + (j + 1))
                    expert(3 * i + (RING + j), slot(RING + j), e_landed[slot(RING + j)])
            for e in (E - 2, E - 1):
                sp.wait_ge(y_full, e + 1 - RING)
                expert(e, slot(e), e_landed[slot(e)])
            half(2 * order.index("pg"))
            half(2 * order.index("pg") + 1)
            sp.wait_ge(offs_ready, 1)
            extra = sp.value_load(wli[0:1, 2 * MAXB:2 * MAXB + 1], min_val=0, max_val=MAXB)
            sp.wait_ge(ys_ready, E)
            with sp.If(extra > 0):
                with sp.Fori(0, extra) as i:
                    sp.wait_ge(xb_done, i + 1)
                    e = sp.value_load(wli[0:1, bass.ds(i, 1)], min_val=0, max_val=E - 1)
                    expert(e, 0, xb_landed)
            moved(sp, ("wc", ST - 1))
            sp.dma_start(wpp[:, :, :], I["w_ple_proj"][0].rearrange("(k p) c -> p k c", p=P)).then_inc(wpp_landed, 16)

            for i, (t0, n) in enumerate(TILES):
                last = ("yo", 2 * i + 1)
                moved(sp, last)
                dst = O[0][0, t0:t0 + n] if i < 2 else O[1].rearrange("b t d -> (b t) d")
                sp.dma_start(dst, x4n[0:n, i, :]).then_inc(out_stored, 16)
            sp.wait_ge(out_stored, 16 * 3)

        @block.tensor
        def _(pe):
            def fill(f, mms):
                refill(pe, f)
                mms(acc(f)).then_inc(acc_full, 1)

            def linear(name, rhs):
                for m in range(KD):
                    if m % 4 == 0:
                        w = weights(pe, name, m // 4)
                    def mms(bk):
                        for k in range(KD):
                            last = pe.matmul(bk[:, 0:T], w[:, k, (m % 4) * P:(m % 4) * P + P], rhs[:, k, 0:T],
                                             start=(k == 0), stop=(k == KD - 1))
                        return last
                    fill((name, m), mms)

            pe.wait_ge(consts, 1)
            pe.wait_ge(in_x, 16 * 3)
            for k in range(KD):
                def mms(bk):
                    for i, (t0, n) in enumerate(TILES):
                        last = pe.transpose(bk[:, t0:t0 + n], xnat[0:n, i, k * P:k * P + P], ident[0:n, 0:n])
                    return last
                fill(("x", k), mms)
            pe.wait_ge(in_rows, 16 * 13)

            def mms(bk):
                for k in range(KD):
                    last = pe.transpose(bk[:, k * R_ALL:(k + 1) * R_ALL], rowsn[:, k * P:k * P + P], ident[0:R_ALL, 0:R_ALL])
                return last
            fill(("rows",), mms)

            def mms(bk):
                for c in range(2):
                    last = pe.transpose(bk[:, c * 32:c * 32 + 32], nnat[:, c:DH:2], ident[0:32, 0:32])
                return last
            fill(("nn",), mms)
            for c in range(2):
                def mms(bk):
                    for i, (t0, n) in enumerate(TILES):
                        last = pe.transpose(bk[:, t0:t0 + n], pnat[0:n, i, c * P:c * P + P], ident[0:n, 0:n])
                    return last
                fill(("pn", c), mms)

            def sums(f, sq, n=KD):
                def mms(bk):
                    for k in range(n):
                        last = pe.matmul(bk[:, 0:T], ones[:, :], sq[:, k, :], start=(k == 0), stop=(k == n - 1))
                    return last
                fill(f, mms)

            pe.wait_ge(consts, 2)
            pe.wait_ge(sq_ready, 1)
            sums(("ss", 0), sqx)

            pe.wait_ge(h_ready, 1)
            linear("xm", hT)
            pe.wait_ge(in_small, 16 * 8)
            for g in range(2):
                def mms(bk):
                    for k in range(KD):
                        last = pe.matmul(bk[0:H, 0:T], wif[:, k, g * H:g * H + H], hT[:, k, 0:T], start=(k == 0), stop=(k == KD - 1))
                    return last
                fill(("if", g), mms)
            for j in range(2):
                w = weights(pe, "v", j)
                for i, (t0, n) in enumerate(TILES):
                    def mms(bk):
                        for k in range(KD):
                            last = pe.matmul(bk[0:n, :], hT[:, k, t0:t0 + n], w[:, k, :], start=(k == 0), stop=(k == KD - 1))
                        return last
                    fill(("v", 3 * j + i), mms)
            pe.wait_ge(rows_ready, 1)
            def mms(bk):
                for r, row in enumerate((0, 1)):
                    for i, (t0, n) in enumerate(TILES):
                        c = (3 * r + i) * H
                        last = pe.transpose(bk[0:n, c:c + H], rows[:, row, t0:t0 + n], ident[0:H, 0:H])
                return last
            fill(("aw", 0), mms)

            def qk(h):
                pe.wait_ge(wqk_landed, 32 * (h + 1))
                if h == 0:
                    pe.wait_ge(xq_ready, 1)
                for n in range(4):
                    r, c = divmod(n, 2)
                    def mms(bk):
                        for d in range(2):
                            last = pe.matmul(bk[:, 0:T], wqk[:, r, d, c:DH:2], xq[:, 2 * h + d, :], start=(d == 0), stop=(d == 1))
                        return last
                    fill(("qk", h, n), mms)
                for i, (t0, n) in enumerate(TILES):
                    def mms(bk):
                        for d in range(2):
                            last = pe.matmul(bk[0:n, 0:DH], xq[:, 2 * h + d, t0:t0 + n], wqk[:, 1, d, :], start=(d == 0), stop=(d == 1))
                        return last
                    fill(("kn", h, i), mms)

            def scores(h):
                p = h % 2
                moved(pe, ("qk", h, 3))
                if h == 0:
                    pe.wait_ge(rows_ready, 2)
                    pe.wait_ge(consts, 4)
                else:
                    pe.wait_ge(hm_ready, h)
                for (o, n, s0, sn, t0) in ((0, 256, 0, P, 0), (256, P, P, P, P), (384, NS, TP, NS, TP)):
                    for c in range(2):
                        last = pe.matmul(b_s[0:sn, o:o + n], kT[:, p, c, s0:s0 + sn], qT[:, p, c, t0:t0 + n], start=(c == 0), stop=(c == 1))
                pe.matmul(b_bc[:, 0:T], selh[:, h, :], rows[:, 2, :], start=True, stop=True)
                pe.matmul(b_bc[:, T:T + NS], selh[:, h, :], rows[:, 3, 0:NS], start=True, stop=True)
                if h:
                    pe.wait_ge(ss_taken, h)
                pe.matmul(b_enm[:, 0:T], selh[:, h, :], rows[:, 7, :], start=True, stop=True).then_inc(scores_full, 1)

            def pv(h):
                pe.wait_ge(probs_ready, h + 1)
                for i in range(3):
                    moved(pe, ("v", 3 + i))
                pe.wait_ge(c_landed, 16 * (h + 1))
                for c in range(2):
                    e0 = h * DH + c * P
                    bk = b_num[c]
                    pe.matmul(bk[:, 0:256], vn[:, 0, e0:e0 + P], pt[:, 0:256], start=True, stop=False, skip_group_check=True)
                    pe.matmul(bk[:, P:256], vn[:, 1, e0:e0 + P], pt[:, 256:384], start=False, stop=False, skip_group_check=True)
                    pe.matmul(bk[:, TP:T], vn[0:NS, 2, e0:e0 + P], pt[0:NS, 384:448], start=False, stop=False, skip_group_check=True)
                    for b in range(NB):
                        for d in range(2):
                            pe.matmul(bk[:, TP + b * TS:TP + (b + 1) * TS], cbuf[:, b, d, c * P:c * P + P], qw[:, d, b * TS:(b + 1) * TS],
                                      start=False, stop=(b == NB - 1 and d == 1), skip_group_check=True)
                pe.matmul(b_s[:, 0:256], ones[:, :], pt[:, 0:256], start=True, stop=False, skip_group_check=True)
                pe.matmul(b_s[:, P:256], ones[:, :], pt[:, 256:384], start=False, stop=False, skip_group_check=True)
                pe.matmul(b_s[:, TP:T], ones[0:NS, :], pt[0:NS, 384:448], start=False, stop=False, skip_group_check=True)
                for d in range(2):
                    last = pe.matmul(b_s[:, TP:T], ones[:, :], qn[:, d, :], start=False, stop=(d == 1), skip_group_check=True)
                last.then_inc(pv_full, 1)

            def states(h):
                pe.wait_ge(wk_ready, h + 1)
                for b in range(NB):
                    def mms(bk):
                        for d in range(2):
                            last = pe.matmul(bk[:, d * DH:(d + 1) * DH], wkm[:, b, d:DH:2], vn[0:NS, 2, h * DH:(h + 1) * DH], start=True, stop=True)
                        return last
                    fill(("C", h, b), mms)
                def mms(bk):
                    for d in range(2):
                        for i in range(2):
                            last = pe.matmul(bk[:, d * DH:(d + 1) * DH], wkp[:, i, d:DH:2], vn[:, i, h * DH:(h + 1) * DH], start=(i == 0), stop=(i == 1))
                    return last
                fill(("Cp", h), mms)
                def mms(bk):
                    for d in range(2):
                        for b in range(NB):
                            pe.matmul(bk[:, d * (NB + 1) + b:d * (NB + 1) + b + 1], wkm[:, b, d:DH:2], ones[0:NS, 0:1], start=True, stop=True)
                        for i in range(2):
                            last = pe.matmul(bk[:, d * (NB + 1) + NB:(d + 1) * (NB + 1)], wkp[:, i, d:DH:2], ones[:, 0:1], start=(i == 0), stop=(i == 1))
                    return last
                fill(("n", h), mms)

            def head_sums(h):
                pe.wait_ge(hsq_ready, h + 1)
                for c in range(2):
                    last = pe.matmul(b_enm[:, 0:T], ones[:, :], hsq[:, c, :], start=(c == 0), stop=(c == 1))
                last.then_inc(ss_full, 1)

            qk(0)
            for j in range(2):
                if j == 0:
                    pe.wait_ge(tails_ready, 1)
                def mms(bk):
                    for k in range(4):
                        last = pe.transpose(bk[0:27, k * P:k * P + P], tailc[:, 4 * j + k, :], ident[:, :])
                    return last
                fill(("to", j), mms)
            scores(0)
            qk(1)
            for h in range(H):
                linear(MID[h][0], hT)
                pv(h)
                states(h)
                head_sums(h)
                if h + 1 < H:
                    scores(h + 1)
                if h + 2 < H:
                    qk(h + 2)
            def mms(bk):
                for d in range(2):
                    last = pe.transpose(bk[0:36, d * P:d * P + P], nnT[:, d, :], ident[:, :])
                return last
            pe.wait_ge(n_ready, H)
            fill(("tn", 0), mms)
            for j in range(2):
                if j == 0:
                    pe.wait_ge(tails_ready, 2)
                def mms(bk):
                    for k in range(4):
                        last = pe.transpose(bk[0:18, k * P:k * P + P], tailu[:, 4 * j + k, :], ident[:, :])
                    return last
                fill(("tu", j), mms)
            linear("o", hT)
            moved(pe, ("sb", KD - 1))
            linear("sout", s1)
            linear("ga", hT)
            pe.wait_ge(ya_ready, 1)
            linear("a", oT)
            moved(pe, ("a", KD - 1))
            linear("wo", s4)

            pe.wait_ge(sq_ready, 2)
            sums(("ss", 1), sqm)
            pe.wait_ge(h_ready, 2)
            def mms(bk):
                for i in range(3):
                    o = bk[:, i * 36:i * 36 + 36]
                    pe.matmul(o, ones[0:1, :], brow[:, :], start=True, stop=False)
                    for k in range(KD):
                        last = pe.matmul(o, hT[:, k, i * P:i * P + P], wr36[:, k, :], start=False, stop=(k == KD - 1))
                return last
            fill(("lg", 0), mms)
            for i in range(3):
                for j in range(2):
                    def mms(bk):
                        for k in range(4):
                            last = pe.transpose(bk[:, k * P:k * P + P], hT[:, 4 * j + k, i * P:i * P + P], ident[:, :])
                        return last
                    fill(("hn", 2 * i + j), mms)
            pe.wait_ge(m32_ready, 1)
            def mms(bk):
                for i in range(3):
                    for q in range(i):
                        pe.matmul(bk[:, i * E:(i + 1) * E], ones[:, :], m32[:, q, :], start=(q == 0), stop=False)
                    pe.matmul(bk[:, i * E:(i + 1) * E], tri[:, :], m32[:, i, :], start=(i == 0), stop=True)
                for i in range(3):
                    last = pe.matmul(bk[:, 3 * E:4 * E], ones[:, :], m32[:, i, :], start=(i == 0), stop=(i == 2))
                return last
            fill(("rank", 0), mms)
            pe.wait_ge(gsel_ready, 1)
            moved(pe, ("hn", 5))
            for k in range(KD):
                for j in range(2):
                    def mms(bk):
                        for i in range(3):
                            last = pe.matmul(bk[:, 0:T], hn[:, i, k * P:k * P + P], gsel[:, i, j * T:j * T + T], start=(i == 0), stop=(i == 2))
                        return last
                    fill(("xs", 2 * k + j), mms)
            pe.wait_ge(gw_ready, 1)
            for s in range(ST):
                def mms(bk):
                    for i, (t0, n) in enumerate(TILES):
                        last = pe.transpose(bk[:, t0:t0 + n], gsel[0:n, i, s * P:s * P + P], ident[0:n, 0:n])
                    return last
                fill(("wc", s), mms)
            moved(pe, ("wc", ST - 1))
            moved(pe, ("xs", 2 * KD - 1))
            pe.wait_ge(offs_ready, 1)

            def ffn(off, s, landed, value, full, h_sem, h_value, free, y_done):
                pe.wait_ge(landed, value)
                gu, y = bank[s], bank[3 + s]
                for f in range(2):
                    for w, o in ((eg[s], 0), (eu[s], 2)):
                        for k in range(KD):
                            last = pe.matmul(gu[:, (o + f) * CAP:(o + f + 1) * CAP], w[:, k, f * P:f * P + P], xs[:, k, bass.ds(off, CAP)],
                                             start=(k == 0), stop=(k == KD - 1))
                last.then_inc(full, 1)
                if free is not None:
                    pe.wait_ge(*free)
                pe.wait_ge(h_sem, h_value)
                for m in range(KD):
                    for f in range(2):
                        last = pe.matmul(y[:, m * CAP:(m + 1) * CAP], ed[s][:, f, m * P:m * P + P], eh[:, s, f, :], start=(f == 0), stop=(f == 1))
                last.then_inc(y_done, 1)

            for e in range(FIRST):
                off = pe.value_load(offi[0:1, e:e + 1], min_val=0, max_val=PAIRS)
                ffn(off, slot(e), e_landed[slot(e)], 48 * (e // RING + 1), gu_full, eh_ready, e + 1,
                    (ys_ready, e + 1 - RING) if e >= RING else None, y_full)
            with pe.Fori(0, (E - FIRST) // RING) as i:
                for j in range(RING):
                    off = pe.value_load(offi[0:1, bass.ds(3 * i + (FIRST + j), 1)], min_val=0, max_val=PAIRS)
                    ffn(off, slot(FIRST + j), e_landed[slot(FIRST + j)], 48 * i + 48 * ((FIRST + j) // RING + 1),
                        gu_full, eh_ready, 3 * i + (FIRST + j + 1), (ys_ready, 3 * i + (FIRST + j + 1 - RING)), y_full)
            extra = pe.value_load(wli[0:1, 2 * MAXB:2 * MAXB + 1], min_val=0, max_val=MAXB)
            pe.wait_ge(ys_ready, E)
            with pe.If(extra > 0):
                with pe.Fori(0, extra) as i:
                    off = pe.value_load(wli[0:1, bass.ds(i + MAXB, 1)], min_val=0, max_val=PAIRS)
                    ffn(off, 0, xb_landed, 48 * i + 48, xb_gu, xb_h, i + 1, None, xb_y)
            pe.wait_ge(experts_done, 1)
            for s in range(ST):
                for j in range(2):
                    def mms(bk):
                        for k in range(4):
                            last = pe.transpose(bk[:, k * P:k * P + P], ys[:, 4 * j + k, s * P:s * P + P], ident[:, :])
                        return last
                    fill(("yn", 2 * s + j), mms)
            for n in (8, 9):
                moved(pe, ("yn", n))
            for k in range(KD):
                def mms(bk):
                    for s in range(ST):
                        last = pe.matmul(bk[:, 0:T], ynat[:, s, k * P:k * P + P], wcT[:, s, :], start=(s == 0), stop=(s == ST - 1))
                    return last
                fill(("mo", k), mms)
            pe.wait_ge(wpp_landed, 16)
            for k in range(KD):
                def mms(bk):
                    for c in range(2):
                        last = pe.matmul(bk[:, 0:T], wpp[:, c, k * P:k * P + P], pT[:, c, :], start=(c == 0), stop=(c == 1))
                    return last
                fill(("pp", k), mms)
            pe.wait_ge(sq_ready, 3)
            sums(("ss", 2), sqm)
            pe.wait_ge(h_ready, 3)
            linear("pg", hT)
            pe.wait_ge(sq_ready, 4)
            sums(("ss", 3), sqm)
            pe.wait_ge(h_ready, 4)
            for i, (t0, n) in enumerate(TILES):
                for j in range(2):
                    def mms(bk):
                        for k in range(4):
                            last = pe.transpose(bk[0:n, k * P:k * P + P], hT[:, 4 * j + k, t0:t0 + n], ident[:, :])
                        return last
                    fill(("yo", 2 * i + j), mms)

        @block.scalar
        def _(act):
            def take(f, *outs, func=ACT.Copy, scale=1.0, n=P):
                filled(act, f)
                for out, a in outs:
                    last = act.activation(out, a, func, scale=scale)
                last.then_inc(acc_empty["act"], 1)

            def wide(f):
                return acc(f)[:, 0:T]

            def norm(n, sq):
                act.activation(sq[:, :, :], xT[:, :, :], ACT.Square).then_inc(sq_ready, 1)

            def norm_root(n):
                filled(act, ("ss", n))
                if n:
                    act.wait_ge(h_ready, n)
                act.activation(root[:, :], wide(("ss", n)), ACT.Sqrt, bias=eps[:, 0:1], scale=1.0 / D).then_inc(acc_empty["act"], 1)

            for k in range(KD):
                take(("x", k), (xT[:, k, :], wide(("x", k))))
            for c in range(2):
                take(("pn", c), (pT[:, c, :], wide(("pn", c))))
            moved(act, ("x", KD - 1))
            norm(0, sqx)
            act.wait_ge(consts, 2)
            norm_root(0)
            act.wait_ge(hist_ready, 1)
            for m in range(KD):
                bk = acc(("xm", m))
                take(("xm", m), (xme[:, m, 3:PX], bk[:, 0:TP]),
                     (xme[:, m, PX:XE].rearrange("p (b j) -> p b j", b=NB)[:, :, 3:SXX], bk[:, TP:T].rearrange("p (b j) -> p b j", b=NB)))
            act.wait_ge(conv_done, 1)
            act.activation(xq[:, :, 0:TP], cv[:, :, 0:TP], ACT.Sigmoid)
            for k in range(KD):
                last = act.activation(xq[:, k, TP:T].rearrange("p (b j) -> p b j", b=NB),
                                      cv_sample(k), ACT.Sigmoid)
            last.then_inc(sig_ready, 1)
            for m in range(6):
                j, i = divmod(m, 3)
                n = TILES[i][1]
                take(("v", m), (vn[0:n, i, 512 * j:512 * j + 512], acc(("v", m))[0:n, :]))
            act.wait_ge(gate_step, 1)
            act.activation(rows[:, 2, :], rows[:, 2, :], ACT.Exp, scale=-1.0).then_inc(act_step, 1)
            act.wait_ge(act_step, 1)
            act.activation(rows[:, 2, :], rows[:, 2, :], ACT.Ln, bias=1.0).then_inc(gate_act, 1)
            act.wait_ge(gate_step, 2)
            act.activation(rows[:, 1, :], rows[:, 1, :], ACT.Exp).then_inc(rows_ready, 1)
            act.activation(rows[:, 3, 0:NS], rows[:, 3, 0:NS], ACT.Exp)
            act.activation(rows[:, 7, :], rows[:, 7, :], ACT.Exp, scale=-1.0).then_inc(rows_ready, 1)

            def take_qk(h):
                p = h % 2
                for n in range(4):
                    r, c = divmod(n, 2)
                    f = ("qk", h, n)
                    take(f, ((kT if r else qT)[:, p, c, :], wide(f)), scale=1.0 if r else DH ** -0.5)
                for i, (t0, n) in enumerate(TILES):
                    f = ("kn", h, i)
                    take(f, (kn[0:n, p, i, :], acc(f)[0:n, 0:DH]))

            def exps(h):
                act.wait_ge(args_ready, h + 1)
                for o, n, i, r in ((0, 256, 0, P), (256, P, 1, P), (384, NS, 2, NS)):
                    last = act.activation(expo[0:r, o:o + n], expo[0:r, o:o + n], ACT.Exp, bias=awT[0:r, 0, i, h:h + 1])
                last.then_inc(exps_ready, 1)

            take_qk(0)
            for j in range(2):
                if j == 0:
                    act.wait_ge(cols_ready, 1)
                    filled(act, ("pn", 1))
                take(("to", j), (tailn[:, 512 * j:512 * j + 512], acc(("to", j))[0:27, :]))
            exps(0)
            take_qk(1)
            for h in range(H):
                if MID[h][0] == "sc":
                    for m in range(KD):
                        take(("sc", m), (s1[:, m, :], wide(("sc", m))))
                if MID[h][0] == "gb":
                    act.wait_ge(tailn_stored, 32)
                    for m in range(KD):
                        take(("gb", m), (s4[:, m, :], wide(("gb", m))), func=ACT.Sigmoid)
                act.wait_ge(hm_ready, h + 1)
                act.activation(hsq[:, :, :], xq[:, 2 * h:2 * h + 2, :], ACT.Square).then_inc(hsq_ready, 1)
                if h:
                    act.wait_ge(cp_stored, 16 * h)
                take(("Cp", h), (cpn[:, :, :].rearrange("p a b -> p (a b)"), acc(("Cp", h))[:, :]))
                act.wait_ge(ss_full, h + 1)
                act.activation(ssT[:, h, :], b_enm[:, 0:T], ACT.Copy).then_inc(ss_taken, 1)
                if h + 1 < H:
                    exps(h + 1)
                if h + 2 < H:
                    take_qk(h + 2)
            act.wait_ge(c_stored, 16 * H)
            f = ("tn", 0)
            take(f, *[(nno[:, d:DH:2], acc(f)[0:36, d * P:d * P + P]) for d in range(2)])
            for j in range(2):
                take(("tu", j), (tails[:, 512 * j:512 * j + 512], acc(("tu", j))[0:18, :]))
            act.wait_ge(ss_taken, H)
            act.activation(ssT[:, :, :], ssT[:, :, :], ACT.Sqrt, bias=eps[:, 0:1], scale=1.0 / DH).then_inc(hroot, 1)
            for m in range(KD):
                take(("o", m), (oT[:, m, :], wide(("o", m))), func=ACT.Sigmoid)
            for m in range(KD):
                take(("ga", m), (s1[:, m, :], wide(("ga", m))), func=ACT.Sigmoid)

            moved(act, ("wo", KD - 1))
            act.wait_ge(stored, 16 * 6)
            act.wait_ge(cp_stored, 16 * H)
            norm(1, sqm)
            norm_root(1)
            for i in range(3):
                for j in range(2):
                    f = ("hn", 2 * i + j)
                    take(f, (hn[:, i, 512 * j:512 * j + 512], acc(f)[:, :]))
            act.wait_ge(rt_arg, 1)
            act.activation(r4[:, :, 2, :], r4[:, :, 2, :], ACT.Exp)
            act.activation(r1[:, :, 7:8], r1[:, :, 7:8], ACT.Exp).then_inc(rt_exp, 1)
            for k in range(KD):
                for j in range(2):
                    f = ("xs", 2 * k + j)
                    take(f, (xs[:, k, j * T:j * T + T], wide(f)))
            for s in range(ST):
                f = ("wc", s)
                take(f, (wcT[:, s, :], wide(f)))

            def expert(off, s, full, n, free, sig, y_done, done):
                act.wait_ge(full, n)
                if free is not None:
                    act.wait_ge(*free)
                act.activation(sg[:, s, :, :].rearrange("p a b -> p (a b)"), bank[s][:, 0:2 * CAP], ACT.Sigmoid).then_inc(sig, 1)
                act.wait_ge(y_done, n)
                act.activation(ys[:, :, bass.ds(off, CAP)], bank[3 + s][:, :].rearrange("p (k c) -> p k c", k=KD), ACT.Copy).then_inc(done, 1)

            act.wait_ge(offs_ready, 1)
            for e in range(FIRST):
                off = act.value_load(offi[0:1, e:e + 1], min_val=0, max_val=PAIRS)
                expert(off, slot(e), gu_full, e + 1, (eh_ready, e + 1 - RING) if e >= RING else None, esig_ready, y_full, ys_ready)
            with act.Fori(0, (E - FIRST) // RING) as i:
                for j in range(RING):
                    off = act.value_load(offi[0:1, bass.ds(3 * i + (FIRST + j), 1)], min_val=0, max_val=PAIRS)
                    expert(off, slot(FIRST + j), gu_full, 3 * i + (FIRST + j + 1), (eh_ready, 3 * i + (FIRST + j + 1 - RING)),
                           esig_ready, y_full, ys_ready)
            extra = act.value_load(wli[0:1, 2 * MAXB:2 * MAXB + 1], min_val=0, max_val=MAXB)
            act.wait_ge(ys_ready, E)
            act.sem_inc(xb_done, 1)
            with act.If(extra > 0):
                with act.Fori(0, extra) as i:
                    off = act.value_load(wli[0:1, bass.ds(i + MAXB, 1)], min_val=0, max_val=PAIRS)
                    expert(off, 0, xb_gu, i + 1, None, xb_sig, xb_y, xb_done)
            act.sem_inc(experts_done, 1)

            for n in range(2 * ST):
                s, j = divmod(n, 2)
                take(("yn", n), (ynat[:, s, 512 * j:512 * j + 512], acc(("yn", n))[:, :]))
            for k in range(KD):
                take(("pp", k), (ppr[:, k, :], wide(("pp", k))))
            moved(act, ("mo", KD - 1))
            norm(2, sqm)
            norm_root(2)
            for m in range(KD):
                take(("pg", m), (sqm[:, m, :], wide(("pg", m))), func=ACT.Sigmoid)
            act.wait_ge(x4_ready, 1)
            norm(3, sqm)
            norm_root(3)
            for i, (t0, n) in enumerate(TILES):
                for j in range(2):
                    f = ("yo", 2 * i + j)
                    take(f, (x4n[0:n, i, 512 * j:512 * j + 512], acc(f)[0:n, :]))

        @block.gpsimd
        def _(pool):
            def select(out, pattern, cm, base_, fill, op=ALU.is_ge):
                return pool.affine_select(out=out, in_=out, pattern=pattern, compare_op=op, fill=fill, base=base_, channel_multiplier=cm)

            own = [0]
            go = step(pool, pool_step, own)
            go(pool.memset(ident[:, :], 0.0))
            select(ident[:, :], [[-1, P]], 1, 0, 1.0, ALU.not_equal).then_inc(consts, 1)
            pool.memset(eps[:, :], EPS)
            pool.memset(ones[:, :], 1.0).then_inc(consts, 1)
            go(pool.memset(selh[:, :, :], 0.0))
            select(selh[:, :, :], [[-1, H], [0, P]], 1, 0, 1.0, ALU.not_equal).then_inc(consts, 1)
            go(pool.memset(mask[:, :], 0.0))
            go(select(mask[:, 0:256], [[1, 256]], -1, 0, NEG))
            go(select(mask[:, 256:384], [[1, P]], -1, 0, NEG))
            ms = mask[0:NS, 384:448].rearrange("p (b j) -> p b j", b=NB)
            go(select(ms, [[-TS, NB], [0, TS]], 1, 0, NEG))
            select(ms, [[TS, NB], [1, TS]], -1, 0, NEG).then_inc(consts, 1)
            go(pool.memset(oneb[:, :], 1.0))
            go(select(oneb[:, :], [[-TS, NB]], 1, 0, 0.0))
            select(oneb[:, :], [[TS, NB]], -1, TS - 1, 0.0).then_inc(consts, 1)

            def load_wqk(h):
                if h:
                    pool.wait_ge(acc_full, index[("kn", h - 1, 2)] + 1)
                for r, w in enumerate((I["w_q"], I["w_k"])):
                    pool.dma_start(wqk[:, r, :, :], w[0, h].rearrange("(d p) e -> p d e", p=P)).then_inc(wqk_landed, 16)

            def load_c(h):
                pool.dma_start(cbuf_rows, I["state_mlstm_C"][0, :, h].rearrange("b (p d) e -> p b (d e)", p=P)).then_inc(c_landed, 16)

            load_wqk(0)
            pool.wait_ge(acc_full, index[("x", KD - 1)] + 1)
            load_c(0)
            pool.wait_ge(m_ready, 1)
            pool.dma_start(O[9][0].rearrange("b h -> h b"), mo[:, 0:NB]).then_inc(stored, 16)
            pool.dma_start(O[4][0].rearrange("a h -> h a"), mo[:, NB:NB + 1]).then_inc(stored, 16)
            load_wqk(1)
            moved(pool, ("to", 1))
            pool.dma_start(O[5][0, 0], tailn[0:3, :]).then_inc(tailn_stored, 16)
            pool.dma_start(O[10][0].rearrange("b j d -> (b j) d"), tailn[3:27, :]).then_inc(tailn_stored, 16)
            pool.wait_ge(aw_ready, 1)
            for h in range(H):
                p = h % 2
                moved(pool, ("kn", h, 2))
                if h:
                    pool.wait_ge(acc_full, index[("n", h - 1)] + 1)
                pool.tensor_tensor(wkm[:, :, :], kn[0:NS, p, 2:3, :].to_broadcast([NS, NB, DH]),
                                   wsel[:, h, :].unsqueeze(2).to_broadcast([NS, NB, DH]), ALU.mult)
                for i in range(2):
                    last = pool.tensor_scalar(wkp[:, i, :], kn[:, p, i, :], awT[:, 1, i, h:h + 1], None, ALU.mult)
                last.then_inc(wk_ready, 1)
                if h + 2 < H:
                    load_wqk(h + 2)
                pool.wait_ge(c_updated, h + 1)
                pool.dma_start(O[7][0, :, h].rearrange("b (p d) e -> p b (d e)", p=P), cbuf_rows).then_inc(c_stored, 16)
                moved(pool, ("Cp", h))
                pool.dma_start(O[2][0, 0, h].rearrange("(p d) e -> p d e", p=P), cpn[:, :, :]).then_inc(cp_stored, 16)
                if h + 1 < H:
                    pool.wait_ge(c_stored, 16 * (h + 1))
                    load_c(h + 1)
            moved(pool, ("tn", 0))
            pool.dma_start(O[8][0].rearrange("b h d -> (b h) d"), nno[0:32, :]).then_inc(stored, 16)
            pool.dma_start(O[3][0, 0], nno[32:36, :]).then_inc(stored, 16)
            moved(pool, ("tu", 1))
            pool.dma_start(O[6][0, 0], tails[0:2, :]).then_inc(stored, 16)
            pool.dma_start(O[11][0].rearrange("b j d -> (b j) d"), tails[2:18, :]).then_inc(stored, 16)
            pool.wait_ge(tailn_stored, 32)
            moved(pool, ("wo", KD - 1))
            pool.wait_ge(stored, 16 * 6)
            pool.wait_ge(cp_stored, 16 * H)
            pool.memset(valid[:, :], 1.0)
            go(pool.memset(tri[:, :], 1.0))
            go(select(tri[:, :], [[1, P]], -1, -1, 0.0))
            go(select(valid[:, :], [[-P, 3]], -1, T - 1, 0.0))
            f = dict(allow_small_or_imprecise_dtypes=True)
            pool.iota(io4[:, :], [[1, G]], base=0, channel_multiplier=0, **f)
            pool.iota(io8[:, :], [[1, EG]], base=0, channel_multiplier=0, **f)
            pool.iota(ios[:, :], [[1, PAIRS]], base=0, channel_multiplier=0, **f)
            pool.iota(ioe[:, :, :], [[0, JX], [1, E]], base=0, channel_multiplier=0, **f)
            pool.iota(ioj[:, :, :], [[CAP, JX], [0, E]], base=CAP, channel_multiplier=0, **f).then_inc(consts2, 1)

        @block.vector
        def _(dve):
            own = [0]
            go = step(dve, dve_step, own)
            empty = acc_empty["dve"]

            def wide(f):
                return acc(f)[:, 0:T]

            def norm_scale(n, g):
                moved(dve, ("ss", n))
                if n == 0:
                    dve.wait_ge(cols_ready, 1)
                go(dve.reciprocal(rstd[:, :], root[:, :]))
                for k in range(KD):
                    last = dve.scalar_tensor_tensor(hT[:, k, 0:T], xT[:, k, :], cols[:, k, g:g + 1], rstd[:, :], ALU.mult, ALU.mult)
                last.then_inc(h_ready, 1)

            seq = lambda a: a.rearrange("p (b j) -> p b j", b=NB)
            dve.memset(hT[:, :, T:3 * P], 0.0)
            dve.memset(xme[:, :, 0:3], 0.0)
            dve.memset(rows[:, 3, :], 1.0)
            go(dve.memset(rows[:, 4, :], 0.0))
            dve.memset(rows[:, 3, 0:1], 0.0)
            dve.memset(rows[:, 3, TP:T:TS], 0.0)
            dve.memset(rows[:, 4, 0:1], NEG)
            go(dve.memset(rows[:, 4, TP:T:TS], NEG))
            filled(dve, ("rows",))
            dve.tensor_copy(cols[:, :, :].rearrange("p k r -> p (k r)"), acc(("rows",))[:, 0:KD * R_ALL]).then_inc(empty, 1)
            moved(dve, ("rows",))
            for k in range(KD):
                last = dve.tensor_copy(seq(xme[:, k, PX:XE])[:, :, 0:3], seq(cols[:, k, R_MCH:R_SCH]))
            last.then_inc(hist_ready, 1)
            filled(dve, ("nn",))
            dve.tensor_copy(nT[:, :, :].rearrange("p c n -> p (c n)"), acc(("nn",))[:, 0:64]).then_inc(empty, 1)
            dve.sem_inc(cols_ready, 1)
            norm_scale(0, R_MIX)

            moved(dve, ("xm", KD - 1))
            for j in range(4):
                for k in range(KD):
                    x, w = xme[:, k, j:j + XE - 3], cols[:, k, R_MCW + j:R_MCW + j + 1]
                    last = dve.tensor_scalar(cv[:, k, :], x, w, None, ALU.mult) if j == 0 else \
                        dve.scalar_tensor_tensor(cv[:, k, :], x, w, cv[:, k, :], ALU.mult, ALU.add)
                last.then_inc(conv_done if j == 3 else dve_step, 1)
                if j < 3:
                    own[0] += 1
                    dve.wait_ge(dve_step, own[0])
            dve.tensor_copy(tailc[:, :, 0:3], xme[:, :, PX - 3:PX])
            for k in range(KD):
                last = dve.tensor_copy(seq(tailc[:, k, 3:27]), seq(xme[:, k, PX:XE])[:, :, SXX - 3:SXX])
            last.then_inc(tails_ready, 1)

            R = lambda i, a=0, b=T: rows[:, i, a:b]
            bc = lambda a: a.unsqueeze(2).to_broadcast([H, NB, TS])
            last_of = lambda i: rows[:, i, TP + TS - 1:T:TS]
            dve.wait_ge(in_small, 16 * 8)
            filled(dve, ("if", 0))
            dve.tensor_scalar(R(0), acc(("if", 0))[0:H, 0:T], bif[:, 0:1], None, ALU.add).then_inc(empty, 1)
            filled(dve, ("if", 1))
            dve.tensor_scalar(R(1), acc(("if", 1))[0:H, 0:T], bif[:, 1:2], None, ALU.add).then_inc(empty, 1)
            moved(dve, ("if", 1))
            dve.scalar_tensor_tensor(R(2), R(1), -1.0, R(1), ALU.mult, ALU.max).then_inc(gate_step, 1)
            dve.wait_ge(gate_step, 1)
            go(dve.tensor_scalar(R(1), R(1), 0.0, None, ALU.min))
            dve.wait_ge(sig_ready, 1)
            dve.tensor_tensor(xq[:, :, 0:TP], xq[:, :, 0:TP], cv[:, :, 0:TP], ALU.mult)
            for k in range(KD):
                last = dve.tensor_tensor(seq(xq[:, k, TP:T]), seq(xq[:, k, TP:T]), cv_sample(k), ALU.mult)
            last.then_inc(xq_ready, 1)
            dve.wait_ge(gate_act, 1)
            go(dve.tensor_tensor(R(1), R(1), R(2), ALU.subtract))
            go(dve.tensor_tensor_scan(R(5), R(3), R(1), 0.0, ALU.mult, ALU.add))
            go(dve.tensor_tensor(R(0), R(0), R(5), ALU.subtract))
            go(dve.tensor_copy(R(1), R(0)))
            dve.tensor_scalar(R(1, 0, 1), R(1, 0, 1), 0.0, None, ALU.max)
            go(dve.tensor_tensor(rows[:, 1, TP:T:TS], rows[:, 1, TP:T:TS], m0r[:, :], ALU.max))
            go(dve.tensor_tensor_scan(R(6), R(4), R(1), 0.0, ALU.add, ALU.max))
            dve.tensor_scalar(R(2), R(6), -1.0, None, ALU.mult)
            dve.tensor_tensor(R(7), R(5), R(6), ALU.add)
            dve.tensor_tensor(seq(R(3, 0, NS)), bc(m0r[:, :]), seq(R(6, TP, T)), ALU.subtract)
            dve.tensor_scalar(R(1, 0, TP), R(0, 0, TP), R(6, TP - 1, TP), None, ALU.subtract)
            go(dve.tensor_tensor(seq(R(1, TP, T)), seq(R(0, TP, T)), bc(last_of(6)), ALU.subtract))
            dve.tensor_copy(mo[:, NB:NB + 1], R(7, TP - 1, TP))
            dve.tensor_copy(mo[:, 0:NB], last_of(7)).then_inc(m_ready, 1)
            dve.wait_ge(m_ready, 1)
            dve.sem_inc(gate_step, 1)
            filled(dve, ("aw", 0))
            for r in range(2):
                for i, (t0, n) in enumerate(TILES):
                    c = (3 * r + i) * H
                    last = dve.tensor_copy(awT[0:n, r, i, :], acc(("aw", 0))[0:n, c:c + H])
            last.then_inc(empty, 1)
            moved(dve, ("aw", 0))
            dve.wait_ge(consts, 5)
            dve.tensor_tensor(wsel[:, :, :], awT[0:NS, 1, 2, :].unsqueeze(2).to_broadcast([NS, H, NB]),
                              oneb[:, :].unsqueeze(1).to_broadcast([NS, H, NB]), ALU.mult).then_inc(aw_ready, 1)

            def probs(h):
                p = h % 2
                dve.wait_ge(scores_full, h + 1)
                dve.tensor_tensor(expo[:, 0:256], b_bc[:, 0:256], mask[:, 0:256], ALU.add)
                dve.tensor_tensor(expo[:, 256:384], b_bc[:, P:256], mask[:, 256:384], ALU.add)
                dve.tensor_tensor(expo[0:NS, 384:448], b_bc[0:NS, TP:T], mask[0:NS, 384:448], ALU.add).then_inc(args_ready, 1)
                dve.tensor_copy(den[:, :], b_enm[:, 0:T])
                go(dve.tensor_copy(wint[:, :], b_bc[:, T:T + NS]))
                qs = qT[:, p, :, TP:T]
                go(dve.tensor_tensor(qw[:, :, :], qs, wint[:, :].unsqueeze(1).to_broadcast([P, 2, NS]), ALU.mult))
                for c in range(2):
                    n0 = nT[:, c, :].rearrange("p (b h) -> p b h", h=H)[:, :, h:h + 1].to_broadcast([P, NB, TS])
                    last = dve.tensor_tensor(seq(qn[:, c, :]), seq(qw[:, c, :]), n0, ALU.mult)
                dve.wait_ge(exps_ready, h + 1)
                dve.tensor_tensor(pt[:, 0:384], expo[:, 0:384], b_s[:, 0:384], ALU.mult)
                dve.tensor_tensor(pt[0:NS, 384:448], expo[0:NS, 384:448], b_s[0:NS, 384:448], ALU.mult).then_inc(probs_ready, 1)

            def outputs(h):
                dve.wait_ge(pv_full, h + 1)
                go(dve.tensor_tensor(den[:, :], b_s[:, 0:T], den[:, :], ALU.max))
                go(dve.scalar_tensor_tensor(den[:, :], b_s[:, 0:T], -1.0, den[:, :], ALU.mult, ALU.max))
                go(dve.reciprocal(den[:, :], den[:, :]))
                for c in range(2):
                    last = dve.tensor_tensor(xq[:, 2 * h + c, :], b_num[c][:, 0:T], den[:, :], ALU.mult)
                last.then_inc(hm_ready, 1)

            def new_states(h):
                dec = wint[:, TS - 1:NS:TS]
                for b in range(NB):
                    f = ("C", h, b)
                    filled(dve, f)
                    c = cbuf[:, b, :, :].rearrange("p d e -> p (d e)")
                    last = dve.scalar_tensor_tensor(c, c, wint[:, b * TS + TS - 1:b * TS + TS], acc(f)[:, :], ALU.mult, ALU.add)
                    last.then_inc(empty, 1)
                moved(dve, ("C", h, NB - 1))
                dve.sem_inc(c_updated, 1)
                f = ("n", h)
                for d in range(2):
                    last = dve.tensor_tensor(nnT[:, d, h:32:H], nT[:, d, h:32:H], dec, ALU.mult)
                go(last)
                filled(dve, f)
                for d in range(2):
                    o = d * (NB + 1)
                    dve.tensor_tensor(nnT[:, d, h:32:H], nnT[:, d, h:32:H], acc(f)[:, o:o + NB], ALU.add)
                    last = dve.tensor_copy(nnT[:, d, 32 + h:33 + h], acc(f)[:, o + NB:o + NB + 1])
                last.then_inc(empty, 1)
                moved(dve, f)
                dve.sem_inc(n_ready, 1)

            sample_u = lambda a, n: a.rearrange("p (b j) -> p b j", b=NB)
            probs(0)
            for h in range(H):
                if MID[h][0] == "sx":
                    moved(dve, ("sc", KD - 1))
                    dve.memset(cxe[:, :, 0:2], 0.0)
                    for k in range(KD):
                        dve.tensor_copy(seq(cxe[:, k, PU:UE])[:, :, 0:2], seq(cols[:, k, R_SCH:R_ALL]))
                    for m in range(KD):
                        f = ("sx", m)
                        filled(dve, f)
                        dve.tensor_tensor(cxe[:, m, 2:PU], acc(f)[:, 0:TP], s1[:, m, 0:TP], ALU.mult)
                        dve.tensor_tensor(seq(cxe[:, m, PU:UE])[:, :, 2:SU], seq(acc(f)[:, TP:T]), seq(s1[:, m, TP:T]), ALU.mult)\
                            .then_inc(empty, 1)
                    moved(dve, ("sx", KD - 1))
                if MID[h][0] == "sb":
                    for m in range(KD):
                        f = ("sb", m)
                        filled(dve, f)
                        dve.tensor_tensor(s1[:, m, 0:TP], acc(f)[:, 0:TP], uT[:, m, 0:TP], ALU.mult)
                        us = seq(uT_sample(m))[:, :, 0:TS]
                        dve.tensor_tensor(seq(s1[:, m, TP:T]), seq(acc(f)[:, TP:T]), us, ALU.mult).then_inc(empty, 1)
                outputs(h)
                new_states(h)
                if h + 1 < H:
                    probs(h + 1)
                if MID[h][0] == "sx":
                    for j in range(3):
                        for k in range(KD):
                            x, w = cxe[:, k, j:j + UE - 2], cols[:, k, R_SCW + j:R_SCW + j + 1]
                            last = dve.tensor_scalar(uT[:, k, :], x, w, None, ALU.mult) if j == 0 else \
                                dve.scalar_tensor_tensor(uT[:, k, :], x, w, uT[:, k, :], ALU.mult, ALU.add)
                        go(last)
                    dve.tensor_copy(tailu[:, :, 0:2], cxe[:, :, PU - 2:PU])
                    for k in range(KD):
                        last = dve.tensor_copy(seq(tailu[:, k, 2:18]), seq(cxe[:, k, PU:UE])[:, :, SU - 2:SU])
                    last.then_inc(tails_ready, 1)

            dve.wait_ge(hroot, 1)
            go(dve.reciprocal(ssT[:, :, :], ssT[:, :, :]))
            for k in range(KD):
                last = dve.scalar_tensor_tensor(xq[:, k, :], xq[:, k, :], cols[:, k, R_HEAD:R_HEAD + 1], ssT[:, k // 2, :], ALU.mult, ALU.mult)
            go(last)
            moved(dve, ("o", KD - 1))
            dve.tensor_tensor(oT[:, :, :], oT[:, :, :], xq[:, :, :], ALU.mult).then_inc(ya_ready, 1)
            moved(dve, ("gb", KD - 1))
            for m in range(KD):
                f = ("sout", m)
                filled(dve, f)
                dve.tensor_tensor(s4[:, m, :], wide(f), s4[:, m, :], ALU.mult).then_inc(empty, 1)
            for m in range(KD):
                f = ("a", m)
                filled(dve, f)
                moved(dve, ("ga", m))
                go(dve.tensor_tensor(s1[:, m, :], wide(f), s1[:, m, :], ALU.mult))
                dve.tensor_tensor(s4[:, m, :], s4[:, m, :], s1[:, m, :], ALU.add).then_inc(empty, 1)
            for m in range(KD):
                f = ("wo", m)
                filled(dve, f)
                dve.tensor_tensor(xT[:, m, :], wide(f), xT[:, m, :], ALU.add).then_inc(empty, 1)
            norm_scale(1, R_FFN)

            B3 = lambda a, n: a.to_broadcast([P, 3, n])
            c1 = lambda i: r1[:, :, i:i + 1]
            dve.wait_ge(consts2, 1)
            dve.wait_ge(stored, 16 * 6)
            filled(dve, ("lg", 0))
            dve.tensor_copy(lg[:, :, :].rearrange("p t n -> p (t n)"), acc(("lg", 0))[:, 0:3 * (G + E)]).then_inc(empty, 1)
            moved(dve, ("lg", 0))

            def first_max(x, mx, idx, one, tmp, io, n):
                go(dve.tensor_reduce(mx, x, AX.X, ALU.max))
                go(dve.tensor_tensor(tmp, x, B3(mx, n), ALU.is_equal))
                go(dve.tensor_scalar(tmp, tmp, -100.0, None, ALU.mult))
                go(dve.tensor_tensor(tmp, tmp, io[:, :].unsqueeze(1).to_broadcast([P, 3, n]), ALU.add))
                go(dve.tensor_reduce(idx, tmp, AX.X, ALU.min))
                go(dve.tensor_tensor(one, tmp, B3(idx, n), ALU.is_equal))

            gl = lg[:, :, 0:G]
            first_max(gl, c1(0), c1(2), r4[:, :, 0, :], r4[:, :, 1, :], io4, G)
            go(dve.tensor_tensor(r4[:, :, 2, :], gl, B3(c1(0), G), ALU.subtract))
            for i in range(3):
                g1 = r4[:, i, 0, :].unsqueeze(2).to_broadcast([P, G, EG])
                last = dve.tensor_tensor(pick[:, 0, i, :].rearrange("p (g e) -> p g e", g=G),
                                         lg[:, i, G:G + E].rearrange("p (g e) -> p g e", g=G), g1, ALU.mult)
            go(last)
            for i in range(3):
                last = dve.tensor_reduce(r8[:, i, 0, :], pick[:, 0, i, :].rearrange("p (g e) -> p e g", g=G), AX.X, ALU.add)
            go(last)
            first_max(r8[:, :, 0, :], c1(3), c1(4), r8[:, :, 1, :], r8[:, :, 4, :], io8, EG)
            go(dve.tensor_scalar(r8[:, :, 2, :], r8[:, :, 1, :], NEG, None, ALU.mult))
            go(dve.tensor_tensor(r8[:, :, 2, :], r8[:, :, 2, :], r8[:, :, 0, :], ALU.add))
            first_max(r8[:, :, 2, :], c1(5), c1(6), r8[:, :, 3, :], r8[:, :, 4, :], io8, EG)
            dve.tensor_tensor(c1(7), c1(5), c1(3), ALU.subtract).then_inc(rt_arg, 1)
            for q, o in ((0, 1), (1, 3)):
                for i in range(3):
                    last = dve.tensor_tensor(pick[:, q, i, :].rearrange("p (g e) -> p g e", g=G),
                                             r4[:, i, 0, :].unsqueeze(2).to_broadcast([P, G, EG]),
                                             r8[:, i, o, :].unsqueeze(1).to_broadcast([P, G, EG]), ALU.mult)
            go(last)
            go(dve.tensor_tensor(m32[:, :, :], pick[:, 0, :, :], pick[:, 1, :, :], ALU.add))
            dve.tensor_tensor(m32[:, :, :], m32[:, :, :], valid[:, :].unsqueeze(2).to_broadcast([P, 3, E]), ALU.mult).then_inc(m32_ready, 1)
            dve.wait_ge(rt_exp, 1)
            dve.tensor_reduce(c1(1), r4[:, :, 2, :], AX.X, ALU.add)
            go(dve.tensor_scalar(c1(8), c1(7), 1.0, None, ALU.add))
            go(dve.tensor_tensor(c1(8), c1(8), c1(1), ALU.mult))
            go(dve.reciprocal(c1(8), c1(8)))
            go(dve.tensor_tensor(c1(9), c1(8), c1(7), ALU.mult))
            filled(dve, ("rank", 0))
            rk = acc(("rank", 0))
            go(dve.tensor_copy(cnt[:, 0, :], rk[:, 3 * E:4 * E]))
            dve.memset(cnt[:, 1, :], 1.0)
            go(dve.memset(pos[:, 0, :], 1.0))
            go(dve.tensor_tensor_scan(cnt[:, 1, :], pos[:, 0, :], cnt[:, 0, :], 0.0, ALU.mult, ALU.add))
            go(dve.tensor_tensor(cnt[:, 2, :], cnt[:, 1, :], cnt[:, 0, :], ALU.subtract))
            dve.tensor_tensor(pos[:, :, :], rk[:, 0:3 * E].rearrange("p (t e) -> p t e", t=3),
                              cnt[:, 2:3, :].to_broadcast([P, 3, E]), ALU.add).then_inc(empty, 1)
            moved(dve, ("rank", 0))
            for q in range(2):
                go(dve.tensor_tensor(pick[:, q, :, :], pick[:, q, :, :], pos[:, :, :], ALU.mult))
                go(dve.tensor_reduce(c1(10 + q), pick[:, q, :, :], AX.X, ALU.add))
                go(dve.tensor_scalar(c1(10 + q), c1(10 + q), 1.0, None, ALU.add))
                go(dve.tensor_tensor(c1(10 + q), c1(10 + q), valid[:, :].unsqueeze(2), ALU.mult))
                go(dve.tensor_scalar(c1(10 + q), c1(10 + q), -1.0, None, ALU.add))
            for i in range(3):
                last = dve.tensor_scalar(gsel[:, i, :], ios[:, :], r1[:, i, 10:11], None, ALU.is_equal)
            go(last)
            for i in range(3):
                last = dve.scalar_tensor_tensor(gsel[:, i, :], ios[:, :], r1[:, i, 11:12], gsel[:, i, :], ALU.is_equal, ALU.add)
            last.then_inc(gsel_ready, 1)
            C_ = lambda i: cnt[0:1, i:i + 1, :].to_broadcast([1, JX, E])
            dve.tensor_copy(offi[:, :], cnt[0:1, 2, :])
            go(dve.tensor_tensor(blk[:, 0], C_(0), ioj[:, :, :], ALU.is_gt))
            fl = blk[:, 0].rearrange("p j e -> p (j e)")
            go(dve.memset(blk[:, 1], 1.0))
            flat = lambda i: blk[:, i].rearrange("p j e -> p (j e)")
            go(dve.tensor_tensor_scan(flat(2), flat(1), flat(0), 0.0, ALU.mult, ALU.add))
            go(dve.tensor_copy(wl[:, 2 * MAXB:2 * MAXB + 1], flat(2)[:, JX * E - 1:JX * E]))
            go(dve.tensor_tensor(blk[:, 2], blk[:, 2], blk[:, 0], ALU.mult))
            go(dve.tensor_tensor(blk[:, 1], C_(2), ioj[:, :, :], ALU.add))
            go(dve.tensor_scalar(blk[:, 3], C_(1), -float(CAP), None, ALU.add))
            go(dve.tensor_tensor(blk[:, 1], blk[:, 1], blk[:, 3], ALU.min))
            for w in range(MAXB):
                go(dve.tensor_scalar(blk[:, 0], blk[:, 2], float(w + 1), None, ALU.is_equal))
                go(dve.tensor_tensor(blk[:, 3], blk[:, 0], ioe[:, :, :], ALU.mult))
                go(dve.tensor_reduce(wl[:, w:w + 1], flat(3), AX.X, ALU.add))
                go(dve.tensor_tensor(blk[:, 3], blk[:, 0], blk[:, 1], ALU.mult))
                go(dve.tensor_reduce(wl[:, MAXB + w:MAXB + w + 1], flat(3), AX.X, ALU.add))
            moved(dve, ("xs", 2 * KD - 1))
            dve.memset(xs[:, :, PAIRS:SLOTS], 0.0)
            dve.tensor_copy(wli[:, :], wl[:, :]).then_inc(offs_ready, 1)
            tmp = ys_tmp
            for i in range(3):
                dve.tensor_scalar(gsel[:, i, :], ios[:, :], r1[:, i, 10:11], r1[:, i, 8:9], ALU.is_equal, ALU.mult)
                last = dve.tensor_scalar(tmp[:, i, :], ios[:, :], r1[:, i, 11:12], r1[:, i, 9:10], ALU.is_equal, ALU.mult)
            own[0] += 1
            last.then_inc(dve_step, 1)
            dve.wait_ge(dve_step, own[0])
            dve.tensor_tensor(gsel[:, :, :], gsel[:, :, :], tmp[:, :, :], ALU.add).then_inc(gw_ready, 1)

            def expert(s, sig, n, free, product):
                a = sg[:, s, :, :].rearrange("p a b -> p (a b)")
                dve.wait_ge(sig, n)
                dve.tensor_tensor(a, a, bank[s][:, 0:2 * CAP], ALU.mult).then_inc(product, 1)
                if free is not None:
                    dve.wait_ge(*free)

            def expert_h(s, n, h_done):
                a = sg[:, s, :, :].rearrange("p a b -> p (a b)")
                dve.wait_ge(est, n)
                dve.tensor_tensor(eh[:, s, :, :].rearrange("p a b -> p (a b)"), a, bank[s][:, 2 * CAP:4 * CAP], ALU.mult).then_inc(h_done, 1)

            for e in range(FIRST):
                expert(slot(e), esig_ready, e + 1, (y_full, e + 1 - RING) if e >= RING else None, est)
                expert_h(slot(e), e + 1, eh_ready)
            with dve.Fori(0, (E - FIRST) // RING) as i:
                for j in range(RING):
                    expert(slot(FIRST + j), esig_ready, 3 * i + (FIRST + j + 1), (y_full, 3 * i + (FIRST + j + 1 - RING)), est)
                    expert_h(slot(FIRST + j), 3 * i + (FIRST + j + 1), eh_ready)
            extra = dve.value_load(wli[0:1, 2 * MAXB:2 * MAXB + 1], min_val=0, max_val=MAXB)
            dve.wait_ge(ys_ready, E)
            with dve.If(extra > 0):
                with dve.Fori(0, extra) as i:
                    expert(0, xb_sig, i + 1, None, est)
                    expert_h(0, i + (E + 1), xb_h)

            for k in range(KD):
                f = ("mo", k)
                filled(dve, f)
                dve.tensor_tensor(xT[:, k, :], wide(f), xT[:, k, :], ALU.add).then_inc(empty, 1)
            norm_scale(2, R_PLE)
            for k in range(KD):
                moved(dve, ("pg", k))
                go(dve.tensor_tensor(sqm[:, k, :], sqm[:, k, :], ppr[:, k, :], ALU.mult))
                last = dve.tensor_tensor(xT[:, k, :], xT[:, k, :], sqm[:, k, :], ALU.add)
            last.then_inc(x4_ready, 1)
            dve.wait_ge(x4_ready, 1)
            norm_scale(3, R_FIN)


_INS = ['x_prompt', 'x_sample', 'p_prompt', 'p_sample', 'state_mlstm_C', 'state_mlstm_n', 'state_mlstm_m',
        'state_mlstm_conv', 'state_sconv', 'g_mix', 'w_in', 'w_mconv', 'w_q', 'w_k', 'b_i', 'b_f', 'g_head', 'w_a',
        'w_sconv', 'w_sout', 'w_o', 'g_ffn', 'w_rg', 'b_rg', 'w_re', 'b_re', 'w_gate', 'w_up', 'w_down',
        'g_ple', 'w_ple_gate', 'w_ple_proj', 'g_final']
_OUTS = [(1, TP, D), (NB, TS, D), (1, 1, H, DH, DH), (1, 1, H, DH), (1, 1, H), (1, 1, 3, D), (1, 1, 2, D),
         (1, NB, H, DH, DH), (1, NB, H, DH), (1, NB, H), (1, NB, 3, D), (1, NB, 2, D)]


def kernel(**inputs):
    import concourse.bacc as _bacc
    from concourse.bass_utils import run_bass_kernel_spmd as _run

    nc = _bacc.Bacc("TRN2", target_bir_lowering=False, num_devices=1)
    arrays, ins = {}, {}
    for name in _INS:
        a = np.ascontiguousarray(inputs[name])
        arrays[f"in_{name}_dram"] = a
        ins[name] = nc.dram_tensor(f"in_{name}_dram", a.shape, F32, kind="ExternalInput").ap()
    outs = [nc.dram_tensor(f"out_{i}_dram", shape, F32, kind="ExternalOutput").ap() for i, shape in enumerate(_OUTS)]
    hybrid_step(nc, ins, outs)
    r = _run(nc, [arrays], core_ids=[0])
    return tuple(r.results[0][f"out_{i}_dram"] for i in range(len(_OUTS)))
```

```python
from contextlib import ExitStack

import numpy as np
import concourse.bass as bass
from concourse import mybir

F32 = mybir.dt.float32
I32 = mybir.dt.int32
ALU = mybir.AluOpType
ACT = mybir.ActivationFunctionType
AX = mybir.AxisListType

P = 128
D = 1024
KD = D // P
TP, NB, TS = 256, 8, 8
NS = NB * TS
T = TP + NS
TILES = [(0, 128), (128, 128), (256, 64)]
H, DH = 4, 256
E, G, EG = 32, 4, 8
FE = 256
PLE = 256
EPS = 1e-6
NEG = -1e30
CAP = 64
WIDE = 96
PAIRS = 2 * T
SLOTS = PAIRS + CAP
ST = PAIRS // P
JX = -(-T // CAP) - 1
MAXB = PAIRS // (CAP + 1)
RING = 3
FIRST = RING + E % RING
WR = 2
ACC = 3
XM, VV, OO, IF, SB, SC, SX, GA, GB = 0, 1024, 2048, 3072, 3080, 4104, 5128, 6152, 7176
R_MIX, R_HEAD, R_FFN, R_PLE, R_FIN, R_MCW, R_SCW, R_MCH, R_SCH, R_ALL = 0, 1, 2, 3, 4, 5, 9, 12, 36, 52
PX, SXX = TP + 3, TS + 3
PU, SU = TP + 2, TS + 2
XE, UE = PX + NB * SXX, PU + NB * SU


def slot(e):
    return e % RING


def hybrid_step(nc, I, O):
    with ExitStack() as ctx:
        plan = {}
        base = [nc.sbuf_base + (-nc.sbuf_base) % 64]

        def at(name, shape, offset, dt=F32):
            plan[name] = (offset, offset + 4 * int(np.prod(shape[1:])))
            return nc.alloc_sbuf_tensor_at(name, shape, dt, offset=offset)

        def new(name, shape, dt=F32):
            t = at(name, shape, base[0], dt)
            base[0] = plan[name][1] + (-plan[name][1]) % 64
            return t

        def sem(name):
            return ctx.enter_context(nc.semaphore(name))

        ident = new("ident", [P, P])
        ones = new("ones", [P, P])
        cols = new("cols", [P, KD, R_ALL])
        eps = new("eps", [P, 1])
        xT = new("xT", [P, KD, T])
        hT = new("hT", [P, KD, 3 * P])
        pT = new("pT", [P, 2, T])
        root = new("root", [P, T])
        rstd = new("rstd", [P, T])
        wring = new("wring", [P, WR, KD, 512])
        wr36 = new("wr36", [P, KD, G + E])
        wif = new("wif", [P, KD, 2 * H])
        brow = new("brow", [1, G + E])
        phase = base[0]

        vn = new("vn", [P, 3, D])
        kn = new("kn", [P, 2, 3, DH])
        qT = new("qT", [P, 2, 2, T])
        kT = new("kT", [P, 2, 2, T])
        s1 = new("s1", [P, KD, T])
        xme = new("xme", [P, KD, XE])
        cxe = at("cxe", [P, KD, UE], plan["xme"][0])
        cv_all = new("cv", [P, KD, XE])
        u_all = at("uT", [P, KD, UE], plan["cv"][0])
        cv, uT = cv_all[:, :, 0:XE - 3], u_all[:, :, 0:UE - 2]
        xq = new("xq", [P, KD, T])
        s4 = at("s4", [P, KD, T], plan["xme"][0])
        cbuf = new("cbuf", [P, NB, 2, DH])
        oT = at("oT", [P, KD, T], plan["cbuf"][0])
        xnat = at("xnat", [P, 3, D], plan["cbuf"][0])
        sqx = at("sqx", [P, KD, T], plan["s1"][0])
        rowsn = at("rowsn", [R_ALL, D], plan["kn"][0])
        pnat = at("pnat", [P, 3, PLE], plan["kn"][0] + 4096)
        nnat = at("nnat", [NB * H, DH], plan["kn"][0] + 8192)
        wqk = new("wqk", [P, 2, 2, DH])
        rows = new("rows", [H, 8, T])
        m0r = new("m0r", [H, NB])
        mo = new("mo", [H, NB + 1])
        bif = new("bif", [H, 2])
        selh = new("selh", [H, H, P])
        mask = new("mask", [P, 448])
        expo = new("expo", [P, 448])
        pt = new("pt", [P, 384 + WIDE])
        awT = new("awT", [P, 2, 3, H])
        oneb = new("oneb", [NS, NB])
        wsel = new("wsel", [NS, H, NB])
        wint = new("wint", [P, NS])
        qw = new("qw", [P, 2, NS])
        qz = new("qz", [P, 2, NB, WIDE])
        onet = new("onet", [P, NB, NS])
        qn = new("qn", [P, 2, NS])
        wkm = new("wkm", [NS, NB, DH])
        wkp = new("wkp", [P, 2, DH])
        cpn = new("cpn", [P, 2, DH])
        nT = new("nT", [P, 2, NB * H])
        nall = new("nall", [33, H, DH])
        nrow, npr = nall[0:NB], nall[32:33]
        decT = new("decT", [NB, H])
        den = new("den", [P, T])
        ssT = new("ssT", [P, H, T])
        tailc = new("tailc", [P, KD, 27])
        tailu = new("tailu", [P, KD, 18])
        hsq = new("hsq", [P, 2, T])
        mixer_end = base[0]
        assert mixer_end <= nc.sbuf_usable_end, mixer_end
        tailn = at("tailn", [27, D], plan["s1"][0])
        tails = at("tails", [18, D], plan["cbuf"][0] + 4 * KD * T)

        base[0] = phase
        egu = [None] * RING
        ed = [None] * RING
        for s in range(RING):
            egu[s] = new(f"egu{s}", [P, KD, 2, FE])
            ed[s] = new(f"ed{s}", [P, 2, D])
        xs = new("xs", [P, KD, SLOTS])
        ys = new("ys", [P, KD, SLOTS])
        assert plan["ys"][1] - plan["ys"][0] >= 12288 + 4 * 3 * PAIRS
        hn = at("hn", [P, 3, D], plan["ys"][0])
        ynat = at("ynat", [P, ST, D], plan["egu0"][0])
        x4n = at("x4n", [P, 3, D], plan["xs"][0])
        sqm = at("sqm", [P, KD, T], plan["xs"][0])
        gsel = new("gsel", [P, 3, PAIRS])
        base[0] += 512
        wcT = new("wcT", [P, ST, T])
        ppr = at("ppr", [P, KD, T], plan["ys"][0])
        wpp = at("wpp", [P, 2, D], plan["gsel"][0])
        xb = new("xb", [P, RING, KD, CAP])
        sg = new("sg", [P, RING, P])
        eh = new("eh", [P, RING, P])
        yb = new("yb", [P, 512])
        offi = new("offi", [1, E], I32)
        wli = new("wli", [1, 2 * MAXB + 1], I32)
        expert_end = base[0]
        base[0] = plan["xb"][0]
        lg = new("lg", [P, 3, G + E])
        r4 = new("r4", [P, 3, 4, G])
        r8 = new("r8", [P, 3, 8, EG])
        r1 = new("r1", [P, 3, 12])
        pick = new("pick", [P, 2, 3, E])
        m32 = new("m32", [P, 3, E])
        pos = new("pos", [P, 3, E])
        tri = new("tri", [P, P])
        io4 = new("io4", [P, G])
        io8 = new("io8", [P, EG])
        valid = new("valid", [P, 3])
        cnt = new("cnt", [P, 3, E])
        blk = new("blk", [1, 4, JX, E])
        ioe = new("ioe", [1, JX, E])
        ioj = new("ioj", [1, JX, E])
        wl = new("wl", [1, 2 * MAXB + 1])
        assert base[0] <= expert_end, (base[0], expert_end)
        base[0] = expert_end
        ys_tmp = at("ys_tmp", [P, 3, PAIRS], plan["ys"][0] + 12288)
        ios = at("ios", [P, PAIRS], plan["wcT"][0])
        assert base[0] <= nc.sbuf_usable_end, base[0]

        bank = [ctx.enter_context(nc.psum_tensor(f"bank{i}", [P, 512], F32)) for i in range(8)]
        b_ht, b_y, b_yt = bank[3], bank[4], bank[5]
        b_enm, b_s, b_bc, b_num = bank[3], bank[4], bank[5], (bank[6], bank[7])

        fills = [("x", k) for k in range(KD)] + [("rows",), ("nn",), ("pn", 0), ("pn", 1), ("ss", 0)]
        who = {("rows",): "dve", ("nn",): "dve"}

        def section(name, by, n=KD):
            for m in range(n):
                fills.append((name, m))
                who[(name, m)] = by

        section("xm", "act")
        section("if", "dve", 2)
        section("v", "act", 6)
        section("aw", "dve", 1)

        def qk_fills(h):
            fills.extend([("qk", h, n) for n in range(4)] + [("kn", h, n) for n in range(3)])

        def state_fills(h):
            for f in [("C", h, b) for b in range(NB)] + [("Cp", h), ("n", h)]:
                fills.append(f)
                who[f] = "act" if f[0] == "Cp" else "dve"

        MID = [("sc", "act"), ("sx", "dve"), ("sb", "dve"), ("gb", "act")]
        qk_fills(0)
        section("to", "act", 2)
        qk_fills(1)
        for h in range(H):
            section(*MID[h])
            state_fills(h)
            if h + 2 < H:
                qk_fills(h + 2)
        section("tu", "act", 2)
        section("o", "act")
        section("sout", "dve")
        section("ga", "act")
        section("a", "dve")
        section("wo", "dve")
        fills.append(("ss", 1))
        section("lg", "dve", 1)
        section("hn", "act", 6)
        section("rank", "dve", 1)
        section("xs", "act", 2 * KD)
        section("wc", "act", ST)
        section("yn", "act", 2 * ST)
        section("mo", "dve")
        section("pp", "act")
        fills.append(("ss", 2))
        section("pg", "act")
        fills.append(("ss", 3))
        section("yo", "act", 6)
        index = {f: n for n, f in enumerate(fills)}
        emptied = {}
        done = {"act": 0, "dve": 0}
        for f in fills:
            w = who.setdefault(f, "act")
            done[w] += 1
            emptied[f] = (w, done[w])

        acc_full = sem("acc_full")
        acc_empty = {"act": sem("acc_empty_act"), "dve": sem("acc_empty_dve")}

        def acc(f):
            return bank[index[f] % ACC]

        def refill(pe, f):
            if index[f] >= ACC:
                w, n = emptied[fills[index[f] - ACC]]
                pe.wait_ge(acc_empty[w], n)

        def moved(eng, f):
            w, n = emptied[f]
            eng.wait_ge(acc_empty[w], n)

        def filled(eng, f):
            eng.wait_ge(acc_full, index[f] + 1)

        order = ["xm", "v", "sc", "sx", "sb", "gb", "o", "sout", "ga", "a", "wo", "pg"]
        w_in = I["w_in"][0]
        source = {"xm": w_in[:, XM:XM + D], "v": w_in[:, VV:VV + D], "o": w_in[:, OO:OO + D],
                  "sb": w_in[:, SB:SB + D], "sc": w_in[:, SC:SC + D], "sx": w_in[:, SX:SX + D],
                  "ga": w_in[:, GA:GA + D], "gb": w_in[:, GB:GB + D], "a": I["w_a"][0],
                  "sout": I["w_sout"][0], "wo": I["w_o"][0], "pg": I["w_ple_gate"][0]}
        halves = [(s, j) for s in order for j in range(2)]
        w_landed = [sem(f"w_landed{i}") for i in range(WR)]

        def weights(eng, s, j):
            n = halves.index((s, j))
            eng.wait_ge(w_landed[n % WR], 16 * (n // WR + 1))
            return wring[:, n % WR]

        in_x = sem("in_x"); in_rows = sem("in_rows"); in_small = sem("in_small"); in_m0 = sem("in_m0")
        consts = sem("consts"); pool_step = sem("pool_step"); dve_step = sem("dve_step"); act_step = sem("act_step")
        x_ready = sem("x_ready"); cols_ready = sem("cols_ready"); sq_ready = sem("sq_ready")
        root_ready = sem("root_ready"); h_ready = sem("h_ready")
        xm_ready = sem("xm_ready"); conv_done = sem("conv_done"); sig_ready = sem("sig_ready"); xq_ready = sem("xq_ready")
        gate_step = sem("gate_step"); gate_act = sem("gate_act"); rows_ready = sem("rows_ready"); aw_ready = sem("aw_ready")
        wqk_landed = sem("wqk_landed"); wqk_used = sem("wqk_used"); qk_ready = sem("qk_ready")
        scores_full = sem("scores_full"); args_ready = sem("args_ready"); exps_ready = sem("exps_ready")
        probs_ready = sem("probs_ready"); c_landed = sem("c_landed"); c_updated = sem("c_updated"); c_stored = sem("c_stored")
        pv_full = sem("pv_full"); enm_used = sem("enm_used"); hm_ready = sem("hm_ready"); hsq_ready = sem("hsq_ready")
        ss_full = sem("ss_full"); ss_taken = sem("ss_taken"); wk_ready = sem("wk_ready"); states_full = sem("states_full")
        cp_ready = sem("cp_ready"); cp_stored = sem("cp_stored"); n_ready = sem("n_ready"); tails_ready = sem("tails_ready")
        rows_out = sem("rows_out"); stored = sem("stored"); u_ready = sem("u_ready"); su_ready = sem("su_ready")
        o_ready = sem("o_ready"); ga_ready = sem("ga_ready"); ya_ready = sem("ya_ready"); merged = sem("merged")
        hroot = sem("hroot"); x2_ready = sem("x2_ready"); m_ready = sem("m_ready"); gb_ready = sem("gb_ready")
        lg_ready = sem("lg_ready"); rt_exp = sem("rt_exp"); rt_arg = sem("rt_arg"); m32_ready = sem("m32_ready")
        gsel_ready = sem("gsel_ready"); gw_ready = sem("gw_ready"); hn_ready = sem("hn_ready"); xs_ready = sem("xs_ready")
        offs_ready = sem("offs_ready"); wc_ready = sem("wc_ready")
        gu_landed = [sem(f"gu_landed{s}") for s in range(RING)]
        d_landed = [sem(f"d_landed{s}") for s in range(RING)]
        xb_ready = sem("xb_ready"); ht_full = sem("ht_full"); ht_ready = sem("ht_ready"); yb_ready = sem("yb_ready"); yt_full = sem("yt_full")
        xb_xb = sem("xb_xb"); xb_htf = sem("xb_htf"); xb_ht = sem("xb_ht"); xb_yb = sem("xb_yb"); xb_yt = sem("xb_yt")
        gu_full = sem("gu_full"); esig_ready = sem("esig_ready"); eh_ready = sem("eh_ready")
        y_full = sem("y_full"); ys_ready = sem("ys_ready"); est = sem("est")
        xb_landed = sem("xb_landed"); xb_gu = sem("xb_gu"); xb_sig = sem("xb_sig"); xb_h = sem("xb_h"); xb_st = sem("xb_st")
        xb_y = sem("xb_y"); xb_done = sem("xb_done")
        late_full = sem("late_full"); late_act = sem("late_act"); late_dve = sem("late_dve"); wpp_landed = sem("wpp_landed")
        consts2 = sem("consts2"); out_stored = sem("out_stored"); experts_done = sem("experts_done"); mo_ready = sem("mo_ready")

        hist_ready = sem("hist_ready"); tailn_stored = sem("tailn_stored"); x4_ready = sem("x4_ready")
        cbuf_rows = cbuf[:, :, :, :].rearrange("p b d e -> p b (d e)")
        cv_sample = lambda k: cv_all[:, k, PX:PX + NB * SXX].rearrange("p (b j) -> p b j", b=NB)[:, :, 0:TS]
        uT_sample = lambda k: u_all[:, k, PU:PU + NB * SU]

        def step(eng, signal, count):
            def go(ins):
                count[0] += 1
                ins.then_inc(signal, 1)
                eng.wait_ge(signal, count[0])
            return go

        ctx.enter_context(nc.allow_non_contiguous_dma(reason="gate biases and m: 4 to 32 elements"))
        block = ctx.enter_context(nc.Block())

        @block.sync
        def _(sp):
            for i, (t0, n) in enumerate(TILES):
                src = I["x_prompt"][0, t0:t0 + n] if i < 2 else I["x_sample"].rearrange("b t d -> (b t) d")
                sp.dma_start(xnat[0:n, i, :], src).then_inc(in_x, 16)
            one = lambda a: a.rearrange("(a d) -> a d", a=1)
            for r, src in ((R_MIX, I["g_mix"]), (R_HEAD, I["g_head"].rearrange("a h d -> a (h d)")), (R_FFN, I["g_ffn"]),
                           (R_PLE, I["g_ple"]), (R_FIN, one(I["g_final"])), (R_MCW, I["w_mconv"][0]), (R_SCW, I["w_sconv"][0]),
                           (R_MCH, I["state_mlstm_conv"][0].rearrange("b j d -> (b j) d")),
                           (R_SCH, I["state_sconv"][0].rearrange("b j d -> (b j) d"))):
                sp.dma_start(rowsn[r:r + src.shape[0], :], src).then_inc(in_rows, 16)
            for i, (t0, n) in enumerate(TILES):
                src = I["p_prompt"][0, 0, t0:t0 + n] if i < 2 else I["p_sample"][0].rearrange("b t d -> (b t) d")
                sp.dma_start(pnat[0:n, i, :], src).then_inc(in_rows, 16)
            sp.dma_start(nrow[:, :, :], I["state_mlstm_n"][0]).then_inc(in_small, 16)
            sp.dma_start(nnat[:, :], I["state_mlstm_n"][0].rearrange("b h d -> (b h) d")).then_inc(in_rows, 16)

            def half(n):
                s, j = halves[n]
                if n >= WR:
                    before, i = halves[n - WR]
                    sp.wait_ge(acc_full, index[(before, 3 * i + 2 if before == "v" else 4 * i + 3)] + 1)
                sp.dma_start(wring[:, n % WR], source[s][:, 512 * j:512 * j + 512].rearrange("(k p) c -> p k c", p=P))\
                    .then_inc(w_landed[n % WR], 16)

            half(0)
            half(1)
            sp.dma_start(wif[:, :, :], w_in[:, IF:IF + 2 * H].rearrange("(k p) c -> p k c", p=P)).then_inc(in_small, 16)
            sp.dma_start(bif[:, 0:1], I["b_i"].rearrange("a h -> h a")).then_inc(in_small, 16)
            sp.dma_start(bif[:, 1:2], I["b_f"].rearrange("a h -> h a")).then_inc(in_small, 16)
            sp.dma_start(m0r[:, :], I["state_mlstm_m"][0].rearrange("b h -> h b")).then_inc(in_small, 16)
            sp.dma_start(brow[:, 0:G], I["b_rg"]).then_inc(in_small, 16)
            sp.dma_start(brow[:, G:G + E], I["b_re"]).then_inc(in_small, 16)
            sp.dma_start(wr36[:, :, 0:G], I["w_rg"][0].rearrange("(k p) c -> p k c", p=P)).then_inc(in_small, 16)
            sp.dma_start(wr36[:, :, G:G + E], I["w_re"][0].rearrange("(k p) c -> p k c", p=P)).then_inc(in_small, 16)
            for n in range(WR, 2 * order.index("pg")):
                half(n)
            w_g, w_u, w_d = I["w_gate"][0], I["w_up"][0], I["w_down"][0]

            row = lambda w, e: w[e:e + 1] if isinstance(e, int) else w[bass.ds(e, 1)]

            def load_gu(e, s, signal):
                for j, w in enumerate((w_g, w_u)):
                    sp.dma_start(egu[s][:, :, j, :], row(w, e).rearrange("a (k p) c -> p (a k) c", p=P)).then_inc(signal, 16)

            def load_d(e, s, signal):
                sp.dma_start(ed[s][:, :, :], row(w_d, e).rearrange("a (k p) c -> p (a k) c", p=P)).then_inc(signal, 16)

            moved(sp, ("wo", KD - 1))
            sp.wait_ge(stored, 16 * 6)
            sp.wait_ge(tailn_stored, 32)
            sp.wait_ge(c_stored, 16 * H)
            sp.wait_ge(cp_stored, 16 * H)
            for e in range(RING):
                load_gu(e, slot(e), gu_landed[slot(e)])
                load_d(e, slot(e), d_landed[slot(e)])
            with sp.Fori(0, (E - FIRST) // RING) as i:
                for j in range(RING):
                    s = slot(RING + j)
                    sp.wait_ge(gu_full, 3 * i + (j + 1))
                    load_gu(3 * i + (RING + j), s, gu_landed[s])
                    sp.wait_ge(y_full, 3 * i + (j + 1))
                    load_d(3 * i + (RING + j), s, d_landed[s])
            for e in (E - 2, E - 1):
                sp.wait_ge(gu_full, e + 1 - RING)
                load_gu(e, slot(e), gu_landed[slot(e)])
                sp.wait_ge(y_full, e + 1 - RING)
                load_d(e, slot(e), d_landed[slot(e)])
            half(2 * order.index("pg"))
            half(2 * order.index("pg") + 1)
            sp.wait_ge(offs_ready, 1)
            extra = sp.value_load(wli[0:1, 2 * MAXB:2 * MAXB + 1], min_val=0, max_val=MAXB)
            sp.wait_ge(ys_ready, E)
            with sp.If(extra > 0):
                with sp.Fori(0, extra) as i:
                    sp.wait_ge(xb_done, i + 1)
                    e = sp.value_load(wli[0:1, bass.ds(i, 1)], min_val=0, max_val=E - 1)
                    load_gu(e, 0, xb_landed)
                    load_d(e, 0, xb_landed)
            moved(sp, ("wc", ST - 1))
            sp.dma_start(wpp[:, :, :], I["w_ple_proj"][0].rearrange("(k p) c -> p k c", p=P)).then_inc(wpp_landed, 16)

            for i, (t0, n) in enumerate(TILES):
                last = ("yo", 2 * i + 1)
                moved(sp, last)
                dst = O[0][0, t0:t0 + n] if i < 2 else O[1].rearrange("b t d -> (b t) d")
                sp.dma_start(dst, x4n[0:n, i, :]).then_inc(out_stored, 16)
            sp.wait_ge(out_stored, 16 * 3)

        @block.tensor
        def _(pe):
            def fill(f, mms):
                refill(pe, f)
                mms(acc(f)).then_inc(acc_full, 1)

            def linear(name, rhs):
                for m in range(KD):
                    if m % 4 == 0:
                        w = weights(pe, name, m // 4)
                    def mms(bk):
                        for k in range(KD):
                            last = pe.matmul(bk[:, 0:T], w[:, k, (m % 4) * P:(m % 4) * P + P], rhs[:, k, 0:T],
                                             start=(k == 0), stop=(k == KD - 1))
                        return last
                    fill((name, m), mms)

            pe.wait_ge(consts, 1)
            pe.wait_ge(in_x, 16 * 3)
            for k in range(KD):
                def mms(bk):
                    for i, (t0, n) in enumerate(TILES):
                        last = pe.transpose(bk[:, t0:t0 + n], xnat[0:n, i, k * P:k * P + P], ident[0:n, 0:n])
                    return last
                fill(("x", k), mms)
            pe.wait_ge(in_rows, 16 * 13)

            def mms(bk):
                for k in range(KD):
                    last = pe.transpose(bk[:, k * R_ALL:(k + 1) * R_ALL], rowsn[:, k * P:k * P + P], ident[0:R_ALL, 0:R_ALL])
                return last
            fill(("rows",), mms)

            def mms(bk):
                for c in range(2):
                    last = pe.transpose(bk[:, c * 32:c * 32 + 32], nnat[:, c:DH:2], ident[0:32, 0:32])
                return last
            fill(("nn",), mms)
            for c in range(2):
                def mms(bk):
                    for i, (t0, n) in enumerate(TILES):
                        last = pe.transpose(bk[:, t0:t0 + n], pnat[0:n, i, c * P:c * P + P], ident[0:n, 0:n])
                    return last
                fill(("pn", c), mms)

            def sums(f, sq, n=KD):
                def mms(bk):
                    for k in range(n):
                        last = pe.matmul(bk[:, 0:T], ones[:, :], sq[:, k, :], start=(k == 0), stop=(k == n - 1))
                    return last
                fill(f, mms)

            pe.wait_ge(consts, 2)
            pe.wait_ge(sq_ready, 1)
            sums(("ss", 0), sqx)

            pe.wait_ge(h_ready, 1)
            linear("xm", hT)
            pe.wait_ge(in_small, 16 * 9)
            for g in range(2):
                def mms(bk):
                    for k in range(KD):
                        last = pe.matmul(bk[0:H, 0:T], wif[:, k, g * H:g * H + H], hT[:, k, 0:T], start=(k == 0), stop=(k == KD - 1))
                    return last
                fill(("if", g), mms)
            for j in range(2):
                w = weights(pe, "v", j)
                for i, (t0, n) in enumerate(TILES):
                    def mms(bk):
                        for k in range(KD):
                            last = pe.matmul(bk[0:n, :], hT[:, k, t0:t0 + n], w[:, k, :], start=(k == 0), stop=(k == KD - 1))
                        return last
                    fill(("v", 3 * j + i), mms)
            pe.wait_ge(rows_ready, 2)
            def mms(bk):
                for r, row in enumerate((0, 1)):
                    for i, (t0, n) in enumerate(TILES):
                        c = (3 * r + i) * H
                        pe.transpose(bk[0:n, c:c + H], rows[:, row, t0:t0 + n], ident[0:H, 0:H])
                return pe.transpose(bk[0:NB, 6 * H:7 * H], rows[:, 3, TS - 1:NS:TS], ident[0:H, 0:H])
            fill(("aw", 0), mms)

            def qk(h):
                pe.wait_ge(wqk_landed, 32 * (h + 1))
                if h == 0:
                    pe.wait_ge(xq_ready, 1)
                for n in range(4):
                    r, c = divmod(n, 2)
                    def mms(bk):
                        for d in range(2):
                            last = pe.matmul(bk[:, 0:T], wqk[:, r, d, c:DH:2], xq[:, 2 * h + d, :], start=(d == 0), stop=(d == 1))
                        return last
                    fill(("qk", h, n), mms)
                for i, (t0, n) in enumerate(TILES):
                    def mms(bk):
                        for d in range(2):
                            last = pe.matmul(bk[0:n, 0:DH], xq[:, 2 * h + d, t0:t0 + n], wqk[:, 1, d, :], start=(d == 0), stop=(d == 1))
                        return last
                    fill(("kn", h, i), mms)

            def scores(h):
                p = h % 2
                moved(pe, ("qk", h, 3))
                if h == 0:
                    pe.wait_ge(rows_ready, 2)
                    pe.wait_ge(consts, 4)
                else:
                    pe.wait_ge(hm_ready, h)
                for (o, n, s0, sn, t0) in ((0, 256, 0, P, 0), (256, P, P, P, P), (384, NS, TP, NS, TP)):
                    for c in range(2):
                        last = pe.matmul(b_s[0:sn, o:o + n], kT[:, p, c, s0:s0 + sn], qT[:, p, c, t0:t0 + n], start=(c == 0), stop=(c == 1))
                pe.matmul(b_bc[:, 0:T], selh[:, h, :], rows[:, 2, :], start=True, stop=True)
                pe.matmul(b_bc[:, T:T + NS], selh[:, h, :], rows[:, 3, 0:NS], start=True, stop=True)
                if h:
                    pe.wait_ge(ss_taken, h)
                pe.matmul(b_enm[:, 0:T], selh[:, h, :], rows[:, 7, :], start=True, stop=True).then_inc(scores_full, 1)

            def pv(h):
                pe.wait_ge(probs_ready, h + 1)
                for i in range(3):
                    moved(pe, ("v", 3 + i))
                pe.wait_ge(c_landed, 16 * (h + 1))
                for c in range(2):
                    e0 = h * DH + c * P
                    bk = b_num[c]
                    pe.matmul(bk[:, 0:256], vn[:, 0, e0:e0 + P], pt[:, 0:256], start=True, stop=False, skip_group_check=True)
                    pe.matmul(bk[:, P:256], vn[:, 1, e0:e0 + P], pt[:, 256:384], start=False, stop=False, skip_group_check=True)
                    pe.matmul(bk[:, TP:TP + WIDE], vn[0:NS, 2, e0:e0 + P], pt[0:NS, 384:384 + WIDE], start=False, stop=False, skip_group_check=True)
                    for b in range(NB):
                        for d in range(2):
                            pe.matmul(bk[:, TP:TP + WIDE], cbuf[:, b, d, c * P:c * P + P], qz[:, d, b, :],
                                      start=False, stop=(b == NB - 1 and d == 1), skip_group_check=True)
                pe.matmul(b_s[:, 0:256], ones[:, :], pt[:, 0:256], start=True, stop=False, skip_group_check=True)
                pe.matmul(b_s[:, P:256], ones[:, :], pt[:, 256:384], start=False, stop=False, skip_group_check=True)
                pe.matmul(b_s[:, TP:T], ones[0:NS, :], pt[0:NS, 384:448], start=False, stop=False, skip_group_check=True)
                for d in range(2):
                    last = pe.matmul(b_s[:, TP:T], ones[:, :], qn[:, d, :], start=False, stop=(d == 1), skip_group_check=True)
                last.then_inc(pv_full, 1)

            def states(h):
                pe.wait_ge(wk_ready, h + 1)
                for b in range(NB):
                    def mms(bk):
                        for d in range(2):
                            last = pe.matmul(bk[:, d * DH:(d + 1) * DH], wkm[:, b, d:DH:2], vn[0:NS, 2, h * DH:(h + 1) * DH], start=True, stop=True)
                        return last
                    fill(("C", h, b), mms)
                def mms(bk):
                    for d in range(2):
                        for i in range(2):
                            last = pe.matmul(bk[:, d * DH:(d + 1) * DH], wkp[:, i, d:DH:2], vn[:, i, h * DH:(h + 1) * DH], start=(i == 0), stop=(i == 1))
                    return last
                fill(("Cp", h), mms)
                def mms(bk):
                    pe.matmul(bk[0:NB, 0:DH], wsel[:, h, :], kn[0:NS, h % 2, 2, :], start=True, stop=True)
                    for i in range(2):
                        last = pe.matmul(bk[32:33, DH:2 * DH], awT[:, 1, i, h:h + 1], kn[:, h % 2, i, :], start=(i == 0), stop=(i == 1))
                    return last
                fill(("n", h), mms)

            def head_sums(h):
                pe.wait_ge(hsq_ready, h + 1)
                for c in range(2):
                    last = pe.matmul(b_enm[:, 0:T], ones[:, :], hsq[:, c, :], start=(c == 0), stop=(c == 1))
                last.then_inc(ss_full, 1)

            qk(0)
            for j in range(2):
                if j == 0:
                    pe.wait_ge(tails_ready, 1)
                def mms(bk):
                    for k in range(4):
                        last = pe.transpose(bk[0:27, k * P:k * P + P], tailc[:, 4 * j + k, :], ident[:, :])
                    return last
                fill(("to", j), mms)
            scores(0)
            qk(1)
            for h in range(H):
                linear(MID[h][0], hT)
                pv(h)
                states(h)
                head_sums(h)
                if h + 1 < H:
                    scores(h + 1)
                if h + 2 < H:
                    qk(h + 2)
            for j in range(2):
                if j == 0:
                    pe.wait_ge(tails_ready, 2)
                def mms(bk):
                    for k in range(4):
                        last = pe.transpose(bk[0:18, k * P:k * P + P], tailu[:, 4 * j + k, :], ident[:, :])
                    return last
                fill(("tu", j), mms)
            linear("o", hT)
            moved(pe, ("sb", KD - 1))
            linear("sout", s1)
            linear("ga", hT)
            pe.wait_ge(ya_ready, 1)
            linear("a", oT)
            moved(pe, ("a", KD - 1))
            linear("wo", s4)

            pe.wait_ge(sq_ready, 2)
            sums(("ss", 1), sqm)
            pe.wait_ge(h_ready, 2)
            def mms(bk):
                for i in range(3):
                    o = bk[:, i * 36:i * 36 + 36]
                    pe.matmul(o, ones[0:1, :], brow[:, :], start=True, stop=False)
                    for k in range(KD):
                        last = pe.matmul(o, hT[:, k, i * P:i * P + P], wr36[:, k, :], start=False, stop=(k == KD - 1))
                return last
            fill(("lg", 0), mms)
            for i in range(3):
                for j in range(2):
                    def mms(bk):
                        for k in range(4):
                            last = pe.transpose(bk[:, k * P:k * P + P], hT[:, 4 * j + k, i * P:i * P + P], ident[:, :])
                        return last
                    fill(("hn", 2 * i + j), mms)
            pe.wait_ge(m32_ready, 1)
            def mms(bk):
                for i in range(3):
                    for q in range(i):
                        pe.matmul(bk[:, i * E:(i + 1) * E], ones[:, :], m32[:, q, :], start=(q == 0), stop=False)
                    pe.matmul(bk[:, i * E:(i + 1) * E], tri[:, :], m32[:, i, :], start=(i == 0), stop=True)
                for i in range(3):
                    last = pe.matmul(bk[:, 3 * E:4 * E], ones[:, :], m32[:, i, :], start=(i == 0), stop=(i == 2))
                return last
            fill(("rank", 0), mms)
            pe.wait_ge(gsel_ready, 1)
            moved(pe, ("hn", 5))
            for k in range(KD):
                for j in range(2):
                    def mms(bk):
                        for i in range(3):
                            last = pe.matmul(bk[:, 0:T], hn[:, i, k * P:k * P + P], gsel[:, i, j * T:j * T + T], start=(i == 0), stop=(i == 2))
                        return last
                    fill(("xs", 2 * k + j), mms)
            pe.wait_ge(gw_ready, 1)
            for s in range(ST):
                def mms(bk):
                    for i, (t0, n) in enumerate(TILES):
                        last = pe.transpose(bk[:, t0:t0 + n], gsel[0:n, i, s * P:s * P + P], ident[0:n, 0:n])
                    return last
                fill(("wc", s), mms)
            moved(pe, ("wc", ST - 1))
            moved(pe, ("xs", 2 * KD - 1))
            pe.wait_ge(offs_ready, 1)

            def gate_up(s):
                for k in range(KD):
                    for j in range(2):
                        last = pe.matmul(bank[s][j * CAP:(j + 1) * CAP, 0:FE], xb[:, s, k, :], egu[s][:, k, :, j * P:(j + 1) * P],
                                         start=(k == 0), stop=(k == KD - 1))
                return last

            def turn_h(s):
                return pe.transpose(b_ht[:, 0:P], sg[:, s, :], ident[:, :])

            def down(s):
                for j in range(2):
                    for c in range(2):
                        last = pe.matmul(b_y[c * CAP:(c + 1) * CAP, :], eh[:, s, j * CAP:(j + 1) * CAP], ed[s][:, j, c * 512:(c + 1) * 512],
                                         start=(j == 0), stop=(j == 1))
                return last

            def turn_y():
                for q in range(4):
                    last = pe.transpose(b_yt[:, q * P:(q + 1) * P], yb[:, q * P:(q + 1) * P], ident[:, :])
                return last

            def turn(e, s, uses):
                first = not isinstance(e, int)
                if first or e < E:
                    pe.wait_ge(gu_landed[s], 32 * uses)
                    pe.wait_ge(xb_ready, e + 1)
                    if first or e >= RING:
                        pe.wait_ge(eh_ready, e + (1 - RING))
                    gate_up(s).then_inc(gu_full, 1)
                if first or e >= 2:
                    pe.wait_ge(yb_ready, e - 1)
                    if first or e >= 3:
                        pe.wait_ge(ys_ready, e - 2)
                    turn_y().then_inc(yt_full, 1)
                if first or 1 <= e <= E:
                    sd = slot(s - 1)
                    pe.wait_ge(d_landed[sd], 16 * (uses if s else uses - 1) if first else 16 * ((e - 1) // RING + 1))
                    pe.wait_ge(ht_ready, e)
                    down(sd).then_inc(y_full, 1)
                if first or e < E:
                    pe.wait_ge(eh_ready, e + 1)
                    turn_h(s).then_inc(ht_full, 1)

            for e in range(FIRST):
                turn(e, slot(e), e // RING + 1)
            with pe.Fori(0, (E - FIRST) // RING) as i:
                for j in range(RING):
                    turn(3 * i + (FIRST + j), slot(FIRST + j), i + ((FIRST + j) // RING + 1))
            for e in (E, E + 1):
                turn(e, slot(e), None)
            extra = pe.value_load(wli[0:1, 2 * MAXB:2 * MAXB + 1], min_val=0, max_val=MAXB)
            pe.wait_ge(ys_ready, E)
            with pe.If(extra > 0):
                with pe.Fori(0, extra) as i:
                    pe.wait_ge(xb_landed, 48 * i + 48)
                    pe.wait_ge(xb_xb, i + 1)
                    gate_up(0).then_inc(xb_gu, 1)
                    pe.wait_ge(xb_h, i + 1)
                    turn_h(0).then_inc(xb_htf, 1)
                    pe.wait_ge(xb_ht, i + 1)
                    down(0).then_inc(xb_y, 1)
                    pe.wait_ge(xb_yb, i + 1)
                    turn_y().then_inc(xb_yt, 1)
            pe.wait_ge(experts_done, 1)
            for s in range(ST):
                for j in range(2):
                    def mms(bk):
                        for k in range(4):
                            last = pe.transpose(bk[:, k * P:k * P + P], ys[:, 4 * j + k, s * P:s * P + P], ident[:, :])
                        return last
                    fill(("yn", 2 * s + j), mms)
            for n in (8, 9):
                moved(pe, ("yn", n))
            for k in range(KD):
                def mms(bk):
                    for s in range(ST):
                        last = pe.matmul(bk[:, 0:T], ynat[:, s, k * P:k * P + P], wcT[:, s, :], start=(s == 0), stop=(s == ST - 1))
                    return last
                fill(("mo", k), mms)
            pe.wait_ge(wpp_landed, 16)
            for k in range(KD):
                def mms(bk):
                    for c in range(2):
                        last = pe.matmul(bk[:, 0:T], wpp[:, c, k * P:k * P + P], pT[:, c, :], start=(c == 0), stop=(c == 1))
                    return last
                fill(("pp", k), mms)
            pe.wait_ge(sq_ready, 3)
            sums(("ss", 2), sqm)
            pe.wait_ge(h_ready, 3)
            linear("pg", hT)
            pe.wait_ge(sq_ready, 4)
            sums(("ss", 3), sqm)
            pe.wait_ge(h_ready, 4)
            for i, (t0, n) in enumerate(TILES):
                for j in range(2):
                    def mms(bk):
                        for k in range(4):
                            last = pe.transpose(bk[0:n, k * P:k * P + P], hT[:, 4 * j + k, t0:t0 + n], ident[:, :])
                        return last
                    fill(("yo", 2 * i + j), mms)

        @block.scalar
        def _(act):
            def take(f, *outs, func=ACT.Copy, scale=1.0, n=P):
                filled(act, f)
                for out, a in outs:
                    last = act.activation(out, a, func, scale=scale)
                last.then_inc(acc_empty["act"], 1)

            def wide(f):
                return acc(f)[:, 0:T]

            def norm(n, sq):
                act.activation(sq[:, :, :], xT[:, :, :], ACT.Square).then_inc(sq_ready, 1)

            def norm_root(n):
                filled(act, ("ss", n))
                if n:
                    act.wait_ge(h_ready, n)
                act.activation(root[:, :], wide(("ss", n)), ACT.Sqrt, bias=eps[:, 0:1], scale=1.0 / D).then_inc(acc_empty["act"], 1)

            for k in range(KD):
                take(("x", k), (xT[:, k, :], wide(("x", k))))
            for c in range(2):
                take(("pn", c), (pT[:, c, :], wide(("pn", c))))
            moved(act, ("x", KD - 1))
            norm(0, sqx)
            act.wait_ge(consts, 2)
            norm_root(0)
            act.wait_ge(hist_ready, 1)
            for m in range(KD):
                bk = acc(("xm", m))
                take(("xm", m), (xme[:, m, 3:PX], bk[:, 0:TP]),
                     (xme[:, m, PX:XE].rearrange("p (b j) -> p b j", b=NB)[:, :, 3:SXX], bk[:, TP:T].rearrange("p (b j) -> p b j", b=NB)))
            act.wait_ge(conv_done, 1)
            act.activation(xq[:, :, 0:TP], cv[:, :, 0:TP], ACT.Sigmoid)
            for k in range(KD):
                last = act.activation(xq[:, k, TP:T].rearrange("p (b j) -> p b j", b=NB),
                                      cv_sample(k), ACT.Sigmoid)
            last.then_inc(sig_ready, 1)
            for m in range(6):
                j, i = divmod(m, 3)
                n = TILES[i][1]
                take(("v", m), (vn[0:n, i, 512 * j:512 * j + 512], acc(("v", m))[0:n, :]))
            act.wait_ge(gate_step, 1)
            act.activation(rows[:, 2, :], rows[:, 2, :], ACT.Exp, scale=-1.0).then_inc(act_step, 1)
            act.wait_ge(act_step, 1)
            act.activation(rows[:, 2, :], rows[:, 2, :], ACT.Ln, bias=1.0).then_inc(gate_act, 1)
            act.wait_ge(gate_step, 2)
            act.activation(rows[:, 1, :], rows[:, 1, :], ACT.Exp).then_inc(rows_ready, 1)
            act.activation(rows[:, 3, 0:NS], rows[:, 3, 0:NS], ACT.Exp)
            act.activation(rows[:, 7, :], rows[:, 7, :], ACT.Exp, scale=-1.0).then_inc(rows_ready, 1)

            def take_qk(h):
                p = h % 2
                for n in range(4):
                    r, c = divmod(n, 2)
                    f = ("qk", h, n)
                    take(f, ((kT if r else qT)[:, p, c, :], wide(f)), scale=1.0 if r else DH ** -0.5)
                for i, (t0, n) in enumerate(TILES):
                    f = ("kn", h, i)
                    take(f, (kn[0:n, p, i, :], acc(f)[0:n, 0:DH]))

            def exps(h):
                act.wait_ge(args_ready, h + 1)
                for o, n, i, r in ((0, 256, 0, P), (256, P, 1, P), (384, NS, 2, NS)):
                    last = act.activation(expo[0:r, o:o + n], expo[0:r, o:o + n], ACT.Exp, bias=awT[0:r, 0, i, h:h + 1])
                last.then_inc(exps_ready, 1)

            take_qk(0)
            for j in range(2):
                if j == 0:
                    act.wait_ge(h_ready, 1)
                take(("to", j), (tailn[:, 512 * j:512 * j + 512], acc(("to", j))[0:27, :]))
            exps(0)
            take_qk(1)
            for h in range(H):
                if MID[h][0] == "sc":
                    act.wait_ge(tailn_stored, 32)
                    for m in range(KD):
                        take(("sc", m), (s1[:, m, :], wide(("sc", m))))
                if MID[h][0] == "gb":
                    act.wait_ge(tails_ready, 2)
                    for m in range(KD):
                        take(("gb", m), (s4[:, m, :], wide(("gb", m))), func=ACT.Sigmoid)
                act.wait_ge(hm_ready, h + 1)
                act.activation(hsq[:, :, :], xq[:, 2 * h:2 * h + 2, :], ACT.Square).then_inc(hsq_ready, 1)
                if h:
                    act.wait_ge(cp_stored, 16 * h)
                take(("Cp", h), (cpn[:, :, :].rearrange("p a b -> p (a b)"), acc(("Cp", h))[:, :]))
                act.wait_ge(ss_full, h + 1)
                act.activation(ssT[:, h, :], b_enm[:, 0:T], ACT.Copy).then_inc(ss_taken, 1)
                if h + 1 < H:
                    exps(h + 1)
                if h + 2 < H:
                    take_qk(h + 2)
            act.wait_ge(c_stored, 16 * H)
            for j in range(2):
                take(("tu", j), (tails[:, 512 * j:512 * j + 512], acc(("tu", j))[0:18, :]))
            act.wait_ge(ss_taken, H)
            act.activation(ssT[:, :, :], ssT[:, :, :], ACT.Sqrt, bias=eps[:, 0:1], scale=1.0 / DH).then_inc(hroot, 1)
            for m in range(KD):
                take(("o", m), (oT[:, m, :], wide(("o", m))), func=ACT.Sigmoid)
            for m in range(KD):
                take(("ga", m), (s1[:, m, :], wide(("ga", m))), func=ACT.Sigmoid)

            moved(act, ("wo", KD - 1))
            act.wait_ge(stored, 16 * 6)
            act.wait_ge(cp_stored, 16 * H)
            norm(1, sqm)
            norm_root(1)
            for i in range(3):
                for j in range(2):
                    f = ("hn", 2 * i + j)
                    take(f, (hn[:, i, 512 * j:512 * j + 512], acc(f)[:, :]))
            act.wait_ge(rt_arg, 1)
            act.activation(r4[:, :, 2, :], r4[:, :, 2, :], ACT.Exp)
            act.activation(r1[:, :, 7:8], r1[:, :, 7:8], ACT.Exp).then_inc(rt_exp, 1)
            for k in range(KD):
                for j in range(2):
                    f = ("xs", 2 * k + j)
                    take(f, (xs[:, k, j * T:j * T + T], wide(f)))
            for s in range(ST):
                f = ("wc", s)
                take(f, (wcT[:, s, :], wide(f)))

            def gate_sigmoid(s):
                return act.activation(sg[:, s, :], bank[s][:, 0:P], ACT.Sigmoid)

            def take_y():
                return act.activation(yb[:, :], b_y[:, :], ACT.Copy)

            def place_y(off):
                for c in range(2):
                    last = act.activation(ys[:, 4 * c:4 * c + 4, bass.ds(off, CAP)],
                                          b_yt[:, :].rearrange("p (q c t) -> p q c t", q=4, c=2)[:, :, c, :], ACT.Copy)
                return last

            def turn(e, s):
                first = not isinstance(e, int)
                if first or e < E:
                    act.wait_ge(gu_full, e + 1)
                    if first or e >= RING:
                        act.wait_ge(ht_full, e + (1 - RING))
                    gate_sigmoid(s).then_inc(esig_ready, 1)
                if first or e >= 2:
                    off = act.value_load(offi[0:1, bass.ds(e - 2, 1)], min_val=0, max_val=PAIRS)
                    act.wait_ge(yt_full, e - 1)
                    place_y(off).then_inc(ys_ready, 1)
                if first or 1 <= e <= E:
                    act.wait_ge(y_full, e)
                    take_y().then_inc(yb_ready, 1)

            act.wait_ge(offs_ready, 1)
            for e in range(FIRST):
                turn(e, slot(e))
            with act.Fori(0, (E - FIRST) // RING) as i:
                for j in range(RING):
                    turn(3 * i + (FIRST + j), slot(FIRST + j))
            for e in (E, E + 1):
                turn(e, slot(e))
            extra = act.value_load(wli[0:1, 2 * MAXB:2 * MAXB + 1], min_val=0, max_val=MAXB)
            act.wait_ge(ys_ready, E)
            act.sem_inc(xb_done, 1)
            with act.If(extra > 0):
                with act.Fori(0, extra) as i:
                    off = act.value_load(wli[0:1, bass.ds(i + MAXB, 1)], min_val=0, max_val=PAIRS)
                    act.wait_ge(xb_gu, i + 1)
                    gate_sigmoid(0).then_inc(xb_sig, 1)
                    act.wait_ge(xb_y, i + 1)
                    take_y().then_inc(xb_yb, 1)
                    act.wait_ge(xb_yt, i + 1)
                    place_y(off).then_inc(xb_done, 1)
            act.sem_inc(experts_done, 1)

            for n in range(2 * ST):
                s, j = divmod(n, 2)
                take(("yn", n), (ynat[:, s, 512 * j:512 * j + 512], acc(("yn", n))[:, :]))
            for k in range(KD):
                take(("pp", k), (ppr[:, k, :], wide(("pp", k))))
            moved(act, ("mo", KD - 1))
            norm(2, sqm)
            norm_root(2)
            for m in range(KD):
                take(("pg", m), (sqm[:, m, :], wide(("pg", m))), func=ACT.Sigmoid)
            act.wait_ge(x4_ready, 1)
            norm(3, sqm)
            norm_root(3)
            for i, (t0, n) in enumerate(TILES):
                for j in range(2):
                    f = ("yo", 2 * i + j)
                    take(f, (x4n[0:n, i, 512 * j:512 * j + 512], acc(f)[0:n, :]))

        @block.gpsimd
        def _(pool):
            def select(out, pattern, cm, base_, fill, op=ALU.is_ge):
                return pool.affine_select(out=out, in_=out, pattern=pattern, compare_op=op, fill=fill, base=base_, channel_multiplier=cm)

            own = [0]
            go = step(pool, pool_step, own)
            go(pool.memset(ident[:, :], 0.0))
            select(ident[:, :], [[-1, P]], 1, 0, 1.0, ALU.not_equal).then_inc(consts, 1)
            pool.memset(eps[:, :], EPS)
            pool.memset(ones[:, :], 1.0).then_inc(consts, 1)
            go(pool.memset(selh[:, :, :], 0.0))
            select(selh[:, :, :], [[-1, H], [0, P]], 1, 0, 1.0, ALU.not_equal).then_inc(consts, 1)
            go(pool.memset(mask[:, :], 0.0))
            go(select(mask[:, 0:256], [[1, 256]], -1, 0, NEG))
            go(select(mask[:, 256:384], [[1, P]], -1, 0, NEG))
            ms = mask[0:NS, 384:448].rearrange("p (b j) -> p b j", b=NB)
            go(select(ms, [[-TS, NB], [0, TS]], 1, 0, NEG))
            select(ms, [[TS, NB], [1, TS]], -1, 0, NEG).then_inc(consts, 1)
            go(pool.memset(oneb[:, :], 1.0))
            go(select(oneb[:, :], [[-TS, NB]], 1, 0, 0.0))
            select(oneb[:, :], [[TS, NB]], -1, TS - 1, 0.0).then_inc(consts, 1)

            go(pool.memset(onet[:, :, :], 1.0))
            go(select(onet[:, :, :], [[-TS, NB], [1, NS]], 0, 0, 0.0))
            select(onet[:, :, :], [[TS, NB], [-1, NS]], 0, TS - 1, 0.0).then_inc(consts, 1)

            def load_wqk(h):
                if h:
                    pool.wait_ge(acc_full, index[("kn", h - 1, 2)] + 1)
                for r, w in enumerate((I["w_q"], I["w_k"])):
                    pool.dma_start(wqk[:, r, :, :], w[0, h].rearrange("(d p) e -> p d e", p=P)).then_inc(wqk_landed, 16)

            def load_c(h):
                pool.dma_start(cbuf_rows, I["state_mlstm_C"][0, :, h].rearrange("b (p d) e -> p b (d e)", p=P)).then_inc(c_landed, 16)

            load_wqk(0)
            pool.wait_ge(acc_full, index[("x", KD - 1)] + 1)
            load_c(0)
            pool.wait_ge(m_ready, 1)
            pool.dma_start(O[9][0].rearrange("b h -> h b"), mo[:, 0:NB]).then_inc(stored, 16)
            pool.dma_start(O[4][0].rearrange("a h -> h a"), mo[:, NB:NB + 1]).then_inc(stored, 16)
            load_wqk(1)
            moved(pool, ("to", 1))
            pool.dma_start(O[5][0, 0], tailn[0:3, :]).then_inc(tailn_stored, 16)
            pool.dma_start(O[10][0].rearrange("b j d -> (b j) d"), tailn[3:27, :]).then_inc(tailn_stored, 16)
            pool.wait_ge(aw_ready, 1)
            for h in range(H):
                p = h % 2
                moved(pool, ("kn", h, 2))
                if h:
                    pool.wait_ge(acc_full, index[("n", h - 1)] + 1)
                pool.tensor_tensor(wkm[:, :, :], kn[0:NS, p, 2:3, :].to_broadcast([NS, NB, DH]),
                                   wsel[:, h, :].unsqueeze(2).to_broadcast([NS, NB, DH]), ALU.mult)
                for i in range(2):
                    last = pool.tensor_scalar(wkp[:, i, :], kn[:, p, i, :], awT[:, 1, i, h:h + 1], None, ALU.mult)
                last.then_inc(wk_ready, 1)
                if h + 2 < H:
                    load_wqk(h + 2)
                pool.wait_ge(c_updated, h + 1)
                pool.dma_start(O[7][0, :, h].rearrange("b (p d) e -> p b (d e)", p=P), cbuf_rows).then_inc(c_stored, 16)
                moved(pool, ("Cp", h))
                pool.dma_start(O[2][0, 0, h].rearrange("(p d) e -> p d e", p=P), cpn[:, :, :]).then_inc(cp_stored, 16)
                if h + 1 < H:
                    pool.wait_ge(c_stored, 16 * (h + 1))
                    load_c(h + 1)
            pool.wait_ge(n_ready, H)
            pool.dma_start(O[8][0], nrow[:, :, :]).then_inc(stored, 16)
            pool.dma_start(O[3][0], npr[:, :, :]).then_inc(stored, 16)
            moved(pool, ("tu", 1))
            pool.dma_start(O[6][0, 0], tails[0:2, :]).then_inc(stored, 16)
            pool.dma_start(O[11][0].rearrange("b j d -> (b j) d"), tails[2:18, :]).then_inc(stored, 16)
            pool.wait_ge(tailn_stored, 32)
            moved(pool, ("wo", KD - 1))
            pool.wait_ge(stored, 16 * 6)
            pool.wait_ge(cp_stored, 16 * H)
            pool.memset(valid[:, :], 1.0)
            go(pool.memset(tri[:, :], 1.0))
            go(select(tri[:, :], [[1, P]], -1, -1, 0.0))
            go(select(valid[:, :], [[-P, 3]], -1, T - 1, 0.0))
            f = dict(allow_small_or_imprecise_dtypes=True)
            pool.iota(io4[:, :], [[1, G]], base=0, channel_multiplier=0, **f)
            pool.iota(io8[:, :], [[1, EG]], base=0, channel_multiplier=0, **f)
            pool.iota(ios[:, :], [[1, PAIRS]], base=0, channel_multiplier=0, **f)
            pool.iota(ioe[:, :, :], [[0, JX], [1, E]], base=0, channel_multiplier=0, **f)
            pool.iota(ioj[:, :, :], [[CAP, JX], [0, E]], base=CAP, channel_multiplier=0, **f).then_inc(consts2, 1)

        @block.vector
        def _(dve):
            own = [0]
            go = step(dve, dve_step, own)
            empty = acc_empty["dve"]

            def wide(f):
                return acc(f)[:, 0:T]

            def norm_scale(n, g):
                moved(dve, ("ss", n))
                if n == 0:
                    dve.wait_ge(cols_ready, 1)
                go(dve.reciprocal(rstd[:, :], root[:, :]))
                for k in range(KD):
                    last = dve.scalar_tensor_tensor(hT[:, k, 0:T], xT[:, k, :], cols[:, k, g:g + 1], rstd[:, :], ALU.mult, ALU.mult)
                last.then_inc(h_ready, 1)

            seq = lambda a: a.rearrange("p (b j) -> p b j", b=NB)
            dve.memset(hT[:, :, T:3 * P], 0.0)
            dve.memset(xme[:, :, 0:3], 0.0)
            dve.memset(qz[:, :, :, NS:WIDE], 0.0)
            dve.memset(pt[:, 448:384 + WIDE], 0.0)
            dve.memset(rows[:, 3, :], 1.0)
            go(dve.memset(rows[:, 4, :], 0.0))
            dve.memset(rows[:, 3, 0:1], 0.0)
            dve.memset(rows[:, 3, TP:T:TS], 0.0)
            dve.memset(rows[:, 4, 0:1], NEG)
            go(dve.memset(rows[:, 4, TP:T:TS], NEG))
            filled(dve, ("rows",))
            dve.tensor_copy(cols[:, :, :].rearrange("p k r -> p (k r)"), acc(("rows",))[:, 0:KD * R_ALL]).then_inc(empty, 1)
            moved(dve, ("rows",))
            for k in range(KD):
                last = dve.tensor_copy(seq(xme[:, k, PX:XE])[:, :, 0:3], seq(cols[:, k, R_MCH:R_SCH]))
            last.then_inc(hist_ready, 1)
            filled(dve, ("nn",))
            dve.tensor_copy(nT[:, :, :].rearrange("p c n -> p (c n)"), acc(("nn",))[:, 0:64]).then_inc(empty, 1)
            dve.sem_inc(cols_ready, 1)
            norm_scale(0, R_MIX)

            moved(dve, ("xm", KD - 1))
            for j in range(4):
                for k in range(KD):
                    x, w = xme[:, k, j:j + XE - 3], cols[:, k, R_MCW + j:R_MCW + j + 1]
                    last = dve.tensor_scalar(cv[:, k, :], x, w, None, ALU.mult) if j == 0 else \
                        dve.scalar_tensor_tensor(cv[:, k, :], x, w, cv[:, k, :], ALU.mult, ALU.add)
                last.then_inc(conv_done if j == 3 else dve_step, 1)
                if j < 3:
                    own[0] += 1
                    dve.wait_ge(dve_step, own[0])
            dve.tensor_copy(tailc[:, :, 0:3], xme[:, :, PX - 3:PX])
            for k in range(KD):
                last = dve.tensor_copy(seq(tailc[:, k, 3:27]), seq(xme[:, k, PX:XE])[:, :, SXX - 3:SXX])
            last.then_inc(tails_ready, 1)

            R = lambda i, a=0, b=T: rows[:, i, a:b]
            bc = lambda a: a.unsqueeze(2).to_broadcast([H, NB, TS])
            last_of = lambda i: rows[:, i, TP + TS - 1:T:TS]
            dve.wait_ge(in_small, 16 * 9)
            filled(dve, ("if", 0))
            dve.tensor_scalar(R(0), acc(("if", 0))[0:H, 0:T], bif[:, 0:1], None, ALU.add).then_inc(empty, 1)
            filled(dve, ("if", 1))
            dve.tensor_scalar(R(1), acc(("if", 1))[0:H, 0:T], bif[:, 1:2], None, ALU.add).then_inc(empty, 1)
            moved(dve, ("if", 1))
            dve.scalar_tensor_tensor(R(2), R(1), -1.0, R(1), ALU.mult, ALU.max).then_inc(gate_step, 1)
            dve.wait_ge(gate_step, 1)
            go(dve.tensor_scalar(R(1), R(1), 0.0, None, ALU.min))
            dve.wait_ge(sig_ready, 1)
            dve.tensor_tensor(xq[:, :, 0:TP], xq[:, :, 0:TP], cv[:, :, 0:TP], ALU.mult)
            for k in range(KD):
                last = dve.tensor_tensor(seq(xq[:, k, TP:T]), seq(xq[:, k, TP:T]), cv_sample(k), ALU.mult)
            last.then_inc(xq_ready, 1)
            dve.wait_ge(gate_act, 1)
            go(dve.tensor_tensor(R(1), R(1), R(2), ALU.subtract))
            go(dve.tensor_tensor_scan(R(5), R(3), R(1), 0.0, ALU.mult, ALU.add))
            go(dve.tensor_tensor(R(0), R(0), R(5), ALU.subtract))
            go(dve.tensor_copy(R(1), R(0)))
            dve.tensor_scalar(R(1, 0, 1), R(1, 0, 1), 0.0, None, ALU.max)
            go(dve.tensor_tensor(rows[:, 1, TP:T:TS], rows[:, 1, TP:T:TS], m0r[:, :], ALU.max))
            go(dve.tensor_tensor_scan(R(6), R(4), R(1), 0.0, ALU.add, ALU.max))
            dve.tensor_scalar(R(2), R(6), -1.0, None, ALU.mult)
            dve.tensor_tensor(R(7), R(5), R(6), ALU.add)
            dve.tensor_tensor(seq(R(3, 0, NS)), bc(m0r[:, :]), seq(R(6, TP, T)), ALU.subtract)
            dve.tensor_scalar(R(1, 0, TP), R(0, 0, TP), R(6, TP - 1, TP), None, ALU.subtract)
            go(dve.tensor_tensor(seq(R(1, TP, T)), seq(R(0, TP, T)), bc(last_of(6)), ALU.subtract))
            dve.tensor_copy(mo[:, NB:NB + 1], R(7, TP - 1, TP))
            dve.tensor_copy(mo[:, 0:NB], last_of(7)).then_inc(m_ready, 1)
            dve.wait_ge(m_ready, 1)
            dve.sem_inc(gate_step, 1)
            filled(dve, ("aw", 0))
            for r in range(2):
                for i, (t0, n) in enumerate(TILES):
                    c = (3 * r + i) * H
                    last = dve.tensor_copy(awT[0:n, r, i, :], acc(("aw", 0))[0:n, c:c + H])
            dve.tensor_copy(decT[:, :], acc(("aw", 0))[0:NB, 6 * H:7 * H]).then_inc(empty, 1)
            moved(dve, ("aw", 0))
            dve.wait_ge(consts, 6)
            dve.tensor_tensor(wsel[:, :, :], awT[0:NS, 1, 2, :].unsqueeze(2).to_broadcast([NS, H, NB]),
                              oneb[:, :].unsqueeze(1).to_broadcast([NS, H, NB]), ALU.mult).then_inc(aw_ready, 1)

            def probs(h):
                p = h % 2
                dve.wait_ge(scores_full, h + 1)
                dve.tensor_tensor(expo[:, 0:256], b_bc[:, 0:256], mask[:, 0:256], ALU.add)
                dve.tensor_tensor(expo[:, 256:384], b_bc[:, P:256], mask[:, 256:384], ALU.add)
                dve.tensor_tensor(expo[0:NS, 384:448], b_bc[0:NS, TP:T], mask[0:NS, 384:448], ALU.add).then_inc(args_ready, 1)
                dve.tensor_copy(den[:, :], b_enm[:, 0:T])
                go(dve.tensor_copy(wint[:, :], b_bc[:, T:T + NS]))
                qs = qT[:, p, :, TP:T]
                go(dve.tensor_tensor(qw[:, :, :], qs, wint[:, :].unsqueeze(1).to_broadcast([P, 2, NS]), ALU.mult))
                for c in range(2):
                    n0 = nT[:, c, :].rearrange("p (b h) -> p b h", h=H)[:, :, h:h + 1].to_broadcast([P, NB, TS])
                    last = dve.tensor_tensor(seq(qn[:, c, :]), seq(qw[:, c, :]), n0, ALU.mult)
                for c in range(2):
                    last = dve.tensor_tensor(qz[:, c, :, 0:NS], qw[:, c:c + 1, :].to_broadcast([P, NB, NS]), onet[:, :, :], ALU.mult)
                dve.wait_ge(exps_ready, h + 1)
                dve.tensor_tensor(pt[:, 0:384], expo[:, 0:384], b_s[:, 0:384], ALU.mult)
                dve.tensor_tensor(pt[0:NS, 384:448], expo[0:NS, 384:448], b_s[0:NS, 384:448], ALU.mult).then_inc(probs_ready, 1)

            def outputs(h):
                dve.wait_ge(pv_full, h + 1)
                go(dve.tensor_tensor(den[:, :], b_s[:, 0:T], den[:, :], ALU.max))
                go(dve.scalar_tensor_tensor(den[:, :], b_s[:, 0:T], -1.0, den[:, :], ALU.mult, ALU.max))
                go(dve.reciprocal(den[:, :], den[:, :]))
                for c in range(2):
                    last = dve.tensor_tensor(xq[:, 2 * h + c, :], b_num[c][:, 0:T], den[:, :], ALU.mult)
                last.then_inc(hm_ready, 1)

            def new_states(h):
                for b in range(NB):
                    f = ("C", h, b)
                    filled(dve, f)
                    c = cbuf[:, b, :, :].rearrange("p d e -> p (d e)")
                    last = dve.scalar_tensor_tensor(c, c, wint[:, b * TS + TS - 1:b * TS + TS], acc(f)[:, :], ALU.mult, ALU.add)
                    last.then_inc(empty, 1)
                moved(dve, ("C", h, NB - 1))
                dve.sem_inc(c_updated, 1)
                f = ("n", h)
                filled(dve, f)
                dve.scalar_tensor_tensor(nrow[:, h, :], nrow[:, h, :], decT[:, h:h + 1], acc(f)[0:NB, 0:DH], ALU.mult, ALU.add)
                dve.tensor_copy(npr[:, h, :], acc(f)[32:33, DH:2 * DH]).then_inc(empty, 1)
                moved(dve, f)
                dve.sem_inc(n_ready, 1)

            sample_u = lambda a, n: a.rearrange("p (b j) -> p b j", b=NB)
            probs(0)
            for h in range(H):
                if MID[h][0] == "sx":
                    moved(dve, ("sc", KD - 1))
                    dve.memset(cxe[:, :, 0:2], 0.0)
                    for k in range(KD):
                        dve.tensor_copy(seq(cxe[:, k, PU:UE])[:, :, 0:2], seq(cols[:, k, R_SCH:R_ALL]))
                    for m in range(KD):
                        f = ("sx", m)
                        filled(dve, f)
                        dve.tensor_tensor(cxe[:, m, 2:PU], acc(f)[:, 0:TP], s1[:, m, 0:TP], ALU.mult)
                        dve.tensor_tensor(seq(cxe[:, m, PU:UE])[:, :, 2:SU], seq(acc(f)[:, TP:T]), seq(s1[:, m, TP:T]), ALU.mult)\
                            .then_inc(empty, 1)
                    moved(dve, ("sx", KD - 1))
                if MID[h][0] == "sb":
                    for m in range(KD):
                        f = ("sb", m)
                        filled(dve, f)
                        dve.tensor_tensor(s1[:, m, 0:TP], acc(f)[:, 0:TP], uT[:, m, 0:TP], ALU.mult)
                        us = seq(uT_sample(m))[:, :, 0:TS]
                        dve.tensor_tensor(seq(s1[:, m, TP:T]), seq(acc(f)[:, TP:T]), us, ALU.mult).then_inc(empty, 1)
                outputs(h)
                new_states(h)
                if h + 1 < H:
                    probs(h + 1)
                if MID[h][0] == "sx":
                    for j in range(3):
                        for k in range(KD):
                            x, w = cxe[:, k, j:j + UE - 2], cols[:, k, R_SCW + j:R_SCW + j + 1]
                            last = dve.tensor_scalar(uT[:, k, :], x, w, None, ALU.mult) if j == 0 else \
                                dve.scalar_tensor_tensor(uT[:, k, :], x, w, uT[:, k, :], ALU.mult, ALU.add)
                        go(last)
                    dve.tensor_copy(tailu[:, :, 0:2], cxe[:, :, PU - 2:PU])
                    for k in range(KD):
                        last = dve.tensor_copy(seq(tailu[:, k, 2:18]), seq(cxe[:, k, PU:UE])[:, :, SU - 2:SU])
                    last.then_inc(tails_ready, 1)

            dve.wait_ge(hroot, 1)
            go(dve.reciprocal(ssT[:, :, :], ssT[:, :, :]))
            for k in range(KD):
                last = dve.scalar_tensor_tensor(xq[:, k, :], xq[:, k, :], cols[:, k, R_HEAD:R_HEAD + 1], ssT[:, k // 2, :], ALU.mult, ALU.mult)
            go(last)
            moved(dve, ("o", KD - 1))
            dve.tensor_tensor(oT[:, :, :], oT[:, :, :], xq[:, :, :], ALU.mult).then_inc(ya_ready, 1)
            moved(dve, ("gb", KD - 1))
            for m in range(KD):
                f = ("sout", m)
                filled(dve, f)
                dve.tensor_tensor(s4[:, m, :], wide(f), s4[:, m, :], ALU.mult).then_inc(empty, 1)
            for m in range(KD):
                f = ("a", m)
                filled(dve, f)
                moved(dve, ("ga", m))
                go(dve.tensor_tensor(s1[:, m, :], wide(f), s1[:, m, :], ALU.mult))
                dve.tensor_tensor(s4[:, m, :], s4[:, m, :], s1[:, m, :], ALU.add).then_inc(empty, 1)
            for m in range(KD):
                f = ("wo", m)
                filled(dve, f)
                dve.tensor_tensor(xT[:, m, :], wide(f), xT[:, m, :], ALU.add).then_inc(empty, 1)
            norm_scale(1, R_FFN)

            B3 = lambda a, n: a.to_broadcast([P, 3, n])
            c1 = lambda i: r1[:, :, i:i + 1]
            dve.wait_ge(consts2, 1)
            dve.wait_ge(stored, 16 * 6)
            filled(dve, ("lg", 0))
            dve.tensor_copy(lg[:, :, :].rearrange("p t n -> p (t n)"), acc(("lg", 0))[:, 0:3 * (G + E)]).then_inc(empty, 1)
            moved(dve, ("lg", 0))

            def first_max(x, mx, idx, one, tmp, io, n):
                go(dve.tensor_reduce(mx, x, AX.X, ALU.max))
                go(dve.tensor_tensor(tmp, x, B3(mx, n), ALU.is_equal))
                go(dve.tensor_scalar(tmp, tmp, -100.0, None, ALU.mult))
                go(dve.tensor_tensor(tmp, tmp, io[:, :].unsqueeze(1).to_broadcast([P, 3, n]), ALU.add))
                go(dve.tensor_reduce(idx, tmp, AX.X, ALU.min))
                go(dve.tensor_tensor(one, tmp, B3(idx, n), ALU.is_equal))

            gl = lg[:, :, 0:G]
            first_max(gl, c1(0), c1(2), r4[:, :, 0, :], r4[:, :, 1, :], io4, G)
            go(dve.tensor_tensor(r4[:, :, 2, :], gl, B3(c1(0), G), ALU.subtract))
            for i in range(3):
                g1 = r4[:, i, 0, :].unsqueeze(2).to_broadcast([P, G, EG])
                last = dve.tensor_tensor(pick[:, 0, i, :].rearrange("p (g e) -> p g e", g=G),
                                         lg[:, i, G:G + E].rearrange("p (g e) -> p g e", g=G), g1, ALU.mult)
            go(last)
            for i in range(3):
                last = dve.tensor_reduce(r8[:, i, 0, :], pick[:, 0, i, :].rearrange("p (g e) -> p e g", g=G), AX.X, ALU.add)
            go(last)
            first_max(r8[:, :, 0, :], c1(3), c1(4), r8[:, :, 1, :], r8[:, :, 4, :], io8, EG)
            go(dve.tensor_scalar(r8[:, :, 2, :], r8[:, :, 1, :], NEG, None, ALU.mult))
            go(dve.tensor_tensor(r8[:, :, 2, :], r8[:, :, 2, :], r8[:, :, 0, :], ALU.add))
            first_max(r8[:, :, 2, :], c1(5), c1(6), r8[:, :, 3, :], r8[:, :, 4, :], io8, EG)
            dve.tensor_tensor(c1(7), c1(5), c1(3), ALU.subtract).then_inc(rt_arg, 1)
            for q, o in ((0, 1), (1, 3)):
                for i in range(3):
                    last = dve.tensor_tensor(pick[:, q, i, :].rearrange("p (g e) -> p g e", g=G),
                                             r4[:, i, 0, :].unsqueeze(2).to_broadcast([P, G, EG]),
                                             r8[:, i, o, :].unsqueeze(1).to_broadcast([P, G, EG]), ALU.mult)
            go(last)
            go(dve.tensor_tensor(m32[:, :, :], pick[:, 0, :, :], pick[:, 1, :, :], ALU.add))
            dve.tensor_tensor(m32[:, :, :], m32[:, :, :], valid[:, :].unsqueeze(2).to_broadcast([P, 3, E]), ALU.mult).then_inc(m32_ready, 1)
            dve.wait_ge(rt_exp, 1)
            dve.tensor_reduce(c1(1), r4[:, :, 2, :], AX.X, ALU.add)
            go(dve.tensor_scalar(c1(8), c1(7), 1.0, None, ALU.add))
            go(dve.tensor_tensor(c1(8), c1(8), c1(1), ALU.mult))
            go(dve.reciprocal(c1(8), c1(8)))
            go(dve.tensor_tensor(c1(9), c1(8), c1(7), ALU.mult))
            filled(dve, ("rank", 0))
            rk = acc(("rank", 0))
            go(dve.tensor_copy(cnt[:, 0, :], rk[:, 3 * E:4 * E]))
            dve.memset(cnt[:, 1, :], 1.0)
            go(dve.memset(pos[:, 0, :], 1.0))
            go(dve.tensor_tensor_scan(cnt[:, 1, :], pos[:, 0, :], cnt[:, 0, :], 0.0, ALU.mult, ALU.add))
            go(dve.tensor_tensor(cnt[:, 2, :], cnt[:, 1, :], cnt[:, 0, :], ALU.subtract))
            dve.tensor_tensor(pos[:, :, :], rk[:, 0:3 * E].rearrange("p (t e) -> p t e", t=3),
                              cnt[:, 2:3, :].to_broadcast([P, 3, E]), ALU.add).then_inc(empty, 1)
            moved(dve, ("rank", 0))
            for q in range(2):
                go(dve.tensor_tensor(pick[:, q, :, :], pick[:, q, :, :], pos[:, :, :], ALU.mult))
                go(dve.tensor_reduce(c1(10 + q), pick[:, q, :, :], AX.X, ALU.add))
                go(dve.tensor_scalar(c1(10 + q), c1(10 + q), 1.0, None, ALU.add))
                go(dve.tensor_tensor(c1(10 + q), c1(10 + q), valid[:, :].unsqueeze(2), ALU.mult))
                go(dve.tensor_scalar(c1(10 + q), c1(10 + q), -1.0, None, ALU.add))
            for i in range(3):
                last = dve.tensor_scalar(gsel[:, i, :], ios[:, :], r1[:, i, 10:11], None, ALU.is_equal)
            go(last)
            for i in range(3):
                last = dve.scalar_tensor_tensor(gsel[:, i, :], ios[:, :], r1[:, i, 11:12], gsel[:, i, :], ALU.is_equal, ALU.add)
            last.then_inc(gsel_ready, 1)
            C_ = lambda i: cnt[0:1, i:i + 1, :].to_broadcast([1, JX, E])
            dve.tensor_copy(offi[:, :], cnt[0:1, 2, :])
            go(dve.tensor_tensor(blk[:, 0], C_(0), ioj[:, :, :], ALU.is_gt))
            fl = blk[:, 0].rearrange("p j e -> p (j e)")
            go(dve.memset(blk[:, 1], 1.0))
            flat = lambda i: blk[:, i].rearrange("p j e -> p (j e)")
            go(dve.tensor_tensor_scan(flat(2), flat(1), flat(0), 0.0, ALU.mult, ALU.add))
            go(dve.tensor_copy(wl[:, 2 * MAXB:2 * MAXB + 1], flat(2)[:, JX * E - 1:JX * E]))
            go(dve.tensor_tensor(blk[:, 2], blk[:, 2], blk[:, 0], ALU.mult))
            go(dve.tensor_tensor(blk[:, 1], C_(2), ioj[:, :, :], ALU.add))
            go(dve.tensor_scalar(blk[:, 3], C_(1), -float(CAP), None, ALU.add))
            go(dve.tensor_tensor(blk[:, 1], blk[:, 1], blk[:, 3], ALU.min))
            for w in range(MAXB):
                go(dve.tensor_scalar(blk[:, 0], blk[:, 2], float(w + 1), None, ALU.is_equal))
                go(dve.tensor_tensor(blk[:, 3], blk[:, 0], ioe[:, :, :], ALU.mult))
                go(dve.tensor_reduce(wl[:, w:w + 1], flat(3), AX.X, ALU.add))
                go(dve.tensor_tensor(blk[:, 3], blk[:, 0], blk[:, 1], ALU.mult))
                go(dve.tensor_reduce(wl[:, MAXB + w:MAXB + w + 1], flat(3), AX.X, ALU.add))
            moved(dve, ("xs", 2 * KD - 1))
            dve.memset(xs[:, :, PAIRS:SLOTS], 0.0)
            dve.tensor_copy(wli[:, :], wl[:, :]).then_inc(offs_ready, 1)
            tmp = ys_tmp
            for i in range(3):
                dve.tensor_scalar(gsel[:, i, :], ios[:, :], r1[:, i, 10:11], r1[:, i, 8:9], ALU.is_equal, ALU.mult)
                last = dve.tensor_scalar(tmp[:, i, :], ios[:, :], r1[:, i, 11:12], r1[:, i, 9:10], ALU.is_equal, ALU.mult)
            own[0] += 1
            last.then_inc(dve_step, 1)
            dve.wait_ge(dve_step, own[0])
            dve.tensor_tensor(gsel[:, :, :], gsel[:, :, :], tmp[:, :, :], ALU.add).then_inc(gw_ready, 1)

            def stage_x(off, s):
                return dve.tensor_copy(xb[:, s, :, :], xs[:, :, bass.ds(off, CAP)])

            def half_h(s):
                return dve.tensor_tensor(sg[:, s, :], sg[:, s, :], bank[s][:, 0:P], ALU.mult)

            def full_h(s):
                return dve.tensor_tensor(sg[:, s, :], sg[:, s, :], bank[s][:, P:2 * P], ALU.mult)

            def take_h(s):
                return dve.tensor_copy(eh[:, s, :], b_ht[:, 0:P])

            def turn(e, s, ahead=True):
                first = not isinstance(e, int)
                if ahead:
                    off = dve.value_load(offi[0:1, bass.ds(e + 1, 1)], min_val=0, max_val=PAIRS)
                    if first or e >= 2:
                        dve.wait_ge(gu_full, e - 1)
                    stage_x(off, slot(s + 1)).then_inc(xb_ready, 1)
                dve.wait_ge(esig_ready, e + 1)
                half_h(s).then_inc(est, 1)
                dve.wait_ge(est, e + 1)
                full_h(s).then_inc(eh_ready, 1)
                if first or e >= RING:
                    dve.wait_ge(y_full, e + (1 - RING))
                dve.wait_ge(ht_full, e + 1)
                take_h(s).then_inc(ht_ready, 1)

            dve.wait_ge(offs_ready, 1)
            moved(dve, ("xs", 2 * KD - 1))
            off = dve.value_load(offi[0:1, 0:1], min_val=0, max_val=PAIRS)
            stage_x(off, 0).then_inc(xb_ready, 1)
            for e in range(FIRST):
                turn(e, slot(e))
            with dve.Fori(0, (E - FIRST) // RING - 1) as i:
                for j in range(RING):
                    turn(3 * i + (FIRST + j), slot(FIRST + j))
            for e in range(E - RING, E):
                turn(e, slot(e), ahead=e + 1 < E)
            extra = dve.value_load(wli[0:1, 2 * MAXB:2 * MAXB + 1], min_val=0, max_val=MAXB)
            dve.wait_ge(ys_ready, E)
            with dve.If(extra > 0):
                with dve.Fori(0, extra) as i:
                    off = dve.value_load(wli[0:1, bass.ds(i + MAXB, 1)], min_val=0, max_val=PAIRS)
                    stage_x(off, 0).then_inc(xb_xb, 1)
                    dve.wait_ge(xb_sig, i + 1)
                    half_h(0).then_inc(est, 1)
                    dve.wait_ge(est, i + (E + 1))
                    full_h(0).then_inc(xb_h, 1)
                    dve.wait_ge(xb_htf, i + 1)
                    take_h(0).then_inc(xb_ht, 1)

            for k in range(KD):
                f = ("mo", k)
                filled(dve, f)
                dve.tensor_tensor(xT[:, k, :], wide(f), xT[:, k, :], ALU.add).then_inc(empty, 1)
            norm_scale(2, R_PLE)
            for k in range(KD):
                moved(dve, ("pg", k))
                go(dve.tensor_tensor(sqm[:, k, :], sqm[:, k, :], ppr[:, k, :], ALU.mult))
                last = dve.tensor_tensor(xT[:, k, :], xT[:, k, :], sqm[:, k, :], ALU.add)
            last.then_inc(x4_ready, 1)
            dve.wait_ge(x4_ready, 1)
            norm_scale(3, R_FIN)


_INS = ['x_prompt', 'x_sample', 'p_prompt', 'p_sample', 'state_mlstm_C', 'state_mlstm_n', 'state_mlstm_m',
        'state_mlstm_conv', 'state_sconv', 'g_mix', 'w_in', 'w_mconv', 'w_q', 'w_k', 'b_i', 'b_f', 'g_head', 'w_a',
        'w_sconv', 'w_sout', 'w_o', 'g_ffn', 'w_rg', 'b_rg', 'w_re', 'b_re', 'w_gate', 'w_up', 'w_down',
        'g_ple', 'w_ple_gate', 'w_ple_proj', 'g_final']
_OUTS = [(1, TP, D), (NB, TS, D), (1, 1, H, DH, DH), (1, 1, H, DH), (1, 1, H), (1, 1, 3, D), (1, 1, 2, D),
         (1, NB, H, DH, DH), (1, NB, H, DH), (1, NB, H), (1, NB, 3, D), (1, NB, 2, D)]


def kernel(**inputs):
    import concourse.bacc as _bacc
    from concourse.bass_utils import run_bass_kernel_spmd as _run

    nc = _bacc.Bacc("TRN2", target_bir_lowering=False, num_devices=1)
    arrays, ins = {}, {}
    for name in _INS:
        a = np.ascontiguousarray(inputs[name])
        arrays[f"in_{name}_dram"] = a
        ins[name] = nc.dram_tensor(f"in_{name}_dram", a.shape, F32, kind="ExternalInput").ap()
    outs = [nc.dram_tensor(f"out_{i}_dram", shape, F32, kind="ExternalOutput").ap() for i, shape in enumerate(_OUTS)]
    hybrid_step(nc, ins, outs)
    r = _run(nc, [arrays], core_ids=[0])
    return tuple(r.results[0][f"out_{i}_dram"] for i in range(len(_OUTS)))
```

```python
from contextlib import ExitStack

import numpy as np
import concourse.bass as bass
from concourse import mybir

F32 = mybir.dt.float32
F32R = mybir.dt.float32r
I32 = mybir.dt.int32
ALU = mybir.AluOpType
ACT = mybir.ActivationFunctionType
AX = mybir.AxisListType

P = 128
D = 1024
KD = D // P
TP, NB, TS = 256, 8, 8
NS = NB * TS
T = TP + NS
TILES = [(0, 128), (128, 128), (256, 64)]
H, DH = 4, 256
E, G, EG = 32, 4, 8
FE = 256
PLE = 256
EPS = 1e-6
NEG = -1e30
CAP = 64
WIDE = 96
PAIRS = 2 * T
SLOTS = PAIRS + CAP
ST = PAIRS // P
JX = -(-T // CAP) - 1
MAXB = PAIRS // (CAP + 1)
RING = 3
FIRST = RING + E % RING
WR = 3
QC = D // 4
ACC = 3
XM, VV, OO, IF, SB, SC, SX, GA, GB = 0, 1024, 2048, 3072, 3080, 4104, 5128, 6152, 7176
R_MIX, R_HEAD, R_FFN, R_PLE, R_FIN, R_MCW, R_SCW, R_MCH, R_SCH, R_ALL = 0, 1, 2, 3, 4, 5, 9, 12, 36, 52
PX, SXX = TP + 3, TS + 3
PU, SU = TP + 2, TS + 2
XE, UE = PX + NB * SXX, PU + NB * SU


def slot(e):
    return e % RING


def hybrid_step(nc, I, O):
    with ExitStack() as ctx:
        plan = {}
        base = [nc.sbuf_base + (-nc.sbuf_base) % 64]

        def at(name, shape, offset, dt=F32):
            plan[name] = (offset, offset + 4 * int(np.prod(shape[1:])))
            return nc.alloc_sbuf_tensor_at(name, shape, dt, offset=offset)

        def new(name, shape, dt=F32):
            t = at(name, shape, base[0], dt)
            base[0] = plan[name][1] + (-plan[name][1]) % 64
            return t

        def sem(name):
            return ctx.enter_context(nc.semaphore(name))

        ident = new("ident", [P, P])
        ones = new("ones", [P, P])
        cols = new("cols", [P, KD, R_ALL])
        eps = new("eps", [P, 1])
        xT = new("xT", [P, KD, T])
        hT = new("hT", [P, KD, 3 * P])
        h_hi = at("h_hi", [P, KD, 3 * P], plan["hT"][0], F32R)
        pT = new("pT", [P, 2, T])
        root = new("root", [P, T])
        rstd = new("rstd", [P, T])
        wring = new("wring", [P, WR, KD, QC])
        w_lo = at("w_lo", [P, WR, KD, QC], plan["wring"][0], F32R)
        w_hi = new("w_hi", [P, 2, KD, P], F32R)
        wr36 = new("wr36", [P, KD, G + E])
        wif = new("wif", [P, KD, 2 * H])
        wif_lo = at("wif_lo", [P, KD, 2 * H], plan["wif"][0], F32R)
        brow = new("brow", [1, G + E])
        brow_all = new("brow_all", [P, G + E])
        rootr = at("rootr", [1, 3 * P], plan["root"][0])
        rc = new("rc", [P, 3])
        idle = at("idle", [P, 1], plan["rc"][0] + 32)
        phase = base[0]

        vn = new("vn", [P, 3, D])
        kn = new("kn", [P, 2, 3, DH])
        qT = new("qT", [P, 2, 2, T])
        kT = new("kT", [P, 2, 2, T])
        h_first = new("h_first", [P, KD, T])
        h_lo = at("h_lo", [P, KD, T], plan["h_first"][0], F32R)
        s1 = new("s1", [P, KD, T])
        xme = new("xme", [P, KD, XE])
        cxe = at("cxe", [P, KD, UE], plan["xme"][0])
        cv_all = new("cv", [P, KD, XE])
        u_all = at("uT", [P, KD, UE], plan["cv"][0])
        wv_hi = at("wv_hi", [P, KD, QC], plan["s1"][0], F32R)
        s1_lo = at("s1_lo", [P, KD, T], plan["s1"][0], F32R)
        s1_hi = at("s1_hi", [P, KD, T], plan["cv"][0], F32R)
        cv, uT = cv_all[:, :, 0:XE - 3], u_all[:, :, 0:UE - 2]
        xq = new("xq", [P, KD, T])
        s4 = at("s4", [P, KD, T], plan["xme"][0])
        s4_lo = at("s4_lo", [P, KD, T], plan["xme"][0], F32R)
        s4_hi = at("s4_hi", [P, KD, T], plan["h_first"][0], F32R)
        cbuf = new("cbuf", [P, NB, 2, DH])
        oT_lo = at("oT_lo", [P, KD, T], plan["cbuf"][0], F32R)
        oT_hi = at("oT_hi", [P, KD, T], plan["cv"][0], F32R)
        oT = at("oT", [P, KD, T], plan["cbuf"][0])
        xnat = at("xnat", [P, 3, D], plan["cbuf"][0])
        sqx = at("sqx", [P, KD, T], plan["s1"][0])
        rowsn = at("rowsn", [R_ALL, D], plan["kn"][0])
        pnat = at("pnat", [P, 3, PLE], plan["kn"][0] + 4096)
        nnat = at("nnat", [NB * H, DH], plan["kn"][0] + 8192)
        wqk = new("wqk", [P, 2, 2, DH])
        rows = new("rows", [H, 8, T])
        m0r = new("m0r", [H, NB])
        mo = new("mo", [H, NB + 1])
        bif = new("bif", [H, 2])
        selh = new("selh", [H, H, P])
        mask = new("mask", [P, 448])
        pt = new("pt", [P, 384 + WIDE])
        awT = new("awT", [P, 2, 3, H])
        oneb = new("oneb", [NS, NB])
        wsel = new("wsel", [NS, H, NB])
        wint = new("wint", [P, NS])
        qw = at("qw", [P, 2, NS], plan["root"][0])
        qz = new("qz", [P, 2, NB, WIDE])
        onet = new("onet", [P, NB, NS])
        qn = at("qn", [P, 2, NS], plan["rows"][0] + 4 * 4 * T + 4 * T + 2048)
        wkm = new("wkm", [NS, NB, DH])
        wkp = new("wkp", [P, 2, DH])
        cpn = at("cpn", [P, 2, DH], plan["rows"][0] + 4 * 4 * T + 4 * T)
        nT = new("nT", [P, 2, NB * H])
        nall = new("nall", [33, H, DH])
        nrow, npr = nall[0:NB], nall[32:33]
        decT = new("decT", [NB, H])
        den = at("den", [P, T], plan["rows"][0] + 4 * 4 * T)
        ssT = new("ssT", [P, H, T])
        tailc = new("tailc", [P, KD, 27])
        tailu = at("tailu", [P, KD, 18], plan["root"][0] + 512)
        wif_hi = at("wif_hi", [P, KD, 2 * H], plan["wv_hi"][1], F32R)
        hsq = at("hsq", [P, 2, T], plan["rows"][0])
        assert plan["qn"][1] <= plan["rows"][0] + 7 * 4 * T and plan["tailu"][1] <= plan["rstd"][1]
        mixer_end = base[0]
        assert mixer_end <= nc.sbuf_usable_end, mixer_end
        tailn = at("tailn", [27, D], plan["s1"][0])
        tails = at("tails", [18, D], plan["cbuf"][0] + 4 * KD * T)

        base[0] = phase
        egu = [None] * RING
        ed = [None] * RING
        for s in range(RING):
            egu[s] = new(f"egu{s}", [P, KD, 2, FE])
            ed[s] = new(f"ed{s}", [P, 2, D])
        xs = new("xs", [P, KD, SLOTS])
        ys = new("ys", [P, KD, SLOTS])
        assert plan["ys"][1] - plan["ys"][0] >= 12288 + 4 * 3 * PAIRS
        hn = at("hn", [P, 3, D], plan["ys"][0])
        hn_lo = at("hn_lo", [P, 3, D], plan["ys"][0], F32R)
        hn_hi = at("hn_hi", [P, 3, D], plan["wring"][0], F32R)
        ppr = at("ppr", [P, KD, T], plan["hn_hi"][1])
        wpp = at("wpp", [P, 2, D], plan["ppr"][1])
        assert plan["wpp"][1] <= plan["w_hi"][1]
        sq1 = at("sq1", [P, KD, T], plan["xq"][0])
        pgw = [at("pgw0", [P, KD, 512], plan["egu2"][0]), at("pgw1", [P, KD, 512], plan["egu0"][0])]
        yn_hi = at("yn_hi", [P, ST, D], plan["ed0"][0], F32R)
        sqm = at("sqm", [P, KD, T], plan["yn_hi"][1])
        assert plan["sqm"][1] <= plan["egu2"][0] and plan["pgw1"][1] <= plan["ed0"][0]
        yn_lo = at("yn_lo", [P, ST, D], plan["xs"][0], F32R)
        x4n = at("x4n", [P, 3, D], plan["ys"][0])
        gsel = new("gsel", [P, 3, PAIRS], F32R)
        lgT = at("lgT", [G + E, 3 * P], plan["gsel"][0])
        gfin = at("gfin", [P, D], plan["gsel"][0])
        wcT = new("wcT", [P, ST, T], F32R)
        wslot = new("wslot", [P, ST])
        wlc = new("wlc", [MAXB, 3])
        xb = new("xb", [P, RING, KD, CAP])
        sg = new("sg", [P, RING, P])
        eh = new("eh", [P, RING, P])
        yb = new("yb", [P, 512])
        pgs = at("pgs", [P, 2, T], plan["sg"][0])
        assert plan["pgs"][1] <= plan["yb"][1]
        offi = new("offi", [1, E], I32)
        wli = new("wli", [1, 2 * MAXB + 1], I32)
        expert_end = base[0]
        base[0] = plan["xb"][0]
        lg = new("lg", [P, 3, G + E])
        r4 = new("r4", [P, 3, 4, G])
        r8 = new("r8", [P, 3, 8, EG])
        pick = new("pick", [P, 2, 3, E])
        m32 = new("m32", [P, 3, E])
        pos = new("pos", [P, 3, E])
        tri = new("tri", [P, P])
        io4 = new("io4", [P, G])
        io8 = new("io8", [P, EG])
        valid = new("valid", [P, 3])
        cnt = new("cnt", [P, 3, E])
        blk = new("blk", [MAXB, 4, JX, E])
        ioe = new("ioe", [MAXB, JX, E])
        ioj = new("ioj", [MAXB, JX, E])
        iow = new("iow", [MAXB, 1])
        assert base[0] <= expert_end, (base[0], expert_end)
        base[0] = expert_end
        ys_tmp = at("ys_tmp", [P, 3, PAIRS], plan["ys"][0] + 12288)
        ys_two = at("ys_two", [P, PAIRS], plan["ys"][0] + 12288 + 7680)
        ios = new("ios", [P, PAIRS])
        r1 = new("r1", [P, 3, 12])
        assert base[0] <= nc.sbuf_usable_end, base[0]

        bank = [ctx.enter_context(nc.psum_tensor(f"bank{i}", [P, 512], F32)) for i in range(8)]
        b_ht, b_y, b_yt = bank[3], bank[4], bank[5]
        b_gu = (bank[6], bank[7], bank[6])
        b_enm, b_s, b_bc, b_num = bank[3], bank[4], bank[5], (bank[6], bank[7])

        fills = [("x", k) for k in range(KD)] + [("rows",), ("nn",), ("pn", 0), ("pn", 1), ("ss", 0)]
        who = {("rows",): "dve", ("nn",): "dve"}

        def section(name, by, n=KD):
            for m in range(n):
                fills.append((name, m))
                who[(name, m)] = by

        def section_one(f, by):
            fills.append(f)
            who[f] = by

        section("xm", "act")
        section("if", "dve", 2)
        section("bb", "dve", 1)
        section("v", "act", 12)
        section("aw", "dve", 1)

        def qk_fills(h):
            fills.extend([("qk", h, n) for n in range(4)] + [("kn", h, n) for n in range(3)])

        def state_fills(h):
            for f in [("C", h, b) for b in range(NB)] + [("Cp", h), ("n", h)]:
                fills.append(f)
                who[f] = "act" if f[0] == "Cp" else "dve"

        MID = [("sc", "act"), ("sx", "dve"), ("sb", "dve"), ("gb", "act")]
        qk_fills(0)
        section("to", "act", 2)
        qk_fills(1)
        for h in range(H):
            section(*MID[h])
            state_fills(h)
            if h + 2 < H:
                qk_fills(h + 2)
        section("o", "act")
        section("tu", "act", 2)
        section("sout", "dve")
        section("ga", "act")
        section("a", "dve")
        section("wo", "dve")
        for f in (("hn", 0), ("hn", 1), ("lg", 0), ("hn", 2), ("hn", 3), ("hn", 4), ("hn", 5)):
            fills.append(f)
            who[f] = "dve" if f[0] == "lg" else "act"
        for f in [("pp", k) for k in range(ACC)] + [("rank", 0)] + [("pp", k) for k in range(ACC, KD)]:
            section_one(f, "dve" if f[0] == "rank" else "act")
        section("xs", "act", 2 * KD)
        section("ws", "dve", 1)
        section("wc", "act", ST)
        section("yn", "dve", 2 * ST)
        section("mo", "dve")
        for m in range(KD + 2):
            if m < KD:
                section_one(("pg", m), "dve")
            if m >= 2:
                section_one(("yo", m - 2), "act")
        section_one(("rf", 0), "dve")
        index = {f: n for n, f in enumerate(fills)}
        emptied = {}
        done = {"act": 0, "dve": 0}
        for f in fills:
            w = who.setdefault(f, "act")
            done[w] += 1
            emptied[f] = (w, done[w])

        acc_full = sem("acc_full")
        acc_empty = {"act": sem("acc_empty_act"), "dve": sem("acc_empty_dve")}

        def acc(f):
            return bank[index[f] % ACC]

        def refill(pe, f):
            if index[f] >= ACC:
                w, n = emptied[fills[index[f] - ACC]]
                pe.wait_ge(acc_empty[w], n)

        def moved(eng, f):
            w, n = emptied[f]
            eng.wait_ge(acc_empty[w], n)

        def filled(eng, f):
            eng.wait_ge(acc_full, index[f] + 1)

        order = ["xm", "v", "sc", "sx", "sb", "gb", "o", "sout", "ga", "a", "wo"]
        w_in = I["w_in"][0]
        source = {"xm": w_in[:, XM:XM + D], "v": w_in[:, VV:VV + D], "o": w_in[:, OO:OO + D],
                  "sb": w_in[:, SB:SB + D], "sc": w_in[:, SC:SC + D], "sx": w_in[:, SX:SX + D],
                  "ga": w_in[:, GA:GA + D], "gb": w_in[:, GB:GB + D], "a": I["w_a"][0],
                  "sout": I["w_sout"][0], "wo": I["w_o"][0]}
        quarters = [(s, j) for s in order for j in range(4)]
        w_landed = [sem(f"w_landed{i}") for i in range(WR)]
        whi_ready = sem("whi_ready"); wlo_ready = sem("wlo_ready")

        parts = [(s, m) for s in order for m in range(4 if s == "v" else KD)]

        def quarter_of(s, m):
            return quarters.index((s, m if s == "v" else m // 2))

        def last_fill(s, m):
            return (s, 3 * m + 2) if s == "v" else (s, m)

        def hi_part(s, m):
            if s == "v":
                return (w_hi[:, :, :, :].rearrange("p c k e -> p k c e") if m % 2 else
                        wv_hi[:, :, :].rearrange("p k (c e) -> p k c e", c=2))
            return w_hi[:, m % 2:m % 2 + 1, :, :].rearrange("p c k e -> p k c e")

        def part_of(ring, s, m):
            w = ring[:, quarter_of(s, m) % WR]
            return w if s == "v" else w[:, :, (m % 2) * P:(m % 2) * P + P]

        def hi_free(s, m):
            if s == "v":
                return {0: None, 1: ("xm", KD - 1), 2: last_fill("v", 0), 3: last_fill("v", 1)}[m]
            n = parts.index((s, m))
            return None if n < 2 else last_fill("v", 3) if parts[n - 2][0] == "v" else parts[n - 2]

        def later(s, m, by=2):
            n = parts.index((s, m)) + by
            return parts[n] if n < len(parts) else None

        in_x = sem("in_x"); in_rows = sem("in_rows"); in_small = sem("in_small")
        consts = sem("consts"); pool_step = sem("pool_step"); dve_step = sem("dve_step"); act_step = sem("act_step")
        cols_ready = sem("cols_ready"); sq_ready = sem("sq_ready")
        h_ready = sem("h_ready")
        conv_done = sem("conv_done"); sig_ready = sem("sig_ready"); xq_ready = sem("xq_ready")
        gate_step = sem("gate_step"); gate_act = sem("gate_act"); rows_ready = sem("rows_ready"); aw_ready = sem("aw_ready")
        wqk_landed = sem("wqk_landed")
        scores_full = sem("scores_full"); args_ready = sem("args_ready"); exps_ready = sem("exps_ready")
        probs_ready = sem("probs_ready"); c_landed = sem("c_landed"); c_updated = sem("c_updated"); c_stored = sem("c_stored")
        pv_full = sem("pv_full"); hm_ready = sem("hm_ready"); hsq_ready = sem("hsq_ready")
        ss_full = sem("ss_full"); ss_taken = sem("ss_taken"); wk_ready = sem("wk_ready")
        cp_stored = sem("cp_stored"); n_ready = sem("n_ready"); tails_ready = sem("tails_ready")
        stored = sem("stored")
        ya_ready = sem("ya_ready")
        hroot = sem("hroot"); m_ready = sem("m_ready")
        rt_exp = sem("rt_exp"); rt_arg = sem("rt_arg"); m32_ready = sem("m32_ready")
        gsel_ready = sem("gsel_ready"); gw_ready = sem("gw_ready")
        offs_ready = sem("offs_ready")
        gu_landed = [sem(f"gu_landed{s}") for s in range(RING)]
        d_landed = [sem(f"d_landed{s}") for s in range(RING)]
        xb_ready = sem("xb_ready"); ht_full = sem("ht_full"); ht_ready = sem("ht_ready"); yb_ready = sem("yb_ready"); yt_full = sem("yt_full")
        sq1_ready = sem("sq1_ready"); gx_ready = sem("gx_ready"); lg_full = sem("lg_full"); lgT_ready = sem("lgT_ready"); rc_ready = sem("rc_ready")
        hn_split = sem("hn_split"); yhi_ready = sem("yhi_ready"); pgw_landed = sem("pgw_landed")
        ss2_full = sem("ss2_full"); ss3_full = sem("ss3_full"); root2 = sem("root2"); pgs_ready = sem("pgs_ready")
        root3 = sem("root3"); gfin_landed = sem("gfin_landed"); y_rows = sem("y_rows"); x3_sq = sem("x3_sq"); x4_sq = sem("x4_sq")
        xb_xb = sem("xb_xb"); xb_htf = sem("xb_htf"); xb_ht = sem("xb_ht"); xb_yb = sem("xb_yb"); xb_yt = sem("xb_yt")
        gu_full = sem("gu_full"); esig_ready = sem("esig_ready"); eh_ready = sem("eh_ready")
        y_full = sem("y_full"); ys_ready = sem("ys_ready"); est = sem("est")
        xb_landed = sem("xb_landed"); xb_gu = sem("xb_gu"); xb_sig = sem("xb_sig"); xb_h = sem("xb_h")
        xb_y = sem("xb_y"); xb_done = sem("xb_done")
        wpp_landed = sem("wpp_landed")
        consts2 = sem("consts2"); out_stored = sem("out_stored"); experts_done = sem("experts_done")

        h_scaled = sem("h_scaled"); h_upper = sem("h_upper"); wif_split = sem("wif_split"); s1_split = sem("s1_split"); s1_high = sem("s1_high")
        oT_split = sem("oT_split"); s4_high = sem("s4_high"); s4_low = sem("s4_low")
        table_loaded = sem("table_loaded"); sq0_sum = sem("sq0_sum"); sq1_sum = sem("sq1_sum"); sq2_sum = sem("sq2_sum"); sq3_sum = sem("sq3_sum")
        hist_ready = sem("hist_ready"); tailn_stored = sem("tailn_stored"); x4_ready = sem("x4_ready")
        cbuf_rows = cbuf[:, :, :, :].rearrange("p b d e -> p b (d e)")
        cv_sample = lambda k: cv_all[:, k, PX:PX + NB * SXX].rearrange("p (b j) -> p b j", b=NB)[:, :, 0:TS]
        uT_sample = lambda k: u_all[:, k, PU:PU + NB * SU]

        def step(eng, signal, count):
            def go(ins):
                count[0] += 1
                ins.then_inc(signal, 1)
                eng.wait_ge(signal, count[0])
            return go

        ctx.enter_context(nc.allow_non_contiguous_dma(reason="gate biases and m: 4 to 32 elements"))
        block = ctx.enter_context(nc.Block())

        @block.sync
        def _(sp):
            for i, (t0, n) in enumerate(TILES):
                src = I["x_prompt"][0, t0:t0 + n] if i < 2 else I["x_sample"].rearrange("b t d -> (b t) d")
                sp.dma_start(xnat[0:n, i, :], src).then_inc(in_x, 16)
            one = lambda a: a.rearrange("(a d) -> a d", a=1)
            for r, src in ((R_MIX, I["g_mix"]), (R_HEAD, I["g_head"].rearrange("a h d -> a (h d)")), (R_FFN, I["g_ffn"]),
                           (R_PLE, I["g_ple"]), (R_FIN, one(I["g_final"])), (R_MCW, I["w_mconv"][0]), (R_SCW, I["w_sconv"][0]),
                           (R_MCH, I["state_mlstm_conv"][0].rearrange("b j d -> (b j) d")),
                           (R_SCH, I["state_sconv"][0].rearrange("b j d -> (b j) d"))):
                sp.dma_start(rowsn[r:r + src.shape[0], :], src).then_inc(in_rows, 16)
            for i, (t0, n) in enumerate(TILES):
                src = I["p_prompt"][0, 0, t0:t0 + n] if i < 2 else I["p_sample"][0].rearrange("b t d -> (b t) d")
                sp.dma_start(pnat[0:n, i, :], src).then_inc(in_rows, 16)
            sp.dma_start(nrow[:, :, :], I["state_mlstm_n"][0]).then_inc(in_small, 16)
            sp.dma_start(nnat[:, :], I["state_mlstm_n"][0].rearrange("b h d -> (b h) d")).then_inc(in_rows, 16)

            def quarter(n):
                s, j = quarters[n]
                if n >= WR:
                    before, i = quarters[n - WR]
                    sp.wait_ge(acc_full, index[last_fill(before, i if before == "v" else 2 * i + 1)] + 1)
                sp.dma_start(wring[:, n % WR], source[s][:, QC * j:QC * j + QC].rearrange("(k p) c -> p k c", p=P))\
                    .then_inc(w_landed[n % WR], 16)

            for n in range(WR):
                quarter(n)
            sp.dma_start(wif[:, :, :], w_in[:, IF:IF + 2 * H].rearrange("(k p) c -> p k c", p=P)).then_inc(in_small, 16)
            sp.dma_start(bif[:, 0:1], I["b_i"].rearrange("a h -> h a")).then_inc(in_small, 16)
            sp.dma_start(bif[:, 1:2], I["b_f"].rearrange("a h -> h a")).then_inc(in_small, 16)
            sp.dma_start(m0r[:, :], I["state_mlstm_m"][0].rearrange("b h -> h b")).then_inc(in_small, 16)
            sp.dma_start(brow[:, 0:G], I["b_rg"]).then_inc(in_small, 16)
            sp.dma_start(brow[:, G:G + E], I["b_re"]).then_inc(in_small, 16)
            sp.dma_start(wr36[:, :, 0:G], I["w_rg"][0].rearrange("(k p) c -> p k c", p=P)).then_inc(in_small, 16)
            sp.dma_start(wr36[:, :, G:G + E], I["w_re"][0].rearrange("(k p) c -> p k c", p=P)).then_inc(in_small, 16)
            for n in range(WR, len(quarters)):
                quarter(n)
            w_g, w_u, w_d = I["w_gate"][0], I["w_up"][0], I["w_down"][0]

            row = lambda w, e: w[e:e + 1] if isinstance(e, int) else w[bass.ds(e, 1)]

            def load_gu(e, s, signal):
                for j, w in enumerate((w_g, w_u)):
                    sp.dma_start(egu[s][:, :, j, :], row(w, e).rearrange("a (k p) c -> p (a k) c", p=P)).then_inc(signal, 16)

            def load_d(e, s, signal):
                sp.dma_start(ed[s][:, :, :], row(w_d, e).rearrange("a (k p) c -> p (a k) c", p=P)).then_inc(signal, 16)

            moved(sp, ("wo", KD - 1))
            sp.wait_ge(stored, 16 * 6)
            sp.wait_ge(tailn_stored, 32)
            sp.wait_ge(c_stored, 16 * H)
            sp.wait_ge(cp_stored, 16 * H)
            sp.wait_ge(lg_full, 1)
            sp.dma_start(wpp[:, :, :], I["w_ple_proj"][0].rearrange("(k p) c -> p k c", p=P)).then_inc(wpp_landed, 16)
            for e in range(RING):
                load_gu(e, slot(e), gu_landed[slot(e)])
                load_d(e, slot(e), d_landed[slot(e)])
            sp.wait_ge(gu_full, 1)
            load_gu(RING, 0, gu_landed[0])
            with sp.Fori(0, (E - FIRST) // RING) as i:
                for j in range(RING):
                    s = slot(j + 1)
                    sp.wait_ge(gu_full, 3 * i + (j + 2))
                    load_gu(3 * i + (RING + j + 1), s, gu_landed[s])
                    sp.wait_ge(y_full, 3 * i + (j + 1))
                    load_d(3 * i + (RING + j), slot(j), d_landed[slot(j)])
            sp.wait_ge(gu_full, E - RING)
            load_gu(E - 1, slot(E - 1), gu_landed[slot(E - 1)])
            for e in (E - 2, E - 1):
                sp.wait_ge(y_full, e + 1 - RING)
                load_d(e, slot(e), d_landed[slot(e)])
            w_pg = I["w_ple_gate"][0]
            for j in range(2):
                sp.wait_ge(gu_full, E - 2 + j)
                sp.dma_start(pgw[j][:, :, :], w_pg[:, 512 * j:512 * j + 512].rearrange("(k p) c -> p k c", p=P)).then_inc(pgw_landed, 16)
            moved(sp, ("wc", ST - 1))
            sp.dma_start(gfin[:, :], one(I["g_final"]).to_broadcast([P, D])).then_inc(gfin_landed, 16)
            sp.wait_ge(offs_ready, 2)
            extra = sp.value_load(wli[0:1, 2 * MAXB:2 * MAXB + 1], min_val=0, max_val=MAXB)
            sp.wait_ge(ys_ready, E)
            with sp.If(extra > 0):
                with sp.Fori(0, extra) as i:
                    sp.wait_ge(xb_done, i + 1)
                    e = sp.value_load(wli[0:1, bass.ds(i, 1)], min_val=0, max_val=E - 1)
                    load_gu(e, 1, xb_landed)
                    load_d(e, 1, xb_landed)

            for i, (t0, n) in enumerate(TILES):
                sp.wait_ge(y_rows, i + 1)
                dst = O[0][0, t0:t0 + n] if i < 2 else O[1].rearrange("b t d -> (b t) d")
                sp.dma_start(dst, x4n[0:n, i, :]).then_inc(out_stored, 16)
            sp.wait_ge(out_stored, 16 * 3)

        @block.tensor
        def _(pe):
            def fill(f, mms):
                refill(pe, f)
                mms(acc(f)).then_inc(acc_full, 1)

            def linear(name, hi, lo, chunks=None, tiles=range(KD), after=None):
                for m in tiles:
                    pe.wait_ge(wlo_ready, parts.index((name, m)) + 1)
                    w, wl = hi_part(name, m), part_of(w_lo, name, m)
                    def mms(bk):
                        for k in range(KD):
                            if chunks and m == 0:
                                pe.wait_ge(chunks, k + 1)
                            pe.matmul(bk[:, 0:T], w[:, k, 0, :], hi[:, k, 0:T], start=(k == 0), stop=False)
                            pe.matmul(bk[:, 0:T], w[:, k, 0, :], lo[:, k, 0:T], start=False, stop=False)
                            last = pe.matmul(bk[:, 0:T], wl[:, k, :], hi[:, k, 0:T], start=False, stop=(k == KD - 1))
                        return last
                    fill((name, m), mms)
                    if after:
                        after(m)

            pe.wait_ge(consts, 1)
            pe.wait_ge(in_x, 16 * 3)
            for k in range(KD):
                def mms(bk):
                    for i, (t0, n) in enumerate(TILES):
                        last = pe.transpose(bk[:, t0:t0 + n], xnat[0:n, i, k * P:k * P + P], ident[0:n, 0:n])
                    return last
                fill(("x", k), mms)
            pe.wait_ge(in_rows, 16 * 13)

            def mms(bk):
                for k in range(KD):
                    last = pe.transpose(bk[:, k * R_ALL:(k + 1) * R_ALL], rowsn[:, k * P:k * P + P], ident[0:R_ALL, 0:R_ALL])
                return last
            fill(("rows",), mms)

            def mms(bk):
                for c in range(2):
                    last = pe.transpose(bk[:, c * 32:c * 32 + 32], nnat[:, c:DH:2], ident[0:32, 0:32])
                return last
            fill(("nn",), mms)
            for c in range(2):
                def mms(bk):
                    for i, (t0, n) in enumerate(TILES):
                        last = pe.transpose(bk[:, t0:t0 + n], pnat[0:n, i, c * P:c * P + P], ident[0:n, 0:n])
                    return last
                fill(("pn", c), mms)

            def sum_squares(bk, sq, summed, ready):
                pe.wait_ge(summed, 1)
                pe.matmul(bk[:, 0:T], ones[:, :], sq[:, 0, :], start=True, stop=False)
                pe.wait_ge(*ready)
                return pe.matmul(bk[:, 0:T], ones[:, :], sq[:, KD - 1, :], start=False, stop=True)

            pe.wait_ge(consts, 2)
            fill(("ss", 0), lambda bk: sum_squares(bk, sqx, sq0_sum, (sq_ready, KD)))

            linear("xm", h_hi, h_lo, h_ready)
            pe.wait_ge(in_small, 16 * 9)
            pe.wait_ge(wif_split, 2)
            for g in range(2):
                def mms(bk):
                    c = slice(g * H, g * H + H)
                    for k in range(KD):
                        pe.matmul(bk[0:H, 0:T], wif_hi[:, k, c], h_hi[:, k, 0:T], start=(k == 0), stop=False)
                        pe.matmul(bk[0:H, 0:T], wif_hi[:, k, c], h_lo[:, k, 0:T], start=False, stop=False)
                        last = pe.matmul(bk[0:H, 0:T], wif_lo[:, k, c], h_hi[:, k, 0:T], start=False, stop=(k == KD - 1))
                    return last
                fill(("if", g), mms)
            fill(("bb", 0), lambda bk: pe.matmul(bk[:, 0:G + E], ones[0:1, :], brow[:, :], start=True, stop=True))
            for j in range(4):
                pe.wait_ge(wlo_ready, parts.index(("v", j)) + 1)
                w, wl = hi_part("v", j), part_of(w_lo, "v", j)
                for i, (t0, n) in enumerate(TILES):
                    def mms(bk):
                        for k in range(KD):
                            pe.matmul(bk[0:n, 0:QC], h_hi[:, k, t0:t0 + n], w[:, k, :, :], start=(k == 0), stop=False)
                            pe.matmul(bk[0:n, 0:QC], h_hi[:, k, t0:t0 + n], wl[:, k, :], start=False, stop=False)
                            last = pe.matmul(bk[0:n, 0:QC], h_lo[:, k, t0:t0 + n], w[:, k, :, :], start=False, stop=(k == KD - 1))
                        return last
                    fill(("v", 3 * j + i), mms)
            pe.wait_ge(rows_ready, 2)
            def mms(bk):
                for r, row in enumerate((0, 1)):
                    for i, (t0, n) in enumerate(TILES):
                        c = (3 * r + i) * H
                        pe.transpose(bk[0:n, c:c + H], rows[:, row, t0:t0 + n], ident[0:H, 0:H])
                return pe.transpose(bk[0:NB, 6 * H:7 * H], rows[:, 3, TS - 1:NS:TS], ident[0:H, 0:H])
            fill(("aw", 0), mms)

            def qk(h):
                pe.wait_ge(wqk_landed, 32 * (h + 1))
                if h == 0:
                    pe.wait_ge(xq_ready, 1)
                for n in range(4):
                    r, c = divmod(n, 2)
                    def mms(bk):
                        for d in range(2):
                            last = pe.matmul(bk[:, 0:T], wqk[:, r, d, c:DH:2], xq[:, 2 * h + d, :], start=(d == 0), stop=(d == 1))
                        return last
                    fill(("qk", h, n), mms)
                for i, (t0, n) in enumerate(TILES):
                    def mms(bk):
                        for d in range(2):
                            last = pe.matmul(bk[0:n, 0:DH], xq[:, 2 * h + d, t0:t0 + n], wqk[:, 1, d, :], start=(d == 0), stop=(d == 1))
                        return last
                    fill(("kn", h, i), mms)

            def scores(h):
                p = h % 2
                moved(pe, ("qk", h, 3))
                if h == 0:
                    pe.wait_ge(rows_ready, 2)
                    pe.wait_ge(consts, 4)
                else:
                    pe.wait_ge(hm_ready, h)
                for (o, n, s0, sn, t0) in ((0, 256, 0, P, 0), (256, P, P, P, P), (384, NS, TP, NS, TP)):
                    for c in range(2):
                        last = pe.matmul(b_s[0:sn, o:o + n], kT[:, p, c, s0:s0 + sn], qT[:, p, c, t0:t0 + n], start=(c == 0), stop=(c == 1))
                pe.matmul(b_bc[:, 0:T], selh[:, h, :], rows[:, 2, :], start=True, stop=True)
                pe.matmul(b_bc[:, T:T + NS], selh[:, h, :], rows[:, 3, 0:NS], start=True, stop=True)
                if h:
                    pe.wait_ge(ss_taken, h)
                pe.matmul(b_enm[:, 0:T], selh[:, h, :], rows[:, 7, :], start=True, stop=True).then_inc(scores_full, 1)

            def pv(h):
                pe.wait_ge(probs_ready, h + 1)
                moved(pe, ("v", 11))
                pe.wait_ge(c_landed, 16 * (h + 1))
                for c in range(2):
                    e0 = h * DH + c * P
                    bk = b_num[c]
                    pe.matmul(bk[:, 0:256], vn[:, 0, e0:e0 + P], pt[:, 0:256], start=True, stop=False, skip_group_check=True)
                    pe.matmul(bk[:, P:256], vn[:, 1, e0:e0 + P], pt[:, 256:384], start=False, stop=False, skip_group_check=True)
                    pe.matmul(bk[:, TP:TP + WIDE], vn[0:NS, 2, e0:e0 + P], pt[0:NS, 384:384 + WIDE], start=False, stop=False, skip_group_check=True)
                    for b in range(NB):
                        for d in range(2):
                            pe.matmul(bk[:, TP:TP + WIDE], cbuf[:, b, d, c * P:c * P + P], qz[:, d, b, :],
                                      start=False, stop=(b == NB - 1 and d == 1), skip_group_check=True)
                pe.matmul(b_s[:, 0:256], ones[:, :], pt[:, 0:256], start=True, stop=False, skip_group_check=True)
                pe.matmul(b_s[:, P:256], ones[:, :], pt[:, 256:384], start=False, stop=False, skip_group_check=True)
                pe.matmul(b_s[:, TP:T], ones[0:NS, :], pt[0:NS, 384:448], start=False, stop=False, skip_group_check=True)
                for d in range(2):
                    last = pe.matmul(b_s[:, TP:T], ones[:, :], qn[:, d, :], start=False, stop=(d == 1), skip_group_check=True)
                last.then_inc(pv_full, 1)

            def states(h):
                pe.wait_ge(wk_ready, h + 1)
                for b in range(NB):
                    def mms(bk):
                        for d in range(2):
                            last = pe.matmul(bk[:, d * DH:(d + 1) * DH], wkm[:, b, d:DH:2], vn[0:NS, 2, h * DH:(h + 1) * DH], start=True, stop=True)
                        return last
                    fill(("C", h, b), mms)
                def mms(bk):
                    for d in range(2):
                        for i in range(2):
                            last = pe.matmul(bk[:, d * DH:(d + 1) * DH], wkp[:, i, d:DH:2], vn[:, i, h * DH:(h + 1) * DH], start=(i == 0), stop=(i == 1))
                    return last
                fill(("Cp", h), mms)
                def mms(bk):
                    pe.matmul(bk[0:NB, 0:DH], wsel[:, h, :], kn[0:NS, h % 2, 2, :], start=True, stop=True)
                    for i in range(2):
                        last = pe.matmul(bk[32:33, DH:2 * DH], awT[:, 1, i, h:h + 1], kn[:, h % 2, i, :], start=(i == 0), stop=(i == 1))
                    return last
                fill(("n", h), mms)

            def head_sums(h):
                pe.wait_ge(hsq_ready, h + 1)
                for c in range(2):
                    last = pe.matmul(b_enm[:, 0:T], ones[:, :], hsq[:, c, :], start=(c == 0), stop=(c == 1))
                last.then_inc(ss_full, 1)

            qk(0)
            for j in range(2):
                if j == 0:
                    pe.wait_ge(tails_ready, 1)
                def mms(bk):
                    for k in range(4):
                        last = pe.transpose(bk[0:27, k * P:k * P + P], tailc[:, 4 * j + k, :], ident[:, :])
                    return last
                fill(("to", j), mms)
            scores(0)
            qk(1)
            for h in range(H):
                linear(MID[h][0], h_hi, h_lo, tiles=range(KD - 1))
                pv(h)
                linear(MID[h][0], h_hi, h_lo, tiles=(KD - 1,))
                states(h)
                head_sums(h)
                if h + 1 < H:
                    scores(h + 1)
                if h + 2 < H:
                    qk(h + 2)
            linear("o", h_hi, h_lo)
            for j in range(2):
                if j == 0:
                    pe.wait_ge(tails_ready, 2)
                def mms(bk):
                    for k in range(4):
                        last = pe.transpose(bk[0:18, k * P:k * P + P], tailu[:, 4 * j + k, :], ident[:, :])
                    return last
                fill(("tu", j), mms)
            pe.wait_ge(s1_split, 2)
            linear("sout", s1_hi, s1_lo)
            linear("ga", h_hi, h_lo)
            pe.wait_ge(oT_split, 2)
            linear("a", oT_hi, oT_lo)

            def logits(k):
                pe.wait_ge(gx_ready, k + 1)
                pe.matmul(b_s[0:G + E, 0:T], wr36[:, k, :], hT[:, k, 0:T], start=(k == 0), stop=(k == KD - 1))

            linear("wo", s4_hi, s4_lo, s4_low, after=lambda m: logits(m - 2) if m >= 2 else None)
            logits(KD - 2)
            logits(KD - 1)

            def turn_tokens(n):
                i, j = divmod(n, 2)
                def mms(bk):
                    for k in range(4):
                        last = pe.transpose(bk[:, k * P:k * P + P], hT[:, 4 * j + k, i * P:i * P + P], ident[:, :])
                    return last
                fill(("hn", n), mms)

            turn_tokens(0)
            sum_squares(b_enm, sq1, sq1_sum, (sq1_ready, KD)).then_inc(lg_full, 1)
            turn_tokens(1)
            pe.wait_ge(lgT_ready, 1)
            def mms(bk):
                for i in range(3):
                    pe.transpose(bk[:, i * 36:i * 36 + 36], lgT[:, i * P:i * P + P], ident[0:G + E, 0:G + E])
                for i in range(3):
                    last = pe.transpose(bk[:, 108 + i:109 + i], rootr[:, i * P:i * P + P], ident[0:1, 0:1])
                return last
            fill(("lg", 0), mms)
            for n in range(2, 6):
                turn_tokens(n)
            def embeddings(ks):
                for k in ks:
                    def mms(bk):
                        for c in range(2):
                            last = pe.matmul(bk[:, 0:T], wpp[:, c, k * P:k * P + P], pT[:, c, :], start=(c == 0), stop=(c == 1))
                        return last
                    fill(("pp", k), mms)

            pe.wait_ge(wpp_landed, 16)
            embeddings(range(ACC))
            pe.wait_ge(m32_ready, 1)
            def mms(bk):
                for i in range(3):
                    for q in range(i):
                        pe.matmul(bk[:, i * E:(i + 1) * E], ones[:, :], m32[:, q, :], start=(q == 0), stop=False)
                    pe.matmul(bk[:, i * E:(i + 1) * E], tri[:, :], m32[:, i, :], start=(i == 0), stop=True)
                for i in range(3):
                    last = pe.matmul(bk[:, 3 * E:4 * E], ones[:, :], m32[:, i, :], start=(i == 0), stop=(i == 2))
                return last
            fill(("rank", 0), mms)
            embeddings(range(ACC, KD))
            def gather(j):
                for k in range(KD):
                    def mms(bk):
                        for i in range(3):
                            for q, part in enumerate((hn_hi, hn_lo)):
                                last = pe.matmul(bk[:, 0:T], part[:, i, k * P:k * P + P], gsel[:, i, j * T:j * T + T],
                                                 start=(i == 0 and q == 0), stop=(i == 2 and q == 1))
                        return last
                    fill(("xs", KD * j + k), mms)

            def turn_selection(s):
                def mms(bk):
                    for i, (t0, n) in enumerate(TILES):
                        last = pe.transpose(bk[:, t0:t0 + n], gsel[0:n, i, s * P:s * P + P].bitcast(F32), ident[0:n, 0:n])
                    return last
                fill(("wc", s), mms)

            def slot_weights():
                pe.wait_ge(gw_ready, 1)
                def mms(bk):
                    for s in range(ST):
                        pe.matmul(bk[:, s:s + 1], ys_tmp[:, 0, s * P:s * P + P], ones[:, 0:1], start=True, stop=True)
                    for q in range(3):
                        last = pe.transpose(bk[0:1, P + q * MAXB:P + (q + 1) * MAXB], wlc[:, q:q + 1], ident[0:MAXB, 0:MAXB])
                    return last
                fill(("ws", 0), mms)

            def gate_up(s):
                for k in range(KD):
                    for j in range(2):
                        last = pe.matmul(b_gu[s][j * CAP:(j + 1) * CAP, 0:FE], xb[:, s, k, :], egu[s][:, k, :, j * P:(j + 1) * P],
                                         start=(k == 0), stop=(k == KD - 1))
                return last

            def turn_h(s):
                return pe.transpose(b_ht[:, 0:P], sg[:, s, :], ident[:, :])

            def down(s):
                for j in range(2):
                    for c in range(2):
                        last = pe.matmul(b_y[c * CAP:(c + 1) * CAP, :], eh[:, s, j * CAP:(j + 1) * CAP], ed[s][:, j, c * 512:(c + 1) * 512],
                                         start=(j == 0), stop=(j == 1))
                return last

            def turn_y():
                for q in range(4):
                    last = pe.transpose(b_yt[:, q * P:(q + 1) * P], yb[:, q * P:(q + 1) * P], ident[:, :])
                return last

            def turn(e, s, uses, gu=True):
                first = not isinstance(e, int)
                if gu and (first or e < E):
                    pe.wait_ge(gu_landed[s], 32 * uses)
                    pe.wait_ge(xb_ready, e + 1)
                    gate_up(s).then_inc(gu_full, 1)
                if first or e >= 2:
                    pe.wait_ge(yb_ready, e - 1)
                    if first or e >= 3:
                        pe.wait_ge(ys_ready, e - 2)
                    turn_y().then_inc(yt_full, 1)
                if first or 1 <= e <= E:
                    sd = slot(s - 1)
                    pe.wait_ge(d_landed[sd], 16 * (uses if s else uses - 1) if first else 16 * ((e - 1) // RING + 1))
                    pe.wait_ge(ht_ready, e)
                    down(sd).then_inc(y_full, 1)
                if first or e < E:
                    pe.wait_ge(eh_ready, e + 1)
                    turn_h(s).then_inc(ht_full, 1)

            pe.wait_ge(hn_split, 6)
            pe.wait_ge(gsel_ready, 1)
            gather(0)
            pe.wait_ge(gu_landed[0], 32)
            pe.wait_ge(xb_ready, 1)
            gate_up(0).then_inc(gu_full, 1)
            pe.wait_ge(gsel_ready, 2)
            gather(1)
            turn(0, 0, 1, gu=False)
            turn(1, 1, 1)
            slot_weights()
            for e in range(2, FIRST):
                turn(e, slot(e), e // RING + 1)
                for s in range(ST * (e - 2) // (FIRST - 2), ST * (e - 1) // (FIRST - 2)):
                    turn_selection(s)
            with pe.Fori(0, (E - FIRST) // RING) as i:
                for j in range(RING):
                    turn(3 * i + (FIRST + j), slot(FIRST + j), i + ((FIRST + j) // RING + 1))
            for e in (E, E + 1):
                turn(e, slot(e), None)
            extra = pe.value_load(wli[0:1, 2 * MAXB:2 * MAXB + 1], min_val=0, max_val=MAXB)
            pe.wait_ge(ys_ready, E)
            with pe.If(extra > 0):
                with pe.Fori(0, extra) as i:
                    pe.wait_ge(xb_landed, 48 * i + 48)
                    pe.wait_ge(xb_xb, i + 1)
                    gate_up(1).then_inc(xb_gu, 1)
                    pe.wait_ge(xb_h, i + 1)
                    turn_h(1).then_inc(xb_htf, 1)
                    pe.wait_ge(xb_ht, i + 1)
                    down(1).then_inc(xb_y, 1)
                    pe.wait_ge(xb_yb, i + 1)
                    turn_y().then_inc(xb_yt, 1)
            pe.wait_ge(experts_done, 1)
            for s in range(ST):
                for j in range(2):
                    def mms(bk):
                        for k in range(4):
                            last = pe.transpose(bk[:, k * P:k * P + P], ys[:, 4 * j + k, s * P:s * P + P], ident[:, :])
                        return last
                    fill(("yn", 2 * s + j), mms)
            moved(pe, ("yn", 2 * ST - 1))

            for k in range(KD):
                def mms(bk):
                    for s in range(ST):
                        for q, part in enumerate((yn_hi, yn_lo)):
                            last = pe.matmul(bk[:, 0:T], part[:, s, k * P:k * P + P], wcT[:, s, :],
                                             start=(s == 0 and q == 0), stop=(s == ST - 1 and q == 1))
                    return last
                fill(("mo", k), mms)

            def turn_out(m):
                pe.wait_ge(x4_ready, m + 1)
                def mms(bk):
                    for i, (t0, n) in enumerate(TILES):
                        last = pe.transpose(bk[0:n, i * P:i * P + P], xT[:, m, t0:t0 + n], ident[:, :])
                    return last
                fill(("yo", m), mms)

            pe.wait_ge(pgw_landed, 32)
            for m in range(KD):
                def mms(bk):
                    for k in range(KD):
                        if m == 0:
                            pe.wait_ge(gx_ready, KD + k + 1)
                        last = pe.matmul(bk[:, 0:T], pgw[m // 4][:, k, (m % 4) * P:(m % 4) * P + P], hT[:, k, 0:T],
                                         start=(k == 0), stop=(k == KD - 1))
                    return last
                fill(("pg", m), mms)
                if m == 0:
                    sum_squares(b_enm, sqm, sq2_sum, (x3_sq, KD)).then_inc(ss2_full, 1)
                if m >= 2:
                    turn_out(m - 2)
            turn_out(KD - 2)
            turn_out(KD - 1)
            sum_squares(b_s, sqm, sq3_sum, (x4_sq, KD)).then_inc(ss3_full, 1)
            pe.wait_ge(root3, 1)
            def mms(bk):
                for i in range(3):
                    last = pe.transpose(bk[:, i:i + 1], rootr[:, i * P:i * P + P], ident[0:1, 0:1])
                return last
            fill(("rf", 0), mms)

        @block.scalar
        def _(act):
            def take(f, *outs, func=ACT.Copy, scale=1.0, n=P):
                filled(act, f)
                for out, a in outs:
                    last = act.activation(out, a, func, scale=scale)
                last.then_inc(acc_empty["act"], 1)

            def wide(f):
                return acc(f)[:, 0:T]

            tables = [0]

            def load_table(func):
                if tables[0]:
                    act.wait_ge(table_loaded, tables[0])
                tables[0] += 1
                act.activation(idle[:, :], eps[:, :], func).then_inc(table_loaded, 1)

            def upper(part):
                if part is None:
                    return
                s, m = part
                n = quarter_of(s, m)
                if hi_free(s, m):
                    filled(act, hi_free(s, m))
                act.wait_ge(w_landed[n % WR], 16 * (n // WR + 1))
                hi, w = hi_part(s, m), part_of(wring, s, m)
                for c in range(2 if s == "v" else 1):
                    last = act.activation(hi[:, :, c, :], w[:, :, c * P:c * P + P], ACT.Copy)
                last.then_inc(whi_ready, 1)

            def square_x(k):
                moved(act, ("x", k))
                act.activation(sqx[:, k, :], xT[:, k, :], ACT.Square).then_inc(sq_ready, 1)

            for k in range(KD):
                take(("x", k), (xT[:, k, :], wide(("x", k))))
                if k:
                    square_x(k - 1)
            square_x(KD - 1)
            for c in range(2):
                take(("pn", c), (pT[:, c, :], wide(("pn", c))))
            upper(("xm", 0))
            act.wait_ge(consts, 2)
            load_table(ACT.Sqrt)
            filled(act, ("ss", 0))
            act.activation(root[:, :], wide(("ss", 0)), ACT.Sqrt, bias=eps[:, 0:1], scale=1.0 / D).then_inc(acc_empty["act"], 1)
            for k in range(KD):
                act.wait_ge(h_scaled, k + 1)
                act.activation(h_hi[:, k, 0:T], h_first[:, k, :], ACT.Copy).then_inc(h_upper, 1)
            upper(("xm", 1))
            act.wait_ge(in_small, 16 * 9)
            act.activation(wif_hi[:, :, :], wif[:, :, :], ACT.Copy).then_inc(wif_split, 1)
            act.wait_ge(hist_ready, 1)
            for m in range(KD):
                bk = acc(("xm", m))
                filled(act, ("xm", m))
                upper(later("xm", m))
                take(("xm", m), (xme[:, m, 3:PX], bk[:, 0:TP]),
                     (xme[:, m, PX:XE].rearrange("p (b j) -> p b j", b=NB)[:, :, 3:SXX], bk[:, TP:T].rearrange("p (b j) -> p b j", b=NB)))
            act.wait_ge(gate_step, 1)
            act.activation(rows[:, 2, :], rows[:, 2, :], ACT.Exp, scale=-1.0).then_inc(act_step, 1)
            act.wait_ge(act_step, 1)
            act.activation(rows[:, 2, :], rows[:, 2, :], ACT.Ln, bias=1.0).then_inc(gate_act, 1)

            def take_v(j):
                for i, (t0, n) in enumerate(TILES):
                    f = ("v", 3 * j + i)
                    take(f, (vn[0:n, i, QC * j:QC * j + QC], acc(f)[0:n, 0:QC]))

            take_v(0)
            upper(("v", 2))
            take_v(1)
            upper(("v", 3))
            act.wait_ge(conv_done, 1)
            act.activation(xq[:, :, 0:TP], cv[:, :, 0:TP], ACT.Sigmoid)
            for k in range(KD):
                last = act.activation(xq[:, k, TP:T].rearrange("p (b j) -> p b j", b=NB),
                                      cv_sample(k), ACT.Sigmoid)
            last.then_inc(sig_ready, 1)
            act.wait_ge(gate_step, 2)
            act.activation(rows[:, 1, :], rows[:, 1, :], ACT.Exp).then_inc(rows_ready, 1)
            act.activation(rows[:, 3, 0:NS], rows[:, 3, 0:NS], ACT.Exp)
            act.activation(rows[:, 7, :], rows[:, 7, :], ACT.Exp, scale=-1.0).then_inc(rows_ready, 1)
            take_v(2)
            take_v(3)
            upper(("sc", 0))
            upper(("sc", 1))

            def take_qk(h):
                p = h % 2
                for n in range(4):
                    r, c = divmod(n, 2)
                    f = ("qk", h, n)
                    take(f, ((kT if r else qT)[:, p, c, :], wide(f)), scale=1.0 if r else DH ** -0.5)
                for i, (t0, n) in enumerate(TILES):
                    f = ("kn", h, i)
                    take(f, (kn[0:n, p, i, :], acc(f)[0:n, 0:DH]))

            def exps(h):
                act.wait_ge(args_ready, h + 1)
                for o, n, i, r in ((0, 256, 0, P), (256, P, 1, P), (384, NS, 2, NS)):
                    last = act.activation(pt[0:r, o:o + n], pt[0:r, o:o + n], ACT.Exp, bias=awT[0:r, 0, i, h:h + 1])
                last.then_inc(exps_ready, 1)

            take_qk(0)
            for j in range(2):
                if j == 0:
                    act.wait_ge(h_ready, 1)
                take(("to", j), (tailn[:, 512 * j:512 * j + 512], acc(("to", j))[0:27, :]))
            exps(0)
            take_qk(1)
            for h in range(H):
                if MID[h][0] == "sc":
                    act.wait_ge(tailn_stored, 32)
                    for m in range(KD):
                        filled(act, ("sc", m))
                        upper(later("sc", m))
                        take(("sc", m), (s1[:, m, :], wide(("sc", m))))
                if MID[h][0] == "gb":
                    act.wait_ge(tails_ready, 2)
                    for m in range(KD):
                        filled(act, ("gb", m))
                        upper(later("gb", m))
                        take(("gb", m), (s4[:, m, :], wide(("gb", m))), func=ACT.Sigmoid)
                if MID[h][0] in ("sx", "sb"):
                    for m in range(KD):
                        upper(later(MID[h][0], m))
                act.wait_ge(hm_ready, h + 1)
                act.activation(hsq[:, :, :], xq[:, 2 * h:2 * h + 2, :], ACT.Square).then_inc(hsq_ready, 1)
                if h:
                    act.wait_ge(cp_stored, 16 * h)
                take(("Cp", h), (cpn[:, :, :].rearrange("p a b -> p (a b)"), acc(("Cp", h))[:, :]))
                act.wait_ge(ss_full, h + 1)
                act.activation(ssT[:, h, :], b_enm[:, 0:T], ACT.Copy).then_inc(ss_taken, 1)
                if h + 1 < H:
                    exps(h + 1)
                if h + 2 < H:
                    take_qk(h + 2)
            load_table(ACT.Sqrt)
            act.wait_ge(ss_taken, H)
            act.activation(ssT[:, :, :], ssT[:, :, :], ACT.Sqrt, bias=eps[:, 0:1], scale=1.0 / DH).then_inc(hroot, 1)
            moved(act, ("sb", KD - 1))
            for m in range(KD):
                filled(act, ("o", m))
                upper(later("o", m))
                if m == 0:
                    act.wait_ge(c_stored, 16 * H)
                take(("o", m), (oT[:, m, :], wide(("o", m))), func=ACT.Sigmoid)
                if m in (0, 2):
                    act.activation(s1_hi[:, 2 * m:2 * m + 4, :], s1[:, 2 * m:2 * m + 4, :], ACT.Copy).then_inc(s1_high, 1)
            for j in range(2):
                take(("tu", j), (tails[:, 512 * j:512 * j + 512], acc(("tu", j))[0:18, :]))
            for m in range(KD):
                upper(later("sout", m))
            for m in range(KD):
                filled(act, ("ga", m))
                upper(later("ga", m))
                take(("ga", m), (s1[:, m, :], wide(("ga", m))), func=ACT.Sigmoid)
                if m == 0:
                    act.wait_ge(ya_ready, 1)
                    act.activation(oT_hi[:, :, :], oT[:, :, :], ACT.Copy).then_inc(oT_split, 1)
            for m in range(KD):
                if m < KD - 1:
                    upper(later("a", m))
                moved(act, ("a", m))
                act.activation(s4_hi[:, m, :], s4[:, m, :], ACT.Copy).then_inc(s4_high, 1)
            upper(("wo", 1))

            for m in range(KD):
                upper(later("wo", m))
                moved(act, ("wo", m))
                if m == 0:
                    act.wait_ge(ya_ready, 1)
                act.activation(sq1[:, m, :], xT[:, m, :], ACT.Square).then_inc(sq1_ready, 1)
            load_table(ACT.Sqrt)
            act.wait_ge(lg_full, 1)
            act.activation(rootr[:, 0:T], b_enm[0:1, 0:T], ACT.Sqrt, bias=eps[0:1, 0:1], scale=1.0 / D)
            act.activation(lgT[:, 0:T], b_s[0:G + E, 0:T], ACT.Copy).then_inc(lgT_ready, 1)
            act.wait_ge(rc_ready, 1)
            act.wait_ge(stored, 16 * 6)
            act.wait_ge(cp_stored, 16 * H)
            for n in range(6):
                i, j = divmod(n, 2)
                f = ("hn", n)
                filled(act, f)
                act.activation(hn[:, i, 512 * j:512 * j + 512], acc(f)[:, :], ACT.Copy, scale=rc[:, i:i + 1]).then_inc(acc_empty["act"], 1)
            load_table(ACT.Exp)
            act.wait_ge(rt_arg, 1)
            act.activation(r4[:, :, 2, :], r4[:, :, 2, :], ACT.Exp)
            act.activation(r1[:, :, 7:8], r1[:, :, 7:8], ACT.Exp).then_inc(rt_exp, 1)
            for k in range(KD):
                take(("pp", k), (ppr[:, k, :], wide(("pp", k))))
            def take_xs(j):
                for k in range(KD):
                    f = ("xs", KD * j + k)
                    take(f, (xs[:, k, j * T:j * T + T], wide(f)))

            def gate_sigmoid(s):
                return act.activation(sg[:, s, :], b_gu[s][:, 0:P], ACT.Sigmoid)

            def take_y():
                return act.activation(yb[:, :], b_y[:, :], ACT.Copy)

            def place_y(off):
                for c in range(2):
                    last = act.activation(ys[:, 4 * c:4 * c + 4, bass.ds(off, CAP)],
                                          b_yt[:, :].rearrange("p (q c t) -> p q c t", q=4, c=2)[:, :, c, :], ACT.Copy)
                return last

            def turn(e, s):
                first = not isinstance(e, int)
                if first or e < E:
                    act.wait_ge(gu_full, e + 1)
                    if first or e >= RING:
                        act.wait_ge(ht_full, e + (1 - RING))
                    gate_sigmoid(s).then_inc(esig_ready, 1)
                if first or e >= 2:
                    off = act.value_load(offi[0:1, bass.ds(e - 2, 1)], min_val=0, max_val=PAIRS)
                    act.wait_ge(yt_full, e - 1)
                    place_y(off).then_inc(ys_ready, 1)
                if first or 1 <= e <= E:
                    act.wait_ge(y_full, e)
                    take_y().then_inc(yb_ready, 1)

            take_xs(0)
            load_table(ACT.Sigmoid)
            turn(0, 0)
            take_xs(1)
            turn(1, 1)
            act.wait_ge(offs_ready, 2)
            filled(act, ("ws", 0))
            for e in range(2, FIRST):
                turn(e, slot(e))
                for s in range(ST * (e - 2) // (FIRST - 2), ST * (e - 1) // (FIRST - 2)):
                    take(("wc", s), (wcT[:, s, :], wide(("wc", s))))
            with act.Fori(0, (E - FIRST) // RING) as i:
                for j in range(RING):
                    turn(3 * i + (FIRST + j), slot(FIRST + j))
            for e in (E, E + 1):
                turn(e, slot(e))
            extra = act.value_load(wli[0:1, 2 * MAXB:2 * MAXB + 1], min_val=0, max_val=MAXB)
            act.wait_ge(ys_ready, E)
            act.sem_inc(xb_done, 1)
            with act.If(extra > 0):
                with act.Fori(0, extra) as i:
                    off = act.value_load(wli[0:1, bass.ds(i + MAXB, 1)], min_val=0, max_val=PAIRS)
                    act.wait_ge(xb_gu, i + 1)
                    gate_sigmoid(1).then_inc(xb_sig, 1)
                    act.wait_ge(xb_y, i + 1)
                    take_y().then_inc(xb_yb, 1)
                    act.wait_ge(xb_yt, i + 1)
                    place_y(off).then_inc(xb_done, 1)
            act.sem_inc(experts_done, 1)

            for n in range(2 * ST):
                s, j = divmod(n, 2)
                f = ("yn", n)
                filled(act, f)
                act.activation(yn_hi[:, s, 512 * j:512 * j + 512], acc(f)[:, :], ACT.Copy, scale=wslot[:, s:s + 1]).then_inc(yhi_ready, 1)
            for k in range(KD):
                moved(act, ("mo", k))
                act.activation(sqm[:, k, :], xT[:, k, :], ACT.Square).then_inc(x3_sq, 1)
            load_table(ACT.Sqrt)
            act.wait_ge(ss2_full, 1)
            act.activation(root[:, :], b_enm[:, 0:T], ACT.Sqrt, bias=eps[:, 0:1], scale=1.0 / D).then_inc(root2, 1)
            load_table(ACT.Sigmoid)

            def finish_chunk(m):
                act.wait_ge(x4_ready, m + 1)
                if m == 0:
                    act.wait_ge(ss2_full, 1)
                act.activation(sqm[:, m, :], xT[:, m, :], ACT.Square).then_inc(x4_sq, 1)
                f = ("yo", m)
                take(f, (x4n[:, 0:2, m * P:m * P + P], acc(f)[:, 0:2 * P].rearrange("p (i c) -> p i c", i=2)),
                     (x4n[0:NS, 2, m * P:m * P + P], acc(f)[0:NS, 2 * P:3 * P]))

            for m in range(KD):
                act.wait_ge(pgs_ready, m + 1)
                act.activation(pgs[:, m % 2, :], pgs[:, m % 2, :], ACT.Sigmoid).then_inc(sig_ready, 1)
                if m:
                    finish_chunk(m - 1)
            load_table(ACT.Sqrt)
            finish_chunk(KD - 1)
            act.wait_ge(ss3_full, 1)
            act.activation(rootr[:, 0:T], b_s[0:1, 0:T], ACT.Sqrt, bias=eps[0:1, 0:1], scale=1.0 / D).then_inc(root3, 1)

        @block.gpsimd
        def _(pool):
            def select(out, pattern, cm, base_, fill, op=ALU.is_ge):
                return pool.affine_select(out=out, in_=out, pattern=pattern, compare_op=op, fill=fill, base=base_, channel_multiplier=cm)

            own = [0]
            go = step(pool, pool_step, own)
            go(pool.memset(ident[:, :], 0.0))
            select(ident[:, :], [[-1, P]], 1, 0, 1.0, ALU.not_equal).then_inc(consts, 1)
            pool.memset(eps[:, :], EPS)
            pool.memset(ones[:, :], 1.0).then_inc(consts, 1)
            go(pool.memset(selh[:, :, :], 0.0))
            select(selh[:, :, :], [[-1, H], [0, P]], 1, 0, 1.0, ALU.not_equal).then_inc(consts, 1)
            go(pool.memset(mask[:, :], 0.0))
            go(select(mask[:, 0:256], [[1, 256]], -1, 0, NEG))
            go(select(mask[:, 256:384], [[1, P]], -1, 0, NEG))
            ms = mask[0:NS, 384:448].rearrange("p (b j) -> p b j", b=NB)
            go(select(ms, [[-TS, NB], [0, TS]], 1, 0, NEG))
            select(ms, [[TS, NB], [1, TS]], -1, 0, NEG).then_inc(consts, 1)
            go(pool.memset(oneb[:, :], 1.0))
            go(select(oneb[:, :], [[-TS, NB]], 1, 0, 0.0))
            select(oneb[:, :], [[TS, NB]], -1, TS - 1, 0.0).then_inc(consts, 1)

            go(pool.memset(onet[:, :, :], 1.0))
            go(select(onet[:, :, :], [[-TS, NB], [1, NS]], 0, 0, 0.0))
            select(onet[:, :, :], [[TS, NB], [-1, NS]], 0, TS - 1, 0.0).then_inc(consts, 1)

            def load_wqk(h):
                if h:
                    pool.wait_ge(acc_full, index[("kn", h - 1, 2)] + 1)
                for r, w in enumerate((I["w_q"], I["w_k"])):
                    pool.dma_start(wqk[:, r, :, :], w[0, h].rearrange("(d p) e -> p d e", p=P)).then_inc(wqk_landed, 16)

            def load_c(h):
                pool.dma_start(cbuf_rows, I["state_mlstm_C"][0, :, h].rearrange("b (p d) e -> p b (d e)", p=P)).then_inc(c_landed, 16)

            load_wqk(0)
            pool.wait_ge(acc_full, index[("x", KD - 1)] + 1)
            load_c(0)
            pool.wait_ge(m_ready, 1)
            pool.dma_start(O[9][0].rearrange("b h -> h b"), mo[:, 0:NB]).then_inc(stored, 16)
            pool.dma_start(O[4][0].rearrange("a h -> h a"), mo[:, NB:NB + 1]).then_inc(stored, 16)
            load_wqk(1)
            moved(pool, ("to", 1))
            pool.dma_start(O[5][0, 0], tailn[0:3, :]).then_inc(tailn_stored, 16)
            pool.dma_start(O[10][0].rearrange("b j d -> (b j) d"), tailn[3:27, :]).then_inc(tailn_stored, 16)
            pool.wait_ge(aw_ready, 1)
            for h in range(H):
                p = h % 2
                moved(pool, ("kn", h, 2))
                if h:
                    pool.wait_ge(acc_full, index[("n", h - 1)] + 1)
                pool.tensor_tensor(wkm[:, :, :], kn[0:NS, p, 2:3, :].to_broadcast([NS, NB, DH]),
                                   wsel[:, h, :].unsqueeze(2).to_broadcast([NS, NB, DH]), ALU.mult)
                for i in range(2):
                    last = pool.tensor_scalar(wkp[:, i, :], kn[:, p, i, :], awT[:, 1, i, h:h + 1], None, ALU.mult)
                last.then_inc(wk_ready, 1)
                if h + 2 < H:
                    load_wqk(h + 2)
                pool.wait_ge(c_updated, h + 1)
                pool.dma_start(O[7][0, :, h].rearrange("b (p d) e -> p b (d e)", p=P), cbuf_rows).then_inc(c_stored, 16)
                moved(pool, ("Cp", h))
                pool.dma_start(O[2][0, 0, h].rearrange("(p d) e -> p d e", p=P), cpn[:, :, :]).then_inc(cp_stored, 16)
                if h + 1 < H:
                    pool.wait_ge(c_stored, 16 * (h + 1))
                    load_c(h + 1)
            pool.wait_ge(n_ready, H)
            pool.dma_start(O[8][0], nrow[:, :, :]).then_inc(stored, 16)
            pool.dma_start(O[3][0], npr[:, :, :]).then_inc(stored, 16)
            moved(pool, ("tu", 1))
            pool.dma_start(O[6][0, 0], tails[0:2, :]).then_inc(stored, 16)
            pool.dma_start(O[11][0].rearrange("b j d -> (b j) d"), tails[2:18, :]).then_inc(stored, 16)
            pool.wait_ge(tailn_stored, 32)

            def add_squares(sq, ready, summed):
                for k in range(1, KD - 1):
                    pool.wait_ge(ready, k + 1)
                    last = pool.tensor_tensor(sq[:, 0, :], sq[:, 0, :], sq[:, k, :], ALU.add)
                    if k < KD - 2:
                        go(last)
                last.then_inc(summed, 1)

            add_squares(sq1, sq1_ready, sq1_sum)
            pool.wait_ge(lg_full, 1)
            pool.wait_ge(stored, 16 * 6)
            pool.wait_ge(cp_stored, 16 * H)
            pool.memset(valid[:, :], 1.0)
            go(pool.memset(tri[:, :], 1.0))
            go(select(tri[:, :], [[1, P]], -1, -1, 0.0))
            go(select(valid[:, :], [[-P, 3]], -1, T - 1, 0.0))
            f = dict(allow_small_or_imprecise_dtypes=True)
            pool.iota(io4[:, :], [[1, G]], base=0, channel_multiplier=0, **f)
            pool.iota(io8[:, :], [[1, EG]], base=0, channel_multiplier=0, **f)
            pool.iota(ios[:, :], [[1, PAIRS]], base=0, channel_multiplier=0, **f)
            pool.iota(ioe[:, :, :], [[0, JX], [1, E]], base=0, channel_multiplier=0, **f)
            pool.iota(ioj[:, :, :], [[CAP, JX], [0, E]], base=CAP, channel_multiplier=0, **f)
            pool.iota(iow[:, :], [[0, 1]], base=1, channel_multiplier=1, **f).then_inc(consts2, 1)
            for n in range(6):
                i, j = divmod(n, 2)
                moved(pool, ("hn", n))
                a = hn[:, i, 512 * j:512 * j + 512]
                go(pool.tensor_copy(hn_hi[:, i, 512 * j:512 * j + 512], a))
                pool.tensor_tensor(hn_lo[:, i, 512 * j:512 * j + 512], a, hn_hi[:, i, 512 * j:512 * j + 512].bitcast(F32), ALU.subtract)\
                    .then_inc(hn_split, 1)
            add_squares(sqm, x3_sq, sq2_sum)
            add_squares(sqm, x4_sq, sq3_sum)

        @block.vector
        def _(dve):
            own = [0]
            go = step(dve, dve_step, own)
            empty = acc_empty["dve"]

            def wide(f):
                return acc(f)[:, 0:T]

            def first_norm():
                moved(dve, ("ss", 0))
                dve.wait_ge(cols_ready, 1)
                go(dve.reciprocal(rstd[:, :], root[:, :]))
                for k in range(KD + 1):
                    if k < KD:
                        dve.scalar_tensor_tensor(h_first[:, k, :], xT[:, k, :], cols[:, k, R_MIX:R_MIX + 1], rstd[:, :], ALU.mult, ALU.mult)\
                            .then_inc(h_scaled, 1)
                    if k:
                        dve.wait_ge(h_upper, k)
                        dve.tensor_tensor(h_lo[:, k - 1, :], h_first[:, k - 1, :], h_hi[:, k - 1, 0:T].bitcast(F32), ALU.subtract)\
                            .then_inc(h_ready, 1)

            def lower(part):
                if part is None:
                    return
                s, m = part
                dve.wait_ge(whi_ready, parts.index(part) + 1)
                hi, w, lo = hi_part(s, m), part_of(wring, s, m), part_of(w_lo, s, m)
                for c in range(2 if s == "v" else 1):
                    a = slice(c * P, c * P + P)
                    last = dve.tensor_tensor(lo[:, :, a], w[:, :, a], hi[:, :, c, :].bitcast(F32), ALU.subtract)
                last.then_inc(wlo_ready, 1)

            seq = lambda a: a.rearrange("p (b j) -> p b j", b=NB)
            dve.memset(hT[:, :, T:3 * P], 0.0)
            dve.memset(xme[:, :, 0:3], 0.0)
            dve.memset(qz[:, :, :, NS:WIDE], 0.0)
            dve.memset(pt[:, 448:384 + WIDE], 0.0)
            dve.memset(rows[:, 3, :], 1.0)
            go(dve.memset(rows[:, 4, :], 0.0))
            dve.memset(rows[:, 3, 0:1], 0.0)
            dve.memset(rows[:, 3, TP:T:TS], 0.0)
            dve.memset(rows[:, 4, 0:1], NEG)
            go(dve.memset(rows[:, 4, TP:T:TS], NEG))
            def add_square(k):
                dve.wait_ge(sq_ready, k + 1)
                last = dve.tensor_tensor(sqx[:, 0, :], sqx[:, 0, :], sqx[:, k, :], ALU.add)
                if k < KD - 2:
                    go(last)
                else:
                    last.then_inc(sq0_sum, 1)

            for k in range(1, KD - 2):
                add_square(k)
            filled(dve, ("rows",))
            dve.tensor_copy(cols[:, :, :].rearrange("p k r -> p (k r)"), acc(("rows",))[:, 0:KD * R_ALL]).then_inc(empty, 1)
            moved(dve, ("rows",))
            for k in range(KD):
                last = dve.tensor_copy(seq(xme[:, k, PX:XE])[:, :, 0:3], seq(cols[:, k, R_MCH:R_SCH]))
            last.then_inc(hist_ready, 1)
            filled(dve, ("nn",))
            dve.tensor_copy(nT[:, :, :].rearrange("p c n -> p (c n)"), acc(("nn",))[:, 0:64]).then_inc(empty, 1)
            dve.sem_inc(cols_ready, 1)
            add_square(KD - 2)
            lower(("xm", 0))
            first_norm()
            lower(("xm", 1))
            dve.wait_ge(wif_split, 1)
            dve.tensor_tensor(wif_lo[:, :, :], wif[:, :, :], wif_hi[:, :, :].bitcast(F32), ALU.subtract).then_inc(wif_split, 1)
            for m in range(KD - 1):
                lower(later("xm", m))

            moved(dve, ("xm", KD - 1))
            def tap(j):
                for k in range(KD):
                    x, w = xme[:, k, j:j + XE - 3], cols[:, k, R_MCW + j:R_MCW + j + 1]
                    last = dve.tensor_scalar(cv[:, k, :], x, w, None, ALU.mult) if j == 0 else \
                        dve.scalar_tensor_tensor(cv[:, k, :], x, w, cv[:, k, :], ALU.mult, ALU.add)
                return last

            R = lambda i, a=0, b=T: rows[:, i, a:b]
            bc = lambda a: a.unsqueeze(2).to_broadcast([H, NB, TS])
            last_of = lambda i: rows[:, i, TP + TS - 1:T:TS]
            go(tap(0))
            dve.wait_ge(in_small, 16 * 9)
            filled(dve, ("if", 0))
            dve.tensor_scalar(R(0), acc(("if", 0))[0:H, 0:T], bif[:, 0:1], None, ALU.add).then_inc(empty, 1)
            lower(("v", 1))
            filled(dve, ("if", 1))
            dve.tensor_scalar(R(1), acc(("if", 1))[0:H, 0:T], bif[:, 1:2], None, ALU.add).then_inc(empty, 1)
            filled(dve, ("bb", 0))
            dve.tensor_copy(brow_all[:, :], acc(("bb", 0))[:, 0:G + E]).then_inc(empty, 1)
            moved(dve, ("if", 1))
            dve.scalar_tensor_tensor(R(2), R(1), -1.0, R(1), ALU.mult, ALU.max).then_inc(gate_step, 1)
            dve.wait_ge(gate_step, 1)
            go(dve.tensor_scalar(R(1), R(1), 0.0, None, ALU.min))
            go(tap(1))
            go(tap(2))
            tap(3).then_inc(conv_done, 1)
            lower(("v", 2))
            dve.wait_ge(gate_act, 1)
            go(dve.tensor_tensor(R(1), R(1), R(2), ALU.subtract))
            go(dve.tensor_tensor_scan(R(5), R(3), R(1), 0.0, ALU.mult, ALU.add))
            go(dve.tensor_tensor(R(0), R(0), R(5), ALU.subtract))
            go(dve.tensor_copy(R(1), R(0)))
            dve.tensor_scalar(R(1, 0, 1), R(1, 0, 1), 0.0, None, ALU.max)
            go(dve.tensor_tensor(rows[:, 1, TP:T:TS], rows[:, 1, TP:T:TS], m0r[:, :], ALU.max))
            go(dve.tensor_tensor_scan(R(6), R(4), R(1), 0.0, ALU.add, ALU.max))
            dve.tensor_scalar(R(2), R(6), -1.0, None, ALU.mult)
            dve.tensor_tensor(R(7), R(5), R(6), ALU.add)
            dve.tensor_tensor(seq(R(3, 0, NS)), bc(m0r[:, :]), seq(R(6, TP, T)), ALU.subtract)
            dve.tensor_scalar(R(1, 0, TP), R(0, 0, TP), R(6, TP - 1, TP), None, ALU.subtract)
            go(dve.tensor_tensor(seq(R(1, TP, T)), seq(R(0, TP, T)), bc(last_of(6)), ALU.subtract))
            dve.tensor_copy(mo[:, NB:NB + 1], R(7, TP - 1, TP))
            dve.tensor_copy(mo[:, 0:NB], last_of(7)).then_inc(m_ready, 1)
            dve.wait_ge(m_ready, 1)
            dve.sem_inc(gate_step, 1)
            lower(("v", 3))
            dve.wait_ge(sig_ready, 1)
            dve.tensor_tensor(xq[:, :, 0:TP], xq[:, :, 0:TP], cv[:, :, 0:TP], ALU.mult)
            for k in range(KD):
                last = dve.tensor_tensor(seq(xq[:, k, TP:T]), seq(xq[:, k, TP:T]), cv_sample(k), ALU.mult)
            last.then_inc(xq_ready, 1)
            dve.tensor_copy(tailc[:, :, 0:3], xme[:, :, PX - 3:PX])
            for k in range(KD):
                last = dve.tensor_copy(seq(tailc[:, k, 3:27]), seq(xme[:, k, PX:XE])[:, :, SXX - 3:SXX])
            last.then_inc(tails_ready, 1)
            filled(dve, ("aw", 0))
            for r in range(2):
                for i, (t0, n) in enumerate(TILES):
                    c = (3 * r + i) * H
                    last = dve.tensor_copy(awT[0:n, r, i, :], acc(("aw", 0))[0:n, c:c + H])
            dve.tensor_copy(decT[:, :], acc(("aw", 0))[0:NB, 6 * H:7 * H]).then_inc(empty, 1)
            moved(dve, ("aw", 0))
            dve.wait_ge(consts, 6)
            dve.tensor_tensor(wsel[:, :, :], awT[0:NS, 1, 2, :].unsqueeze(2).to_broadcast([NS, H, NB]),
                              oneb[:, :].unsqueeze(1).to_broadcast([NS, H, NB]), ALU.mult).then_inc(aw_ready, 1)

            def probs(h):
                p = h % 2
                dve.wait_ge(scores_full, h + 1)
                dve.tensor_tensor(pt[:, 0:256], b_bc[:, 0:256], mask[:, 0:256], ALU.add)
                dve.tensor_tensor(pt[:, 256:384], b_bc[:, P:256], mask[:, 256:384], ALU.add)
                dve.tensor_tensor(pt[0:NS, 384:448], b_bc[0:NS, TP:T], mask[0:NS, 384:448], ALU.add).then_inc(args_ready, 1)
                dve.tensor_copy(den[:, :], b_enm[:, 0:T])
                go(dve.tensor_copy(wint[:, :], b_bc[:, T:T + NS]))
                qs = qT[:, p, :, TP:T]
                go(dve.tensor_tensor(qw[:, :, :], qs, wint[:, :].unsqueeze(1).to_broadcast([P, 2, NS]), ALU.mult))
                for c in range(2):
                    n0 = nT[:, c, :].rearrange("p (b h) -> p b h", h=H)[:, :, h:h + 1].to_broadcast([P, NB, TS])
                    last = dve.tensor_tensor(seq(qn[:, c, :]), seq(qw[:, c, :]), n0, ALU.mult)
                for c in range(2):
                    last = dve.tensor_tensor(qz[:, c, :, 0:NS], qw[:, c:c + 1, :].to_broadcast([P, NB, NS]), onet[:, :, :], ALU.mult)
                dve.wait_ge(exps_ready, h + 1)
                dve.tensor_tensor(pt[:, 0:384], pt[:, 0:384], b_s[:, 0:384], ALU.mult)
                dve.tensor_tensor(pt[0:NS, 384:448], pt[0:NS, 384:448], b_s[0:NS, 384:448], ALU.mult).then_inc(probs_ready, 1)

            def outputs(h):
                dve.wait_ge(pv_full, h + 1)
                go(dve.tensor_tensor(den[:, :], b_s[:, 0:T], den[:, :], ALU.max))
                go(dve.scalar_tensor_tensor(den[:, :], b_s[:, 0:T], -1.0, den[:, :], ALU.mult, ALU.max))
                go(dve.reciprocal(den[:, :], den[:, :]))
                for c in range(2):
                    last = dve.tensor_tensor(xq[:, 2 * h + c, :], b_num[c][:, 0:T], den[:, :], ALU.mult)
                last.then_inc(hm_ready, 1)

            def new_states(h):
                for b in range(NB):
                    f = ("C", h, b)
                    filled(dve, f)
                    c = cbuf[:, b, :, :].rearrange("p d e -> p (d e)")
                    last = dve.scalar_tensor_tensor(c, c, wint[:, b * TS + TS - 1:b * TS + TS], acc(f)[:, :], ALU.mult, ALU.add)
                    last.then_inc(empty, 1)
                moved(dve, ("C", h, NB - 1))
                dve.sem_inc(c_updated, 1)
                f = ("n", h)
                filled(dve, f)
                dve.scalar_tensor_tensor(nrow[:, h, :], nrow[:, h, :], decT[:, h:h + 1], acc(f)[0:NB, 0:DH], ALU.mult, ALU.add)
                dve.tensor_copy(npr[:, h, :], acc(f)[32:33, DH:2 * DH]).then_inc(empty, 1)
                moved(dve, f)
                dve.sem_inc(n_ready, 1)

            sample_u = lambda a, n: a.rearrange("p (b j) -> p b j", b=NB)
            def middle(name, m):
                f = (name, m)
                if name in ("sc", "gb"):
                    lower(later(name, m))
                    return
                filled(dve, f)
                if f != ("sb", 0):
                    lower(later(name, m))
                if name == "sx":
                    dve.tensor_tensor(cxe[:, m, 2:PU], acc(f)[:, 0:TP], s1[:, m, 0:TP], ALU.mult)
                    dve.tensor_tensor(seq(cxe[:, m, PU:UE])[:, :, 2:SU], seq(acc(f)[:, TP:T]), seq(s1[:, m, TP:T]), ALU.mult)\
                        .then_inc(empty, 1)
                else:
                    dve.tensor_tensor(s1[:, m, 0:TP], acc(f)[:, 0:TP], uT[:, m, 0:TP], ALU.mult)
                    us = seq(uT_sample(m))[:, :, 0:TS]
                    dve.tensor_tensor(seq(s1[:, m, TP:T]), seq(acc(f)[:, TP:T]), us, ALU.mult).then_inc(empty, 1)

            lower(("sc", 0))
            lower(("sc", 1))
            probs(0)
            for h in range(H):
                if MID[h][0] == "sx":
                    moved(dve, ("sc", KD - 1))
                    dve.memset(cxe[:, :, 0:2], 0.0)
                    for k in range(KD):
                        dve.tensor_copy(seq(cxe[:, k, PU:UE])[:, :, 0:2], seq(cols[:, k, R_SCH:R_ALL]))
                for m in range(KD - 1):
                    middle(MID[h][0], m)
                outputs(h)
                middle(MID[h][0], KD - 1)
                new_states(h)
                if h + 1 < H:
                    probs(h + 1)
                if MID[h][0] == "sx":
                    moved(dve, ("sx", KD - 1))
                    for j in range(3):
                        for k in range(KD):
                            x, w = cxe[:, k, j:j + UE - 2], cols[:, k, R_SCW + j:R_SCW + j + 1]
                            last = dve.tensor_scalar(uT[:, k, :], x, w, None, ALU.mult) if j == 0 else \
                                dve.scalar_tensor_tensor(uT[:, k, :], x, w, uT[:, k, :], ALU.mult, ALU.add)
                            if j == 2 and k == 3:
                                lower(("sb", 2))
                        go(last)
                if MID[h][0] == "sb":
                    dve.tensor_copy(tailu[:, :, 0:2], cxe[:, :, PU - 2:PU])
                    for k in range(KD):
                        last = dve.tensor_copy(seq(tailu[:, k, 2:18]), seq(cxe[:, k, PU:UE])[:, :, SU - 2:SU])
                    last.then_inc(tails_ready, 1)

            for m in range(KD):
                lower(later("o", m))
                if m == 0:
                    dve.wait_ge(hroot, 1)
                h = m // 2
                if m % 2 == 0:
                    go(dve.reciprocal(ssT[:, h, :], ssT[:, h, :]))
                else:
                    for k in (m - 1, m):
                        last = dve.scalar_tensor_tensor(xq[:, k, :], xq[:, k, :], cols[:, k, R_HEAD:R_HEAD + 1], ssT[:, h, :], ALU.mult, ALU.mult)
                    go(last)
                if m in (1, 3):
                    a = slice(2 * m - 2, 2 * m + 2)
                    dve.wait_ge(s1_high, h + 1)
                    dve.tensor_tensor(s1_lo[:, a, :], s1[:, a, :], s1_hi[:, a, :].bitcast(F32), ALU.subtract).then_inc(s1_split, 1)
            moved(dve, ("o", KD - 1))
            dve.tensor_tensor(oT[:, :, :], oT[:, :, :], xq[:, :, :], ALU.mult).then_inc(ya_ready, 1)
            dve.memset(lgT[:, T:3 * P], 0.0)
            dve.memset(rootr[:, T:3 * P], 1.0)
            moved(dve, ("gb", KD - 1))
            for m in range(KD):
                f = ("sout", m)
                filled(dve, f)
                lower(later("sout", m))
                dve.tensor_tensor(s4[:, m, :], wide(f), s4[:, m, :], ALU.mult).then_inc(empty, 1)
            for m in range(KD):
                lower(later("ga", m))
                if m == 1:
                    dve.wait_ge(ya_ready, 1)
                    dve.wait_ge(oT_split, 1)
                    dve.tensor_tensor(oT_lo[:, :, :], oT[:, :, :], oT_hi[:, :, :].bitcast(F32), ALU.subtract).then_inc(oT_split, 1)

            def rest_of_merged(m):
                dve.wait_ge(s4_high, m + 1)
                dve.tensor_tensor(s4_lo[:, m, :], s4[:, m, :], s4_hi[:, m, :].bitcast(F32), ALU.subtract).then_inc(s4_low, 1)

            for m in range(KD):
                f = ("a", m)
                filled(dve, f)
                if m < KD - 1:
                    lower(later("a", m))
                moved(dve, ("ga", m))
                go(dve.tensor_tensor(s1[:, m, :], wide(f), s1[:, m, :], ALU.mult))
                dve.tensor_tensor(s4[:, m, :], s4[:, m, :], s1[:, m, :], ALU.add).then_inc(empty, 1)
                if m:
                    rest_of_merged(m - 1)
            rest_of_merged(KD - 1)
            lower(("wo", 1))
            for m in range(KD):
                f = ("wo", m)
                filled(dve, f)
                lower(later("wo", m))
                dve.tensor_tensor(xT[:, m, :], wide(f), xT[:, m, :], ALU.add).then_inc(empty, 1)
                moved(dve, f)
                if m == 0:
                    moved(dve, ("ga", KD - 1))
                dve.tensor_scalar(hT[:, m, 0:T], xT[:, m, :], cols[:, m, R_FFN:R_FFN + 1], None, ALU.mult).then_inc(gx_ready, 1)

            B3 = lambda a, n: a.to_broadcast([P, 3, n])
            c1 = lambda i: r1[:, :, i:i + 1]
            filled(dve, ("lg", 0))
            dve.reciprocal(rc[:, :], acc(("lg", 0))[:, 108:111]).then_inc(rc_ready, 1)
            dve.wait_ge(rc_ready, 1)
            dve.wait_ge(consts2, 1)
            for i in range(3):
                last = dve.scalar_tensor_tensor(lg[:, i, :], acc(("lg", 0))[:, 36 * i:36 * i + 36], rc[:, i:i + 1], brow_all[:, :], ALU.mult, ALU.add)
            last.then_inc(empty, 1)
            moved(dve, ("lg", 0))

            def first_max(x, mx, idx, one, tmp, io, n):
                go(dve.tensor_reduce(mx, x, AX.X, ALU.max))
                go(dve.tensor_tensor(tmp, x, B3(mx, n), ALU.is_equal))
                go(dve.tensor_scalar(tmp, tmp, -100.0, None, ALU.mult))
                go(dve.tensor_tensor(tmp, tmp, io[:, :].unsqueeze(1).to_broadcast([P, 3, n]), ALU.add))
                go(dve.tensor_reduce(idx, tmp, AX.X, ALU.min))
                go(dve.tensor_tensor(one, tmp, B3(idx, n), ALU.is_equal))

            gl = lg[:, :, 0:G]
            first_max(gl, c1(0), c1(2), r4[:, :, 0, :], r4[:, :, 1, :], io4, G)
            go(dve.tensor_tensor(r4[:, :, 2, :], gl, B3(c1(0), G), ALU.subtract))
            for i in range(3):
                g1 = r4[:, i, 0, :].unsqueeze(2).to_broadcast([P, G, EG])
                last = dve.tensor_tensor(pick[:, 0, i, :].rearrange("p (g e) -> p g e", g=G),
                                         lg[:, i, G:G + E].rearrange("p (g e) -> p g e", g=G), g1, ALU.mult)
            go(last)
            for i in range(3):
                last = dve.tensor_reduce(r8[:, i, 0, :], pick[:, 0, i, :].rearrange("p (g e) -> p e g", g=G), AX.X, ALU.add)
            go(last)
            first_max(r8[:, :, 0, :], c1(3), c1(4), r8[:, :, 1, :], r8[:, :, 4, :], io8, EG)
            go(dve.tensor_scalar(r8[:, :, 2, :], r8[:, :, 1, :], NEG, None, ALU.mult))
            go(dve.tensor_tensor(r8[:, :, 2, :], r8[:, :, 2, :], r8[:, :, 0, :], ALU.add))
            first_max(r8[:, :, 2, :], c1(5), c1(6), r8[:, :, 3, :], r8[:, :, 4, :], io8, EG)
            dve.tensor_tensor(c1(7), c1(5), c1(3), ALU.subtract).then_inc(rt_arg, 1)
            for q, o in ((0, 1), (1, 3)):
                for i in range(3):
                    last = dve.tensor_tensor(pick[:, q, i, :].rearrange("p (g e) -> p g e", g=G),
                                             r4[:, i, 0, :].unsqueeze(2).to_broadcast([P, G, EG]),
                                             r8[:, i, o, :].unsqueeze(1).to_broadcast([P, G, EG]), ALU.mult)
            go(last)
            go(dve.tensor_tensor(m32[:, :, :], pick[:, 0, :, :], pick[:, 1, :, :], ALU.add))
            dve.tensor_tensor(m32[:, :, :], m32[:, :, :], valid[:, :].unsqueeze(2).to_broadcast([P, 3, E]), ALU.mult).then_inc(m32_ready, 1)
            dve.wait_ge(rt_exp, 1)
            dve.tensor_reduce(c1(1), r4[:, :, 2, :], AX.X, ALU.add)
            go(dve.tensor_scalar(c1(8), c1(7), 1.0, None, ALU.add))
            go(dve.tensor_tensor(c1(8), c1(8), c1(1), ALU.mult))
            go(dve.reciprocal(c1(8), c1(8)))
            go(dve.tensor_tensor(c1(9), c1(8), c1(7), ALU.mult))
            filled(dve, ("rank", 0))
            rk = acc(("rank", 0))
            go(dve.tensor_copy(cnt[:, 0, :], rk[:, 3 * E:4 * E]))
            dve.memset(cnt[:, 1, :], 1.0)
            go(dve.memset(pos[:, 0, :], 1.0))
            go(dve.tensor_tensor_scan(cnt[:, 1, :], pos[:, 0, :], cnt[:, 0, :], 0.0, ALU.mult, ALU.add))
            go(dve.tensor_tensor(cnt[:, 2, :], cnt[:, 1, :], cnt[:, 0, :], ALU.subtract))
            dve.tensor_tensor(pos[:, :, :], rk[:, 0:3 * E].rearrange("p (t e) -> p t e", t=3),
                              cnt[:, 2:3, :].to_broadcast([P, 3, E]), ALU.add).then_inc(empty, 1)
            moved(dve, ("rank", 0))
            for q in range(2):
                go(dve.tensor_tensor(pick[:, q, :, :], pick[:, q, :, :], pos[:, :, :], ALU.mult))
                go(dve.tensor_reduce(c1(10 + q), pick[:, q, :, :], AX.X, ALU.add))
                go(dve.tensor_scalar(c1(10 + q), c1(10 + q), 1.0, None, ALU.add))
                go(dve.tensor_tensor(c1(10 + q), c1(10 + q), valid[:, :].unsqueeze(2), ALU.mult))
                go(dve.tensor_scalar(c1(10 + q), c1(10 + q), -1.0, None, ALU.add))
            for j in range(2):
                a = slice(j * T, j * T + T)
                for i in range(3):
                    last = dve.tensor_scalar(ys_tmp[:, i, a], ios[:, a], r1[:, i, 10:11], None, ALU.is_equal)
                go(last)
                for i in range(3):
                    last = dve.scalar_tensor_tensor(gsel[:, i, a], ios[:, a], r1[:, i, 11:12], ys_tmp[:, i, a], ALU.is_equal, ALU.add)
                last.then_inc(gsel_ready, 1)
            dve.memset(xs[:, :, PAIRS:SLOTS], 0.0)
            C_ = lambda i: cnt[0:MAXB, i:i + 1, :].to_broadcast([MAXB, JX, E])
            dve.tensor_copy(offi[:, :], cnt[0:1, 2, :]).then_inc(offs_ready, 1)
            go(dve.tensor_tensor(blk[:, 0], C_(0), ioj[:, :, :], ALU.is_gt))
            go(dve.memset(blk[:, 1], 1.0))
            flat = lambda i: blk[:, i].rearrange("p j e -> p (j e)")
            go(dve.tensor_tensor_scan(flat(2), flat(1), flat(0), 0.0, ALU.mult, ALU.add))
            go(dve.tensor_copy(wlc[:, 2:3], flat(2)[:, JX * E - 1:JX * E]))
            go(dve.tensor_tensor(blk[:, 2], blk[:, 2], blk[:, 0], ALU.mult))
            go(dve.tensor_scalar(blk[:, 0], blk[:, 2], iow[:, :], None, ALU.is_equal))
            go(dve.tensor_tensor(blk[:, 1], C_(2), ioj[:, :, :], ALU.add))
            go(dve.tensor_scalar(blk[:, 3], C_(1), -float(CAP), None, ALU.add))
            go(dve.tensor_tensor(blk[:, 1], blk[:, 1], blk[:, 3], ALU.min))
            go(dve.tensor_tensor(blk[:, 1], blk[:, 1], blk[:, 0], ALU.mult))
            go(dve.tensor_tensor(blk[:, 3], ioe[:, :, :], blk[:, 0], ALU.mult))
            dve.tensor_reduce(wlc[:, 0:1], flat(3), AX.X, ALU.add)
            go(dve.tensor_reduce(wlc[:, 1:2], flat(1), AX.X, ALU.add))
            moved(dve, ("xs", KD - 1))
            dve.tensor_copy(xb[:, 0, :, :], xs[:, :, 0:CAP]).then_inc(xb_ready, 1)
            dve.wait_ge(gsel_ready, 2)
            for n in range(6):
                i, q = divmod(n, 2)
                out = ys_two if n else ys_tmp[:, 0, :]
                go(dve.tensor_scalar(out[:, :], ios[:, :], r1[:, i, 10 + q:11 + q], r1[:, i, 8 + q:9 + q], ALU.is_equal, ALU.mult))
                if n:
                    last = dve.tensor_tensor(ys_tmp[:, 0, :], ys_tmp[:, 0, :], ys_two[:, :], ALU.add)
                    if n == 5:
                        last.then_inc(gw_ready, 1)
                    else:
                        go(last)

            def stage_x(off, s):
                return dve.tensor_copy(xb[:, s, :, :], xs[:, :, bass.ds(off, CAP)])

            def half_h(s):
                return dve.tensor_tensor(sg[:, s, :], sg[:, s, :], b_gu[s][:, 0:P], ALU.mult)

            def full_h(s):
                return dve.tensor_tensor(sg[:, s, :], sg[:, s, :], b_gu[s][:, P:2 * P], ALU.mult)

            def take_h(s):
                return dve.tensor_copy(eh[:, s, :], b_ht[:, 0:P])

            def make_h(e, s):
                dve.wait_ge(esig_ready, e + 1)
                half_h(s).then_inc(est, 1)
                dve.wait_ge(est, e + 1)
                full_h(s).then_inc(eh_ready, 1)

            def turn(e, s, ahead=True):
                first = not isinstance(e, int)
                if not first and e == 0:
                    make_h(e, s)
                    moved(dve, ("xs", 2 * KD - 1))
                if ahead:
                    off = dve.value_load(offi[0:1, bass.ds(e + 1, 1)], min_val=0, max_val=PAIRS)
                    if first or e >= 2:
                        dve.wait_ge(gu_full, e - 1)
                    stage_x(off, slot(s + 1)).then_inc(xb_ready, 1)
                if first or e > 0:
                    make_h(e, s)
                if first or e >= RING:
                    dve.wait_ge(y_full, e + (1 - RING))
                dve.wait_ge(ht_full, e + 1)
                take_h(s).then_inc(ht_ready, 1)

            dve.wait_ge(offs_ready, 1)
            for e in range(FIRST):
                turn(e, slot(e))
                if e == 1:
                    filled(dve, ("ws", 0))
                    dve.tensor_copy(wli[:, :], acc(("ws", 0))[0:1, P:P + 2 * MAXB + 1]).then_inc(offs_ready, 1)
                    dve.tensor_copy(wslot[:, :], acc(("ws", 0))[:, 0:ST]).then_inc(empty, 1)
            with dve.Fori(0, (E - FIRST) // RING - 1) as i:
                for j in range(RING):
                    turn(3 * i + (FIRST + j), slot(FIRST + j))
            for e in range(E - RING, E):
                turn(e, slot(e), ahead=e + 1 < E)
            dve.wait_ge(offs_ready, 2)
            extra = dve.value_load(wli[0:1, 2 * MAXB:2 * MAXB + 1], min_val=0, max_val=MAXB)
            dve.wait_ge(ys_ready, E)
            with dve.If(extra > 0):
                with dve.Fori(0, extra) as i:
                    off = dve.value_load(wli[0:1, bass.ds(i + MAXB, 1)], min_val=0, max_val=PAIRS)
                    stage_x(off, 1).then_inc(xb_xb, 1)
                    dve.wait_ge(xb_sig, i + 1)
                    half_h(1).then_inc(est, 1)
                    dve.wait_ge(est, i + (E + 1))
                    full_h(1).then_inc(xb_h, 1)
                    dve.wait_ge(xb_htf, i + 1)
                    take_h(1).then_inc(xb_ht, 1)

            for n in range(2 * ST):
                s, j = divmod(n, 2)
                f = ("yn", n)
                dve.wait_ge(yhi_ready, n + 1)
                c = slice(512 * j, 512 * j + 512)
                dve.scalar_tensor_tensor(yn_lo[:, s, c], acc(f)[:, :], wslot[:, s:s + 1], yn_hi[:, s, c].bitcast(F32), ALU.mult, ALU.subtract)\
                    .then_inc(empty, 1)
            for k in range(KD):
                f = ("mo", k)
                filled(dve, f)
                dve.tensor_tensor(xT[:, k, :], wide(f), xT[:, k, :], ALU.add).then_inc(empty, 1)
                moved(dve, f)
                dve.tensor_scalar(hT[:, k, 0:T], xT[:, k, :], cols[:, k, R_PLE:R_PLE + 1], None, ALU.mult).then_inc(gx_ready, 1)
            dve.wait_ge(root2, 1)
            go(dve.reciprocal(rstd[:, :], root[:, :]))

            def add_embedding(m):
                g = pgs[:, m % 2, :]
                dve.wait_ge(sig_ready, m + 2)
                go(dve.tensor_tensor(g, g, ppr[:, m, :], ALU.mult))
                dve.tensor_tensor(xT[:, m, :], xT[:, m, :], g, ALU.add).then_inc(x4_ready, 1)

            for m in range(KD):
                f = ("pg", m)
                filled(dve, f)
                if m >= 2:
                    dve.wait_ge(x4_ready, m - 1)
                dve.tensor_tensor(pgs[:, m % 2, :], wide(f), rstd[:, :], ALU.mult).then_inc(empty, 1)
                moved(dve, f)
                dve.sem_inc(pgs_ready, 1)
                if m:
                    add_embedding(m - 1)
            add_embedding(KD - 1)
            filled(dve, ("rf", 0))
            dve.reciprocal(rc[:, :], acc(("rf", 0))[:, 0:3]).then_inc(empty, 1)
            moved(dve, ("rf", 0))
            moved(dve, ("yo", KD - 1))
            dve.wait_ge(gfin_landed, 16)
            for i, (t0, n) in enumerate(TILES):
                dve.scalar_tensor_tensor(x4n[0:n, i, :], x4n[0:n, i, :], rc[0:n, i:i + 1], gfin[0:n, :], ALU.mult, ALU.mult).then_inc(y_rows, 1)


_INS = ['x_prompt', 'x_sample', 'p_prompt', 'p_sample', 'state_mlstm_C', 'state_mlstm_n', 'state_mlstm_m',
        'state_mlstm_conv', 'state_sconv', 'g_mix', 'w_in', 'w_mconv', 'w_q', 'w_k', 'b_i', 'b_f', 'g_head', 'w_a',
        'w_sconv', 'w_sout', 'w_o', 'g_ffn', 'w_rg', 'b_rg', 'w_re', 'b_re', 'w_gate', 'w_up', 'w_down',
        'g_ple', 'w_ple_gate', 'w_ple_proj', 'g_final']
_OUTS = [(1, TP, D), (NB, TS, D), (1, 1, H, DH, DH), (1, 1, H, DH), (1, 1, H), (1, 1, 3, D), (1, 1, 2, D),
         (1, NB, H, DH, DH), (1, NB, H, DH), (1, NB, H), (1, NB, 3, D), (1, NB, 2, D)]


def kernel(**inputs):
    import concourse.bacc as _bacc
    from concourse.bass_utils import run_bass_kernel_spmd as _run

    nc = _bacc.Bacc("TRN2", target_bir_lowering=False, num_devices=1)
    arrays, ins = {}, {}
    for name in _INS:
        a = np.ascontiguousarray(inputs[name])
        arrays[f"in_{name}_dram"] = a
        ins[name] = nc.dram_tensor(f"in_{name}_dram", a.shape, F32, kind="ExternalInput").ap()
    outs = [nc.dram_tensor(f"out_{i}_dram", shape, F32, kind="ExternalOutput").ap() for i, shape in enumerate(_OUTS)]
    hybrid_step(nc, ins, outs)
    r = _run(nc, [arrays], core_ids=[0])
    return tuple(r.results[0][f"out_{i}_dram"] for i in range(len(_OUTS)))
```
